# Optimizing a Trainium2 kernel written in Bass

```python
import jax, jax.numpy as jnp
from jax import lax
import numpy as np

D_MODEL = 1024
BATCH = 1
SEQ = 128
DEPTH = 2
DEC_BATCH = 1
DEC_SEQ = 512
PAST_LEN = 256

GRID_W = 64
MLA_HEADS = D_MODEL // 128
MLA_NOPE = 64
MLA_ROPE = 32
MLA_V = 64
MLA_Q_RANK = 384
MLA_KV_RANK = 256
ROPE_BASE = 10000.0
Q_BLOCK = 128
HG_HEADS = D_MODEL // 256
HG_DK = 64
HG_DV = 64
HG_CHUNK = 16
HG_Z_CLIP = 60.0
MASK_NEG = -1e30
RW_HEADS = D_MODEL // 256
RW_HD = 64
RW_W_RANK = 64
RW_A_RANK = 64
RW_G_RANK = 128
RW_GN_EPS = 64e-5
N_EXPERTS = 16
EXPERT_FF = 1024
EC_FACTOR = 2
MLA_WIDTH = MLA_HEADS * MLA_V
HG_KW = HG_HEADS * HG_DK
HG_WIDTH = HG_HEADS * HG_DV
RW_WIDTH = RW_HEADS * RW_HD
MIX_WIDTH = MLA_WIDTH + HG_WIDTH + RW_WIDTH
MLA_COLS = MLA_Q_RANK + MLA_KV_RANK + MLA_ROPE
HG_COLS = 3 * HG_KW + 2 * HG_WIDTH
RW_COLS = 3 * RW_WIDTH + 2 * RW_W_RANK + 2 * RW_A_RANK + RW_G_RANK
IN_COLS = MLA_COLS + HG_COLS + RW_COLS
DEEPNORM_ALPHA = (2 * DEPTH) ** 0.25
DEEPNORM_BETA = (8 * DEPTH) ** -0.25
LN_EPS = 1e-5
RMS_EPS = 1e-6

kernel_name = 'hybrid_mla_hgrn2_rwkv7_ec_diffusion_step'

def _split(a, sizes):
    return jnp.split(a, [int(i) for i in np.cumsum(sizes)[:-1]], axis=-1)

def _rmsnorm(x, g):
    xf = x.astype(jnp.float32)
    return (xf * lax.rsqrt(jnp.mean(xf * xf, -1, keepdims=True) + RMS_EPS) * g.astype(jnp.float32)).astype(x.dtype)

def _layernorm(x, g, b):
    xf = x.astype(jnp.float32)
    mu = jnp.mean(xf, -1, keepdims=True)
    var = jnp.mean(jnp.square(xf - mu), -1, keepdims=True)
    return ((xf - mu) * lax.rsqrt(var + LN_EPS) * g + b).astype(x.dtype)

def _modulation(cvec, ada_w, ada_b):
    m = jax.nn.silu(cvec) @ ada_w + ada_b
    return jnp.split(m[:, None, :], 6, axis=-1)

def _axial_rope(x):
    n_tok = x.shape[1]
    rows = n_tok // GRID_W
    quarter = MLA_ROPE // 4
    row = jnp.repeat(jnp.arange(rows), GRID_W)
    col = jnp.tile(jnp.arange(GRID_W), rows)
    pos = jnp.stack([row, col], axis=-1).astype(jnp.float32)
    inv_freq = ROPE_BASE ** (-jnp.arange(quarter, dtype=jnp.float32) / quarter)
    ang = (pos[:, :, None] * inv_freq).reshape((n_tok,) + (1,) * (x.ndim - 3) + (2, quarter))
    cos, sin = jnp.cos(ang), jnp.sin(ang)
    xa = x.astype(jnp.float32).reshape(x.shape[:-1] + (2, 2, quarter))
    x1, x2 = xa[..., 0, :], xa[..., 1, :]
    out = jnp.stack([x1 * cos - x2 * sin, x1 * sin + x2 * cos], axis=-2)
    return out.reshape(x.shape).astype(x.dtype)

def _mla_attend(q_nope, q_rope, k_nope, k_rope, v):
    bsz, n_q, n_h, _ = q_nope.shape
    nb = n_q // Q_BLOCK
    scale = (MLA_NOPE + MLA_ROPE) ** -0.5

    def blocks(a):
        return jnp.moveaxis(a.reshape((bsz, nb, Q_BLOCK) + a.shape[2:]), 1, 0)

    def attend_block(qb):
        qn, qr = qb
        s = jnp.einsum('bqhd,bkhd->bhqk', qn, k_nope) + jnp.einsum('bqhr,bkr->bhqk', qr, k_rope)
        pr = jax.nn.softmax(s.astype(jnp.float32) * scale, axis=-1).astype(v.dtype)
        return jnp.einsum('bhqk,bkhd->bqhd', pr, v)

    o = lax.map(attend_block, (blocks(q_nope), blocks(q_rope)))
    return jnp.moveaxis(o, 0, 1).reshape(bsz, n_q, n_h * MLA_V)

def _hgrn_chunk_scan(q, k, v, logf, s0):
    bsz, n_tok, n_h, _ = q.shape
    dv = v.shape[-1]
    nc = n_tok // HG_CHUNK

    def to_chunks(a):
        return a.reshape(bsz, nc, HG_CHUNK, n_h, a.shape[-1]).transpose(0, 3, 1, 2, 4)

    qc, kc, vc, gc = (to_chunks(a) for a in (q, k, v, logf))
    b = jnp.cumsum(gc, axis=3)
    b_last = b[:, :, :, -1:, :]
    causal = jnp.tril(jnp.ones((HG_CHUNK, HG_CHUNK), dtype=bool))[:, :, None]
    rel = jnp.where(causal, b[:, :, :, :, None, :] - b[:, :, :, None, :, :], MASK_NEG)
    att = jnp.einsum('bhntd,bhnsd,bhntsd->bhnts', qc, kc, jnp.exp(rel))
    o_intra = jnp.einsum('bhnts,bhnsv->bhntv', att, vc)
    kv_chunk = jnp.einsum('bhnsd,bhnsv->nbhdv', kc * jnp.exp(b_last - b), vc)
    decay_chunk = jnp.exp(b_last[:, :, :, 0, :]).transpose(2, 0, 1, 3)

    def step(s, inp):
        dec, kv = inp
        return dec[..., None] * s + kv, s

    s_final, s_start = lax.scan(step, s0, (decay_chunk, kv_chunk))
    o_inter = jnp.einsum('bhntd,nbhdv->bhntv', qc * jnp.exp(b), s_start)
    o = (o_intra + o_inter).transpose(0, 2, 3, 1, 4).reshape(bsz, n_tok, n_h, dv)
    return o, s_final

def _hgrn_mixer(cols, lb, norm_g, s0):
    f32 = jnp.float32
    bsz, n_tok, _ = cols.shape
    q, i, zf_fwd, zf_bwd, g = _split(cols.astype(f32), (HG_KW, HG_WIDTH, HG_KW, HG_KW, HG_WIDTH))

    def heads(a, d):
        return a.reshape(bsz, n_tok, HG_HEADS, d)

    qh = heads(jax.nn.silu(q), HG_DK)
    vh = heads(i, HG_DV)
    o_sum = jnp.zeros_like(vh)
    finals = []
    for d, zf in enumerate((zf_fwd, zf_bwd)):
        lb_d = lb[d].reshape(HG_HEADS, HG_DK)
        z = jnp.clip(heads(zf, HG_DK), -HG_Z_CLIP, HG_Z_CLIP)
        logf = jax.nn.log_sigmoid(z) + jnp.log1p(lb_d * jnp.exp(-z))
        kh = -jnp.expm1(logf)
        seq = (qh, kh, vh, logf)
        if d == 1:
            seq = tuple(t[:, ::-1] for t in seq)
        o, s_fin = _hgrn_chunk_scan(*seq, s0[:, d].astype(f32))
        if d == 1:
            o = o[:, ::-1]
        o_sum = o_sum + o
        finals.append(s_fin)
    o_n = o_sum * lax.rsqrt(jnp.mean(o_sum * o_sum, -1, keepdims=True) + RMS_EPS) * norm_g.astype(f32).reshape(HG_HEADS, HG_DV)
    out = (o_n * jax.nn.silu(heads(g, HG_DV))).reshape(bsz, n_tok, HG_WIDTH)
    return out.astype(cols.dtype), jnp.stack(finals, axis=1)

def _token_shift(a, mu):
    prev = jnp.pad(a[:, :-1], ((0, 0), (1, 0), (0, 0)))
    nxt = jnp.pad(a[:, 1:], ((0, 0), (0, 1), (0, 0)))
    return a + mu[0] * (prev - a) + mu[1] * (nxt - a)

def _rwkv_scan(r, w, k, v, kk, a, s0):
    def step(s, inp):
        r_t, w_t, k_t, v_t, kk_t, a_t = inp
        s_kk = jnp.einsum('bhvk,bhk->bhv', s, kk_t)
        s = s * w_t[:, :, None, :] - s_kk[..., None] * (kk_t * a_t)[:, :, None, :] + v_t[..., None] * k_t[:, :, None, :]
        return s, jnp.einsum('bhvk,bhk->bhv', s, r_t)

    xs = tuple(jnp.moveaxis(t, 1, 0) for t in (r, w, k, v, kk, a))
    s_final, y = lax.scan(step, s0, xs)
    return jnp.moveaxis(y, 0, 1), s_final

def _rwkv_mixer(cols, mu, w0, w2, a0, a2, g2, k_k, k_a, r_k, gn_w, gn_b, s0):
    f32 = jnp.float32
    bsz, n_tok, _ = cols.shape
    feat = _token_shift(cols.astype(f32), mu.astype(f32))
    r, k, v, wd_f, wd_b, ad_f, ad_b, gd = _split(feat, (RW_WIDTH,) * 3 + (RW_W_RANK,) * 2 + (RW_A_RANK,) * 2 + (RW_G_RANK,))

    def heads(a):
        return a.reshape(bsz, n_tok, RW_HEADS, RW_HD)

    gate = jax.nn.sigmoid(gd) @ g2.astype(f32)
    kk = heads(k * k_k.astype(f32))
    kk = kk * lax.rsqrt(jnp.maximum(jnp.sum(kk * kk, -1, keepdims=True), 1e-12))
    rh, vh = heads(r), heads(v)
    rk = r_k.astype(f32).reshape(RW_HEADS, RW_HD)
    y_sum = jnp.zeros_like(vh)
    bonus = jnp.zeros_like(vh)
    finals = []
    for d, (wd, ad) in enumerate(((wd_f, ad_f), (wd_b, ad_b))):
        w_log = -jnp.exp(-jax.nn.softplus(-(w0[d] + jnp.tanh(wd) @ w2[d])) - 0.5)
        aa = jax.nn.sigmoid(a0[d] + ad @ a2[d])
        kd = heads(k * (1.0 + (aa - 1.0) * k_a))
        seq = (rh, heads(jnp.exp(w_log)), kd, vh, kk, heads(aa))
        if d == 1:
            seq = tuple(t[:, ::-1] for t in seq)
        y, s_fin = _rwkv_scan(*seq, s0[:, d].astype(f32))
        if d == 1:
            y = y[:, ::-1]
        y_sum = y_sum + y
        finals.append(s_fin)
        bonus = bonus + jnp.sum(rh * kd * rk, -1, keepdims=True) * vh
    mu_y = jnp.mean(y_sum, -1, keepdims=True)
    var_y = jnp.mean(jnp.square(y_sum - mu_y), -1, keepdims=True)
    y_n = (y_sum - mu_y) * lax.rsqrt(var_y + RW_GN_EPS) * gn_w.reshape(RW_HEADS, RW_HD) + gn_b.reshape(RW_HEADS, RW_HD)
    out = (y_n + bonus).reshape(bsz, n_tok, RW_WIDTH) * gate
    return out.astype(cols.dtype), jnp.stack(finals, axis=1)

def _expert_choice(h, router, w1, w3, w2):
    bsz, n_tok, dm = h.shape
    xf = h.reshape(bsz * n_tok, dm)
    cap = EC_FACTOR * (bsz * n_tok) // N_EXPERTS
    aff = jax.nn.softmax((xf @ router).astype(jnp.float32), axis=-1)
    gate, idx = lax.top_k(aff.T, cap)
    xe = xf[idx]
    he = jax.nn.silu(jnp.einsum('ecd,edf->ecf', xe, w1)) * jnp.einsum('ecd,edf->ecf', xe, w3)
    ye = jnp.einsum('ecf,efd->ecd', he, w2) * gate[..., None].astype(h.dtype)
    y = jnp.zeros_like(xf).at[idx.reshape(-1)].add(ye.reshape(-1, dm))
    return y.reshape(bsz, n_tok, dm)

def _trunk_layer(x, mod, p, ctx):
    sh1, sc1, g1, sh2, sc2, g2 = mod
    bsz, n_tok, _ = x.shape
    h = x * (1 + sc1) + sh1
    cols = h @ p['w_in']
    mla_cols, hg_cols, rw_cols = _split(cols, (MLA_COLS, HG_COLS, RW_COLS))
    q_c, ckv, krope = _split(mla_cols, (MLA_Q_RANK, MLA_KV_RANK, MLA_ROPE))
    ckv = _rmsnorm(ckv, p['mla_kv_norm'])
    q = (_rmsnorm(q_c, p['mla_q_norm']) @ p['mla_w_uq']).reshape(bsz, n_tok, MLA_HEADS, MLA_NOPE + MLA_ROPE)
    q_nope, q_rope = q[..., :MLA_NOPE], q[..., MLA_NOPE:]
    if ctx is None:
        k_ckv, k_rope = ckv, krope
        hg_s0 = jnp.zeros((bsz, 2, HG_HEADS, HG_DK, HG_DV), jnp.float32)
        rw_s0 = jnp.zeros((bsz, 2, RW_HEADS, RW_HD, RW_HD), jnp.float32)
    else:
        ckv_c, krope_c, hg_s0, rw_s0 = ctx
        q_rope = _axial_rope(q_rope)
        k_ckv = jnp.concatenate([ckv_c.astype(ckv.dtype), ckv], axis=1)
        k_rope = jnp.concatenate([krope_c.astype(krope.dtype), _axial_rope(krope)], axis=1)
    kv = (k_ckv @ p['mla_w_ukv']).reshape(bsz, -1, MLA_HEADS, MLA_NOPE + MLA_V)
    mla_o = _mla_attend(q_nope, q_rope, kv[..., :MLA_NOPE], k_rope, kv[..., MLA_NOPE:])
    hg_o, hg_s = _hgrn_mixer(hg_cols, p['hg_lb'], p['hg_norm'], hg_s0)
    rw_o, rw_s = _rwkv_mixer(rw_cols, p['rw_mu'], p['rw_w0'], p['rw_w2'], p['rw_a0'], p['rw_a2'], p['rw_g2'],
                             p['rw_k_k'], p['rw_k_a'], p['rw_r_k'], p['rw_gn_w'], p['rw_gn_b'], rw_s0)
    mix = jnp.concatenate([mla_o, hg_o, rw_o], axis=-1) @ p['w_out']
    x = _layernorm(DEEPNORM_ALPHA * x + g1 * mix, p['ln_g'][0], p['ln_b'][0])
    h2 = x * (1 + sc2) + sh2
    ffn = _expert_choice(h2, p['router'], p['ex_w1'], p['ex_w3'], p['ex_w2'])
    x = _layernorm(DEEPNORM_ALPHA * x + g2 * ffn, p['ln_g'][1], p['ln_b'][1])
    return x, (ckv, krope, hg_s, rw_s)

def setup_inputs(seed: int = 0) -> dict:
    key = jax.random.key(seed)
    ks = iter(jax.random.split(key, 40))
    f32 = jnp.float32
    D = D_MODEL

    def nrm(shape, scale):
        return scale * jax.random.normal(next(ks), shape, f32)

    def unif(shape, lo, hi):
        return jax.random.uniform(next(ks), shape, f32, lo, hi)

    return {
        'x_prompt': nrm((BATCH, SEQ, D), 1.0),
        'x_sample': nrm((DEC_BATCH, DEC_SEQ, D), 1.0),
        'cache_ckv': nrm((DEC_BATCH, DEPTH, PAST_LEN, MLA_KV_RANK), 1.0),
        'cache_krope': nrm((DEC_BATCH, DEPTH, PAST_LEN, MLA_ROPE), 1.0),
        'state_hgrn': nrm((DEC_BATCH, DEPTH, 2, HG_HEADS, HG_DK, HG_DV), 0.5),
        'state_rwkv': nrm((DEC_BATCH, DEPTH, 2, RW_HEADS, RW_HD, RW_HD), 0.5),
        'c': nrm((DEC_BATCH, D), 1.0),
        'c_ctx': nrm((D,), 1.0),
        'ada_w': nrm((DEPTH, D, 6 * D), D ** -0.5),
        'ada_b': nrm((DEPTH, 6 * D), 0.02),
        'w_in': nrm((DEPTH, D, IN_COLS), D ** -0.5),
        'mla_q_norm': 1.0 + nrm((DEPTH, MLA_Q_RANK), 0.02),
        'mla_w_uq': nrm((DEPTH, MLA_Q_RANK, MLA_HEADS * (MLA_NOPE + MLA_ROPE)), MLA_Q_RANK ** -0.5),
        'mla_kv_norm': 1.0 + nrm((DEPTH, MLA_KV_RANK), 0.02),
        'mla_w_ukv': nrm((DEPTH, MLA_KV_RANK, MLA_HEADS * (MLA_NOPE + MLA_V)), MLA_KV_RANK ** -0.5),
        'hg_lb_logits': nrm((DEPTH, 2, HG_KW), 0.1),
        'hg_norm': 1.0 + nrm((DEPTH, HG_WIDTH), 0.02),
        'rw_mu': unif((DEPTH, 2, RW_COLS), 0.0, 0.5),
        'rw_w0': unif((DEPTH, 2, RW_WIDTH), -5.0, -0.5),
        'rw_w2': nrm((DEPTH, 2, RW_W_RANK, RW_WIDTH), 0.1 * RW_W_RANK ** -0.5),
        'rw_a0': nrm((DEPTH, 2, RW_WIDTH), 0.1),
        'rw_a2': nrm((DEPTH, 2, RW_A_RANK, RW_WIDTH), RW_A_RANK ** -0.5),
        'rw_g2': nrm((DEPTH, RW_G_RANK, RW_WIDTH), RW_G_RANK ** -0.5),
        'rw_k_k': 0.85 + nrm((DEPTH, RW_WIDTH), 0.02),
        'rw_k_a': 1.0 + nrm((DEPTH, RW_WIDTH), 0.02),
        'rw_r_k': nrm((DEPTH, RW_WIDTH), 0.1),
        'rw_gn_w': 1.0 + nrm((DEPTH, RW_WIDTH), 0.02),
        'rw_gn_b': nrm((DEPTH, RW_WIDTH), 0.01),
        'w_out': nrm((DEPTH, MIX_WIDTH, D), MIX_WIDTH ** -0.5 * DEEPNORM_BETA),
        'ln_g': 1.0 + nrm((DEPTH, 2, D), 0.02),
        'ln_b': nrm((DEPTH, 2, D), 0.02),
        'router': nrm((DEPTH, D, N_EXPERTS), D ** -0.5),
        'ex_w1': nrm((DEPTH, N_EXPERTS, D, EXPERT_FF), D ** -0.5),
        'ex_w3': nrm((DEPTH, N_EXPERTS, D, EXPERT_FF), D ** -0.5),
        'ex_w2': nrm((DEPTH, N_EXPERTS, EXPERT_FF, D), EXPERT_FF ** -0.5 * DEEPNORM_BETA),
    }

def reference(x_prompt, x_sample, cache_ckv, cache_krope, state_hgrn, state_rwkv, c, c_ctx,
              ada_w, ada_b, w_in, mla_q_norm, mla_w_uq, mla_kv_norm, mla_w_ukv,
              hg_lb_logits, hg_norm, rw_mu, rw_w0, rw_w2, rw_a0, rw_a2, rw_g2,
              rw_k_k, rw_k_a, rw_r_k, rw_gn_w, rw_gn_b, w_out, ln_g, ln_b,
              router, ex_w1, ex_w3, ex_w2):
    lb_w = jax.nn.softmax(hg_lb_logits.astype(jnp.float32), axis=0)
    hg_lb = jnp.maximum(jnp.cumsum(lb_w, axis=0) - lb_w[:1], 0.0)
    y_p, y_s = x_prompt, x_sample
    ckv_l, kr_l, hg_l, rw_l = [], [], [], []
    for l in range(DEPTH):
        p = {
            'w_in': w_in[l], 'mla_q_norm': mla_q_norm[l], 'mla_w_uq': mla_w_uq[l],
            'mla_kv_norm': mla_kv_norm[l], 'mla_w_ukv': mla_w_ukv[l],
            'hg_lb': hg_lb[l], 'hg_norm': hg_norm[l],
            'rw_mu': rw_mu[l], 'rw_w0': rw_w0[l], 'rw_w2': rw_w2[l], 'rw_a0': rw_a0[l], 'rw_a2': rw_a2[l],
            'rw_g2': rw_g2[l], 'rw_k_k': rw_k_k[l], 'rw_k_a': rw_k_a[l], 'rw_r_k': rw_r_k[l],
            'rw_gn_w': rw_gn_w[l], 'rw_gn_b': rw_gn_b[l],
            'w_out': w_out[l], 'ln_g': ln_g[l], 'ln_b': ln_b[l],
            'router': router[l], 'ex_w1': ex_w1[l], 'ex_w3': ex_w3[l], 'ex_w2': ex_w2[l],
        }
        y_p, (ckv, kr, hg_s, rw_s) = _trunk_layer(y_p, _modulation(c_ctx[None, :], ada_w[l], ada_b[l]), p, None)
        ckv_l.append(ckv)
        kr_l.append(kr)
        hg_l.append(hg_s.astype(x_prompt.dtype))
        rw_l.append(rw_s.astype(x_prompt.dtype))
        ctx = (cache_ckv[:, l], cache_krope[:, l], state_hgrn[:, l], state_rwkv[:, l])
        y_s, _ = _trunk_layer(y_s, _modulation(c, ada_w[l], ada_b[l]), p, ctx)
    return (y_p, y_s, jnp.stack(ckv_l, axis=1), jnp.stack(kr_l, axis=1), jnp.stack(hg_l, axis=1), jnp.stack(rw_l, axis=1))


_drawn_inputs = setup_inputs


def setup_inputs(seed=0):
    import zlib

    import numpy as np

    out = dict(_drawn_inputs(seed))
    spreads = {}
    factors = {'cache_ckv': 6.522,
     'cache_krope': 8.0,
     'state_hgrn': 8.0,
     'state_rwkv': 8.0,
     'mla_q_norm': 8.0,
     'mla_kv_norm': 2.864,
     'hg_norm': 8.0,
     'rw_w2': 3.071,
     'rw_gn_w': 8.0,
     'rw_gn_b': 38.991}
    for name, (base, spread) in spreads.items():
        noise = np.random.default_rng([zlib.crc32(name.encode()), seed]).standard_normal(out[name].shape)
        drawn = base * np.exp(spread * noise) if base else spread * noise
        out[name] = __import__('jax').numpy.asarray(drawn.astype(out[name].dtype))
    for name, factor in factors.items():
        out[name] = (out[name] * factor).astype(out[name].dtype)
    return out
```

```python
from contextlib import ExitStack

import numpy as np
import concourse.bass as bass
from concourse import mybir

F32 = mybir.dt.float32
U32 = mybir.dt.uint32
ALU = mybir.AluOpType
ACT = mybir.ActivationFunctionType
AX = mybir.AxisListType.X

P = 128
DEPTH, DM, NPR, NSM = 2, 1024, 128, 512
NTOK = NPR + NSM
TILES = NTOK // P
KD = DM // P
PAST = 256
GRID_W = 64
NH, NOPE, ROPE, DV = 8, 64, 32, 64
QK = NOPE + ROPE
QR, KVR = 384, 256
MLA_COLS = QR + KVR + ROPE
HH, HD = 4, 64
HG0 = MLA_COLS
RW0 = HG0 + 5 * HH * HD
NRW = 9
NE, FF = 16, 1024
CAPS, CAPP = 2 * NSM // NE, 2 * NPR // NE
CAP = CAPS + CAPP
C = 64
NCH = NTOK // C
LV = 7
ALPHA = float((2 * DEPTH) ** 0.25)
SCALE = float(QK) ** -0.5
PAD = NTOK + 3
TOKC = MLA_COLS + 2 * HH * HD
HGT = 6
WRING = 6


def pad_at(n):
    return n + 1 + (n >= NPR)


def constants():
    i = np.arange(P)
    s, t = i[:, None], i[None, :]
    m = np.zeros((2, LV + 1, P, P), np.float32)
    m[:, 0] = np.eye(P)
    for j in range(LV):
        h = 1 << j
        same = s // (2 * h) == t // (2 * h)
        m[0, j + 1] = same & (s % (2 * h) < h) & (t % (2 * h) >= h)
        m[1, j + 1] = m[0, j + 1].T
    hgm = m.transpose(2, 0, 1, 3).reshape(P, 2 * (LV + 1) * P)
    rwm = np.zeros((P, 2, P), np.float32)
    a, b = np.arange(C)[:, None], np.arange(C)[None, :]
    for d in range(2):
        strict, incl = ((a < b), (a <= b)) if d == 0 else ((a > b), (a >= b))
        for r in range(2):
            rwm[r * C:(r + 1) * C, d, :C] = strict
            rwm[r * C:(r + 1) * C, d, C:] = incl
    rwl = np.zeros((P, 2, 6, C), np.float32)
    for d in range(2):
        for j in range(6):
            rwl[C:, d, j] = m[d, j + 1, :C, :C]
    blk = (s // C == t // C).astype(np.float32)
    quarter = ROPE // 4
    pos = np.stack([np.arange(NSM) // GRID_W, np.arange(NSM) % GRID_W], -1).astype(np.float32)
    inv = (np.float32(10000.0) ** (-np.arange(quarter, dtype=np.float32) / np.float32(quarter))).astype(np.float32)
    ang = pos[:, :, None] * inv
    rope = np.zeros((QK, 2, NSM), np.float32)
    rope[:NOPE, 0] = 1.0
    rot = np.zeros((QK, ROPE), np.float32)
    for ax in range(2):
        for half in range(2):
            for q in range(quarter):
                c = ax * 2 * quarter + half * quarter + q
                rope[NOPE + c, 0] = np.cos(ang[:, ax, q])
                rope[NOPE + c, 1] = np.sin(ang[:, ax, q])
                o = ax * 2 * quarter + (1 - half) * quarter + q
                rot[NOPE + o, c] = 1.0 if half else -1.0
    reset = np.ones((P, 2, NTOK), np.float32)
    reset[:, 0, 0::C] = 0
    reset[:, 1, C - 1::C] = 0
    iota = np.broadcast_to(np.arange(NTOK, dtype=np.float32), (P, NTOK))
    base = np.broadcast_to(np.where(np.arange(CAP) < CAPS, NPR, 0).astype(np.float32), (NE, CAP))
    return {
        "ident": np.eye(P, dtype=np.float32), "hgm": hgm, "rwm": rwm.reshape(P, -1), "rwl": rwl.reshape(P, -1),
        "blk": blk, "rope": rope.reshape(QK, -1), "rot": rot, "reset": reset.reshape(P, -1), "iota": iota,
        "base": base,
    }


PC = {}
_n = 0
for _name, _w in (("qn", 3), ("mu0", 9), ("mu1", 9), ("w0", 4), ("a0", 4), ("kk", 2), ("ka", 2), ("rk", 2)):
    PC[_name] = _n
    _n += _w
NPC = _n


def layout(i):
    f = lambda n: np.asarray(i[n])
    cols = lambda a: a.reshape(DEPTH, -1, P).transpose(0, 2, 1)
    w = f("w_in").reshape(DEPTH, KD, P, -1)
    tch = [HG0 + P * n for n in (0, 1)] + [HG0 + 2 * HH * HD + P * n for n in range(4)] + [RW0 + P * n for n in range(NRW)]
    w_t = np.stack([w[:, :, :, c:c + P] for c in tch], 1).transpose(0, 1, 3, 2, 4)
    tok = np.concatenate([w[..., :MLA_COLS], w[..., HG0 + 256:HG0 + 512], w[..., HG0 + 1024:HG0 + 1280]], -1)
    ukv = f("mla_w_ukv").reshape(DEPTH, 2, P, NH, 2, NOPE)
    out = {
        "x": np.concatenate([f("x_prompt").reshape(NPR, DM), f("x_sample").reshape(NSM, DM)], 0),
        "cvec": np.stack([f("c_ctx").reshape(KD, P), f("c").reshape(KD, P)], -1).transpose(1, 0, 2),
        "ada_w": f("ada_w"), "ada_b": f("ada_b"),
        "w_t": w_t, "w_tok": tok.transpose(0, 2, 1, 3),
        "w_uq": f("mla_w_uq").reshape(DEPTH, 3, P, NH * QK).transpose(0, 2, 1, 3),
        "w_uk": ukv[..., 0, :].reshape(DEPTH, 2, P, NH * NOPE).transpose(0, 2, 1, 3),
        "w_uv": ukv[..., 1, :].reshape(DEPTH, 2, P, NH * DV).transpose(0, 2, 1, 3),
        "c_ckv": f("cache_ckv").reshape(DEPTH, PAST, KVR), "c_kr": f("cache_krope").reshape(DEPTH, PAST, ROPE),
        "lb": f("hg_lb_logits").reshape(DEPTH * 4, P).T,
        "pcol": np.concatenate([cols(f(n)) for n in
                                ("mla_q_norm",)] + [cols(f("rw_mu")[:, 0]), cols(f("rw_mu")[:, 1])] +
                               [cols(f(n)) for n in ("rw_w0", "rw_a0", "rw_k_k", "rw_k_a", "rw_r_k")], -1),
        "prow": np.concatenate([f(n) for n in ("mla_kv_norm", "hg_norm", "rw_gn_w", "rw_gn_b")], -1),
        "w_wa": np.stack([f("rw_w2"), f("rw_a2")], 1).reshape(DEPTH, 2, P, HH * HD).transpose(0, 2, 1, 3),
        "w_g2": f("rw_g2"),
        "s_hg": f("state_hgrn").reshape(DEPTH, 2, 2, P, HD),
        "s_rw": f("state_rwkv").reshape(DEPTH, 2, HH, HD, HD).transpose(0, 1, 2, 4, 3).reshape(DEPTH, 2, 2, P, HD),
        "w_out": f("w_out"), "ln_g": f("ln_g"), "ln_b": f("ln_b"),
        "router": f("router").reshape(DEPTH, KD, P, NE).transpose(0, 2, 1, 3),
        "ex_w1": f("ex_w1"), "ex_w3": f("ex_w3"), "ex_w2": f("ex_w2"),
    }
    out.update(constants())
    return {k: np.ascontiguousarray(v) for k, v in out.items()}


OUTS = [("y_p", (1, NPR, DM)), ("y_s", (1, NSM, DM)), ("n_ckv", (1, DEPTH, NPR, KVR)), ("n_kr", (1, DEPTH, NPR, ROPE)),
        ("n_hg", (1, DEPTH, 2, HH, HD, HD)), ("n_rw", (1, DEPTH, 2, HH, HD, HD))]


class Shared:
    pass


class Chain:

    def __init__(self, eng, sem, at=0):
        self.eng, self.sem, self.n = eng, sem, at

    def add(self, ins):
        self.n += 1
        ins.then_inc(self.sem, 1)
        return self.n

    def join(self):
        self.eng.wait_ge(self.sem, self.n)

    def link(self, ins):
        self.add(ins)
        self.join()


def program(nc, d, o, taps=(), depth=DEPTH, stop=99):
    ctx = ExitStack()
    used = []
    with ctx:
        def sb(name, shape, dt=F32):
            return ctx.enter_context(nc.sbuf_tensor(name, shape, dt))

        def sem(name):
            s = ctx.enter_context(nc.semaphore(name))
            used.append(s)
            return s

        x = sb("x_sb", [P, TILES, DM])
        ident = sb("ident_sb", [P, P])
        hgm = sb("hgm_sb", [P, 2, (LV + 1) * P])
        rwm = sb("rwm_sb", [P, 2, P])
        rwl = sb("rwl_sb", [P, 2, 6, C])
        blk = sb("blk_sb", [P, P])
        rope = sb("rope_sb", [QK, 2, NSM])
        rot = sb("rot_sb", [QK, ROPE])
        reset = sb("reset_sb", [P, 2, NTOK])
        scT = sb("scT", [P, KD, 2])
        lball = sb("lball", [P, DEPTH, 4])
        lb = sb("lb_sb", [P, 4])
        oml = sb("oml", [P, 4])
        modc = sb("modc", [P, 2, 6, KD])
        pcol = sb("pcol_sb", [P, NPC])
        prow = sb("prow_sb", [P, 4, 256])
        eps = sb("eps_sb", [P, 3])
        arena = sb("arena", [P, 40600])
        ps = ctx.enter_context(nc.psum_tensor("ps", [P, 8, 512], F32))
        mod_d = nc.dram_tensor("mod_d", (2, 6, KD, P), F32, kind="Internal").ap()
        h2_d = nc.dram_tensor("h2_d", (NTOK, DM), F32, kind="Internal").ap()

        def part(at, *shape, rows=P, dt=F32):
            n = int(np.prod(shape))
            v = arena[0:rows, at:at + n]
            if dt != F32:
                v = v.bitcast(dt)
            if len(shape) > 1:
                names = "abcdef"[:len(shape)]
                v = v.rearrange(f"p ({' '.join(names)}) -> p {' '.join(names)}", **dict(zip(names, shape)))
            return v, at + n

        hT, a0 = part(0, KD, NTOK)
        mixT = hT
        hgT, a1 = part(a0, HGT, NTOK)
        rwT, a2 = part(a1, NRW, PAD)
        tok, FREE = part(a2, TILES, TOKC)

        chains = {k: sem(k + "_chain") for k in ("dve", "act", "pool", "pe")}
        count = dict.fromkeys(chains, 0)

        def chain(kind, eng):
            c = Chain(eng, chains[kind], count[kind])
            return c

        def done(kind, c):
            count[kind] = c.n

        S = {n: sem(n) for n in ("ld_const", "tap", "st_y")}
        S.update({n: ctx.enter_context(nc.semaphore(n)) for n in ("ld_x0", "ld_x1")})

        with nc.Block() as block:
            cv, z = part(0, KD, 2)
            lg, z = part(z, DEPTH, 4)
            tmp, z = part(z, 8, 4)

            @block.sync
            def _(sp):
                for dst, src in ((ident, "ident"), (blk, "blk"), (rot, "rot")):
                    sp.dma_start(dst[:, :], d[src]).then_inc(S["ld_const"], 16)
                sp.dma_start(hgm[:, :, :].rearrange("p a b -> p (a b)"), d["hgm"]).then_inc(S["ld_const"], 16)
                sp.dma_start(rwm[:, :, :].rearrange("p a b -> p (a b)"), d["rwm"]).then_inc(S["ld_const"], 16)
                sp.dma_start(rwl[:, :, :, :].rearrange("p a b c -> p (a b c)"), d["rwl"]).then_inc(S["ld_const"], 16)
                sp.dma_start(rope[:, :, :].rearrange("p a b -> p (a b)"), d["rope"]).then_inc(S["ld_const"], 16)
                sp.dma_start(reset[:, :, :].rearrange("p a b -> p (a b)"), d["reset"]).then_inc(S["ld_const"], 16)
                sp.dma_start(cv, d["cvec"]).then_inc(S["ld_const"], 16)
                sp.dma_start(lg.rearrange("p a b -> p (a b)"), d["lb"]).then_inc(S["ld_const"], 16)
                sp.dma_start(x[:, :, :], d["x"].rearrange("(t p) n -> p t n", p=P)).then_inc(S["ld_const"], 16)
                sp.wait_ge(S["ld_const"], 16 * 11)

            @block.scalar
            def _(act):
                a = chain("act", act)
                act.wait_ge(S["ld_const"], 176)
                a.add(nc.scalar.activation(scT[:, :, :], cv, ACT.Silu))
                act.wait_ge(chains["dve"], 2)
                a.link(nc.scalar.activation(tmp[:, 1:1 + DEPTH, :], tmp[:, 4:4 + DEPTH, :], ACT.Exp))
                done("act", a)

            @block.vector
            def _(dve):
                v = chain("dve", dve)
                dve.wait_ge(S["ld_const"], 176)
                v.link(nc.vector.tensor_tensor(tmp[:, 0, :], lg[:, 0, :], lg[:, 1, :], ALU.max))
                v.link(nc.vector.tensor_tensor(tmp[:, 4:4 + DEPTH, :], lg, tmp[:, 0:1, :].to_broadcast([P, DEPTH, 4]),
                                               ALU.subtract))
                dve.wait_ge(chains["act"], 2)
                v.link(nc.vector.tensor_tensor(tmp[:, 3, :], tmp[:, 1, :], tmp[:, 2, :], ALU.add))
                v.link(nc.vector.reciprocal(tmp[:, 3, :], tmp[:, 3, :]))
                v.link(nc.vector.tensor_tensor(tmp[:, 1:1 + DEPTH, :], tmp[:, 1:1 + DEPTH, :],
                                               tmp[:, 3:4, :].to_broadcast([P, DEPTH, 4]), ALU.mult))
                v.link(nc.vector.tensor_tensor(tmp[:, 6, :], tmp[:, 1, :], tmp[:, 1, :], ALU.subtract))
                v.link(nc.vector.tensor_scalar(lball[:, 0, :], tmp[:, 6, :], 0.0, None, ALU.max))
                v.link(nc.vector.tensor_tensor(tmp[:, 7, :], tmp[:, 1, :], tmp[:, 2, :], ALU.add))
                v.link(nc.vector.tensor_tensor(tmp[:, 7, :], tmp[:, 7, :], tmp[:, 1, :], ALU.subtract))
                v.link(nc.vector.tensor_scalar(lball[:, 1, :], tmp[:, 7, :], 0.0, None, ALU.max))
                v.add(nc.vector.memset(eps[:, 0:1], 1e-6))
                v.add(nc.vector.memset(eps[:, 1:2], 1e-5))
                v.link(nc.vector.memset(eps[:, 2:3], 64e-5))
                done("dve", v)

        def clear_all():
            nc.all_engine_barrier()
            with nc.Block() as block:
                @block.sync
                def _(sp):
                    for s in used:
                        sp.sem_clear(s)
            nc.all_engine_barrier()
            for k in count:
                count[k] = 0

        e = Shared()
        e.nc, e.d, e.o, e.x, e.ident, e.hgm = nc, d, o, x, ident, hgm
        e.rwm, e.rwl, e.blk, e.rope, e.rot, e.reset = rwm, rwl, blk, rope, rot, reset
        e.scT, e.lball, e.lb, e.oml, e.modc, e.pcol = scT, lball, lb, oml, modc, pcol
        e.prow, e.eps, e.ps, e.mod_d, e.h2_d, e.part = prow, eps, ps, mod_d, h2_d, part
        e.hT, e.mixT, e.hgT, e.rwT, e.tok, e.a0 = hT, mixT, hgT, rwT, tok, a0
        e.a1, e.a2, e.FREE, e.chains, e.count, e.chain = a1, a2, FREE, chains, count, chain
        e.done = done
        clear_all()
        with nc.Fori(0, depth) as l:
            e.l = l
            last = []

            def clear_last(sp):
                for s in last:
                    sp.sem_clear(s)

            e.clear_last = clear_last
            for n, (f, names) in enumerate(PHASES):
                if n >= stop:
                    break
                own = {name: nc.alloc_semaphore(name=f"{name}") for name in names}
                e.S = {**S, **own}
                f(e)
                for s in last:
                    nc.release_semaphore(s)
                last[:] = own.values()
            if taps:
                with nc.Block() as block:
                    @block.sync
                    def _(sp):
                        for k, (name, f) in enumerate(taps):
                            sp.dma_start(o[name][l], f(e)).then_inc(S["tap"], 16)
                        sp.wait_ge(S["tap"], 16 * len(taps))
            used.extend(last)
            clear_all()
        with nc.Block() as block:
            @block.sync
            def _(sp):
                sp.dma_start(o["y_p"][0], x[:, 0, :]).then_inc(S["st_y"], 16)
                sp.dma_start(o["y_s"][0].rearrange("(t p) n -> p t n", p=P), x[:, 1:TILES, :]).then_inc(S["st_y"], 16)
                sp.wait_ge(S["st_y"], 32)


MODULATION_SEMS = (
    "ld_adab",
    "mod_out", "mod_in", "ada_ps", "ada_row", "modt", "ld_par", "ld_ada0", "ld_ada1", "ld_ada2", "ld_ada3",
)


def phase_modulation(e):
    nc, d, l, S = e.nc, e.d, e.l, e.S
    NB = 6 * DM // 512
    RING = 4
    slot, z = e.part(0, RING, KD, 512)
    brow, z = e.part(z, 6 * DM, rows=2)
    mrow, z = e.part(z, 6 * DM, rows=2)
    mt, z = e.part(z, P, rows=96)
    ps = e.ps
    with nc.Block() as block:
        @block.sync
        def _(sp):
            e.clear_last(sp)
            sp.dma_start(brow, d["ada_b"][l].rearrange("(o n) -> o n", o=1).to_broadcast([2, 6 * DM])).then_inc(S["ld_adab"], 16)
            for n in range(NB):
                if n >= RING:
                    sp.wait_ge(S["ada_ps"], n - RING + 1)
                sp.dma_start(slot[:, n % RING], d["ada_w"][l].rearrange("(k p) n -> p k n", p=P)[:, :, n * 512:(n + 1) * 512]
                             ).then_inc(S[f"ld_ada{n % RING}"], 16)
            sp.dma_start(e.pcol[:, :], d["pcol"][l]).then_inc(S["ld_par"], 16)
            sp.dma_start(e.prow[:, :, :].rearrange("p a b -> p (a b)"),
                         d["prow"][l].rearrange("(o n) -> o n", o=1).to_broadcast([P, 1024])).then_inc(S["ld_par"], 16)
            sp.wait_ge(S["ada_row"], NB)
            sp.dma_start(e.mod_d.rearrange("g s k p -> g (s k p)"), mrow).then_inc(S["mod_out"], 16)
            sp.wait_ge(S["mod_out"], 16)
            sp.dma_start(mt, e.mod_d.rearrange("g s k p -> (g s k) p")).then_inc(S["mod_in"], 16)
            sp.wait_ge(S["ld_par"], 32)

        @block.tensor
        def _(pe):
            for n in range(NB):
                pe.wait_ge(S[f"ld_ada{n % RING}"], 16 * (n // RING + 1))
                if n >= 8:
                    pe.wait_ge(S["ada_row"], n - 7)
                for k in range(KD):
                    i = nc.tensor.matmul(ps[0:2, n % 8, :], e.scT[:, k, :], slot[:, n % RING, k, :],
                                         start=k == 0, stop=k == KD - 1)
                i.then_inc(S["ada_ps"], 1)
            pe.wait_ge(S["mod_in"], 16)
            pe.wait_ge(S["ada_row"], NB)
            nc.tensor.transpose(ps[:, 0, 0:96], mt, e.ident[0:96, 0:96]).then_inc(S["modt"], 1)

        @block.vector
        def _(dve):
            v = e.chain("dve", dve)
            dve.wait_ge(S["ld_adab"], 16)
            for n in range(NB):
                dve.wait_ge(S["ada_ps"], n + 1)
                nc.vector.tensor_tensor(mrow[:, n * 512:(n + 1) * 512], ps[0:2, n % 8, :], brow[:, n * 512:(n + 1) * 512],
                                        ALU.add).then_inc(S["ada_row"], 1)
            dve.wait_ge(S["modt"], 1)
            v.link(nc.vector.tensor_copy(e.modc[:, :, :, :].rearrange("p g s k -> p (g s k)"), ps[:, 0, 0:96]))
            for s in (1, 4):
                v.add(nc.vector.tensor_scalar(e.modc[:, :, s, :], e.modc[:, :, s, :], 1.0, None, ALU.add))
            v.link(nc.vector.tensor_copy(e.lb[:, :], e.lball[:, bass.ds(l, 1), :].rearrange("p a b -> p (a b)")))
            v.link(nc.vector.tensor_scalar(e.oml[:, :], e.lb[:, :], -1.0, 1.0, ALU.mult, ALU.add))
            e.done("dve", v)


PROJECT_SEMS = (
    "ld_tokw", "pj_ps", "pj_act", "pj_dve", "ld_wt0", "ld_wt1", "ld_wt2", "ld_wt3", "ld_wt4", "ld_wt5",
)


def phase_project(e):
    nc, d, l, S, ps = e.nc, e.d, e.l, e.S, e.ps
    tokw, z = e.part(e.FREE, KD, TOKC)
    ring, z = e.part(z, WRING, KD, P)
    NT = HGT + NRW
    spans = ((0, 512), (512, MLA_COLS), (MLA_COLS, TOKC))
    groups = [("x", t, h) for t in range(TILES) for h in range(2)]
    NX = len(groups)
    groups += [("T", c, g) for c in range(NT) for g in (1, 0)]
    groups += [("tok", t, s) for t in range(TILES) for s in range(3)]

    with nc.Block() as block:
        @block.sync
        def _(sp):
            e.clear_last(sp)
            for c in range(NT):
                if c >= WRING:
                    sp.wait_ge(S["pj_ps"], NX + 2 * (c - WRING + 1))
                sp.dma_start(ring[:, c % WRING], d["w_t"][l, c]).then_inc(S[f"ld_wt{c % WRING}"], 16)
                if c == WRING - 1:
                    sp.dma_start(tokw, d["w_tok"][l]).then_inc(S["ld_tokw"], 16)

        @block.tensor
        def _(pe):
            for n, (kind, a, b) in enumerate(groups):
                if n >= 8:
                    pe.wait_ge(S["pj_dve" if n % 2 else "pj_act"], (n - 8) // 2 + 1)
                if n == NX:
                    pe.wait_ge(S["pj_act"], NX // 2)
                    pe.wait_ge(S["pj_dve"], NX // 2)
                if kind == "x":
                    for k in range(4):
                        kk = 4 * b + k
                        i = nc.tensor.transpose(ps[:, n % 8, k * P:(k + 1) * P], e.x[:, a, kk * P:(kk + 1) * P], e.ident[:, :])
                elif kind == "T":
                    pe.wait_ge(S[f"ld_wt{a % WRING}"], 16 * (a // WRING + 1))
                    c0, c1 = (NPR, NTOK) if b else (0, NPR)
                    for k in range(KD):
                        i = nc.tensor.matmul(ps[:, n % 8, 0:c1 - c0], ring[:, a % WRING, k, :], e.hT[:, k, c0:c1],
                                             start=k == 0, stop=k == KD - 1)
                else:
                    pe.wait_ge(S["ld_tokw"], 16)
                    c0, c1 = spans[b]
                    for k in range(KD):
                        i = nc.tensor.matmul(ps[:, n % 8, 0:c1 - c0], e.hT[:, k, a * P:(a + 1) * P], tokw[:, k, c0:c1],
                                             start=k == 0, stop=k == KD - 1)
                i.then_inc(S["pj_ps"], 1)

        def place(n):
            kind, a, b = groups[n]
            if kind == "T":
                c0, c1 = (NPR, NTOK) if b else (0, NPR)
                dst = e.hgT[:, a, c0:c1] if a < HGT else e.rwT[:, a - HGT, pad_at(c0):pad_at(c0) + c1 - c0]
            else:
                c0, c1 = spans[b]
                dst = e.tok[:, a, c0:c1]
            return dst, ps[:, n % 8, 0:c1 - c0]

        @block.scalar
        def _(act):
            for n in range(0, len(groups), 2):
                act.wait_ge(S["pj_ps"], n + 1)
                kind, a, b = groups[n]
                if kind == "x":
                    g = 1 if a else 0
                    for k in range(4):
                        kk = 4 * b + k
                        i = nc.scalar.activation(e.hT[:, kk, a * P:(a + 1) * P], ps[:, n % 8, k * P:(k + 1) * P], ACT.Identity,
                                                 bias=e.modc[:, g, 0, kk:kk + 1], scale=e.modc[:, g, 1, kk:kk + 1])
                else:
                    dst, src = place(n)
                    i = nc.scalar.activation(dst, src, ACT.Copy)
                i.then_inc(S["pj_act"], 1)

        @block.vector
        def _(dve):
            v = e.chain("dve", dve)
            for col in (0, pad_at(NPR) - 1, PAD - 1):
                v.add(nc.vector.memset(e.rwT[:, :, col:col + 1], 0.0))
            for n in range(1, len(groups), 2):
                dve.wait_ge(S["pj_ps"], n + 1)
                kind, a, b = groups[n]
                if kind == "x":
                    g = 1 if a else 0
                    for k in range(4):
                        kk = 4 * b + k
                        i = nc.vector.tensor_scalar(e.hT[:, kk, a * P:(a + 1) * P], ps[:, n % 8, k * P:(k + 1) * P],
                                                    e.modc[:, g, 1, kk:kk + 1], e.modc[:, g, 0, kk:kk + 1], ALU.mult, ALU.add)
                else:
                    dst, src = place(n)
                    i = nc.vector.tensor_copy(dst, src)
                i.then_inc(S["pj_dve"], 1)
            e.done("dve", v)


ATTENTION_SEMS = (
    "st_cache", "ld_mla", "q_norm", "kv_norm", "rms", "tq_ps", "tq_ev", "tk_ps", "tk_ev", "v_ps", "v_ev", "krot_ps",
    "k_rope0", "k_rope", "qk_ps", "qk_free", "sc_ps", "sc_neg", "sc_exp", "pt_ps", "pt_sb", "pv_ps", "pv_o", "mo_ps",
    "mo_ev",
)


def phase_attention(e):
    nc, d, o, l, S, ps, tok = e.nc, e.d, e.o, e.l, e.S, e.ps, e.tok
    NKEY = NTOK + PAST
    KT = NKEY // P
    uq, z = e.part(e.FREE, 3, NH * QK)
    uk, z = e.part(z, 2, NH * NOPE)
    uv, z = e.part(z, 2, NH * DV)
    cqT, z = e.part(z, 3, NTOK)
    ckvT, z = e.part(z, 2, NKEY)
    V, z = e.part(z, KT, NH * DV)
    cache, z = e.part(z, 2, KVR + ROPE)
    QT, z = e.part(z, 2, NTOK, rows=QK)
    Kh, z = e.part(z, 2, NKEY, rows=QK)
    pr, z = e.part(z, 2, PAST + NSM)
    pT, z = e.part(z, 2, PAST + NSM)
    st, z = e.part(z, 2 * TILES)
    negm, z = e.part(z, NH * TILES)
    rsum, z = e.part(z, NH * TILES)
    rinv, z = e.part(z, NH * TILES)
    assert z <= 40600
    rt = pT[NOPE:QK].rearrange("p a b -> p (a b)")
    units = [(h, t) for h in range(NH) for t in range(TILES)]
    U = len(units)
    r1, z = e.part(z, NSM)
    assert z <= 40600, z
    r1 = r1[NOPE:QK]
    proj = ("q_grid", "rot", "q_ctx", "k_grid", "k_rest")

    with nc.Block() as block:
        @block.sync
        def _(sp):
            e.clear_last(sp)
            for dst, src in ((uq, d["w_uq"][l]), (uk, d["w_uk"][l]), (uv, d["w_uv"][l]),
                             (cache[:, :, 0:KVR], d["c_ckv"][l].rearrange("(t p) n -> p t n", p=P)),
                             (cache[:, :, KVR:], d["c_kr"][l].rearrange("(t p) n -> p t n", p=P))):
                sp.dma_start(dst, src).then_inc(S["ld_mla"], 16)
            sp.wait_ge(S["kv_norm"], 1)
            sp.dma_start(o["n_ckv"][0, l], tok[:, 0, QR:QR + KVR]).then_inc(S["st_cache"], 16)
            sp.dma_start(o["n_kr"][0, l], tok[:, 0, QR + KVR:MLA_COLS]).then_inc(S["st_cache"], 16)
            sp.wait_ge(S["st_cache"], 32)

        def head_product(pe, h, g):
            n = 5 * h + g
            if n:
                pe.wait_ge(S["qk_free"], n)
            if h >= 2 and g == 0:
                pe.wait_ge(S["sc_ps"], TILES * (h - 1))
            b = h % 2
            kind = proj[g]
            if kind in ("q_grid", "q_ctx"):
                c0, c1 = (NPR, NTOK) if kind == "q_grid" else (0, NPR)
                for k in range(3):
                    i = nc.tensor.matmul(ps[0:QK, 7, 0:c1 - c0], uq[:, k, h * QK:(h + 1) * QK], cqT[:, k, c0:c1],
                                         start=k == 0, stop=k == 2)
            elif kind == "rot":
                i = nc.tensor.matmul(ps[NOPE:QK, 7, :], e.rot[NOPE:QK, :], QT[NOPE:QK, b, NPR:NTOK], start=True, stop=True)
            else:
                c0, c1 = (NPR + PAST, NKEY) if kind == "k_grid" else (0, NPR + PAST)
                for k in range(2):
                    i = nc.tensor.matmul(ps[0:NOPE, 7, 0:c1 - c0], uk[:, k, h * NOPE:(h + 1) * NOPE], ckvT[:, k, c0:c1],
                                         start=k == 0, stop=k == 1)
            i.then_inc(S["qk_ps"], 1)

        def keys(t):
            return (0, NPR) if t == 0 else (NPR, NKEY)

        @block.tensor
        def _(pe):
            for t in range(TILES):
                pe.wait_ge(S["q_norm"], t + 1)
                if t >= 4:
                    pe.wait_ge(S["tq_ev"], t - 3)
                for k in range(3):
                    i = nc.tensor.transpose(ps[:, 2 * (t % 4), k * P:(k + 1) * P], tok[:, t, k * P:(k + 1) * P], e.ident[:, :])
                i.then_inc(S["tq_ps"], 1)
            pe.wait_ge(S["ld_mla"], 80)
            for t in range(KT):
                if t < TILES:
                    pe.wait_ge(S["kv_norm"], t + 1)
                    src = tok[:, t, QR:MLA_COLS]
                else:
                    src = cache[:, t - TILES, :]
                if t >= 4:
                    pe.wait_ge(S["tk_ev"], t - 3)
                for k in range(2):
                    nc.tensor.transpose(ps[:, 2 * (t % 4) + 1, k * P:(k + 1) * P], src[:, k * P:(k + 1) * P], e.ident[:, :])
                nc.tensor.transpose(ps[0:ROPE, 2 * (t % 4) + 1, 2 * P:3 * P], src[:, KVR:KVR + ROPE],
                                    e.ident[:, :]).then_inc(S["tk_ps"], 1)
            pe.wait_ge(S["tk_ev"], KT)
            pe.wait_ge(S["tq_ev"], TILES)
            for t in range(KT):
                if t >= 4:
                    pe.wait_ge(S["v_ev"], t - 3)
                for k in range(2):
                    i = nc.tensor.matmul(ps[:, t % 4, :], ckvT[:, k, t * P:(t + 1) * P], uv[:, k, :], start=k == 0, stop=k == 1)
                i.then_inc(S["v_ps"], 1)
            nc.tensor.matmul(ps[NOPE:QK, 6, :], e.rot[NOPE:QK, :], Kh[NOPE:QK, 0, NPR + PAST:], start=True, stop=True
                             ).then_inc(S["krot_ps"], 1)
            for g in range(5):
                if g == 1:
                    pe.wait_ge(S["qk_free"], 1)
                head_product(pe, 0, g)

            def scores(i):
                h, t = units[i]
                if t == 0:
                    pe.wait_ge(S["qk_free"], 5 * (h + 1))
                    pe.wait_ge(S["k_rope"], 1)
                if i >= 2:
                    pe.wait_ge(S["sc_exp"], i - 1)
                elif i == 0:
                    pe.wait_ge(S["v_ev"], KT)
                c0, c1 = keys(t)
                m = nc.tensor.matmul(ps[:, 2 * (i % 2), 0:min(512, c1 - c0)], QT[:, h % 2, t * P:(t + 1) * P],
                                     Kh[:, h % 2, c0:min(c0 + 512, c1)], start=True, stop=True)
                if c1 - c0 > 512:
                    m = nc.tensor.matmul(ps[:, 2 * (i % 2) + 1, 0:c1 - c0 - 512], QT[:, h % 2, t * P:(t + 1) * P],
                                         Kh[:, h % 2, c0 + 512:c1], start=True, stop=True)
                m.then_inc(S["sc_ps"], 1)

            def attend(i):
                h, t = units[i]
                c0, c1 = keys(t)
                pe.wait_ge(S["pt_sb"], i + 1)
                if i >= 2:
                    pe.wait_ge(S["pv_o"], i - 1)
                n = (c1 - c0) // P
                for k in range(n):
                    m = nc.tensor.matmul(ps[:, 6, (i % 2) * DV:(i % 2 + 1) * DV], pT[:, i % 2, k * P:(k + 1) * P],
                                         V[:, c0 // P + k, h * DV:(h + 1) * DV], start=k == 0, stop=k == n - 1)
                m.then_inc(S["pv_ps"], 1)

            scores(0)
            for i, (h, t) in enumerate(units):
                if h + 1 < NH:
                    head_product(pe, h + 1, t)
                if i + 1 < U:
                    scores(i + 1)
                if i == 1:
                    pe.wait_ge(S["k_rope"], 1)
                if i:
                    attend(i - 1)
                pe.wait_ge(S["sc_exp"], i + 1)
                if i:
                    pe.wait_ge(S["pt_sb"], i)
                c0, c1 = keys(t)
                for k in range((c1 - c0) // P):
                    m = nc.tensor.transpose(ps[:, 4 + k // 4, (k % 4) * P:(k % 4 + 1) * P], pr[:, i % 2, k * P:(k + 1) * P],
                                            e.ident[:, :])
                m.then_inc(S["pt_ps"], 1)
            attend(U - 1)
            for t in range(TILES):
                pe.wait_ge(S["pv_o"], U)
                pe.wait_ge(S["sc_exp"], U)
                if t >= 4:
                    pe.wait_ge(S["mo_ev"], t - 3)
                for k in range(4):
                    m = nc.tensor.transpose(ps[:, t % 4, k * P:(k + 1) * P], tok[:, t, k * P:(k + 1) * P], e.ident[:, :])
                m.then_inc(S["mo_ps"], 1)

        @block.scalar
        def _(act):
            a = e.chain("act", act)
            for t in range(TILES):
                a.add(nc.scalar.activation(pr[:, 0, 0:QR], tok[:, t, 0:QR], ACT.Square, accum_out=st[:, t:t + 1]))
                a.link(nc.scalar.activation(pr[:, 1, 0:KVR], tok[:, t, QR:QR + KVR], ACT.Square,
                                            accum_out=st[:, TILES + t:TILES + t + 1]))
            a.add(nc.scalar.activation(st[:, 0:TILES], st[:, 0:TILES], ACT.Sqrt, bias=e.eps[:, 0:1], scale=1.0 / QR))
            nc.scalar.activation(st[:, TILES:], st[:, TILES:], ACT.Sqrt, bias=e.eps[:, 0:1], scale=1.0 / KVR).then_inc(S["rms"], 1)
            for t in range(TILES):
                act.wait_ge(S["tq_ps"], t + 1)
                for k in range(3):
                    m = nc.scalar.activation(cqT[:, k, t * P:(t + 1) * P], ps[:, 2 * (t % 4), k * P:(k + 1) * P], ACT.Copy,
                                             scale=e.pcol[:, PC["qn"] + k:PC["qn"] + k + 1])
                m.then_inc(S["tq_ev"], 1)
            for t in range(KT):
                act.wait_ge(S["v_ps"], t + 1)
                nc.scalar.activation(V[:, t, :], ps[:, t % 4, :], ACT.Copy).then_inc(S["v_ev"], 1)

            def head_evacuate(h, g):
                kind, b = proj[g], h % 2
                if kind == "rot":
                    return
                act.wait_ge(S["qk_ps"], 5 * h + g + 1)
                if kind[0] == "q":
                    c0, c1 = (NPR, NTOK) if kind == "q_grid" else (0, NPR)
                    m = nc.scalar.activation(QT[:, b, c0:c1], ps[0:QK, 7, 0:c1 - c0], ACT.Copy)
                else:
                    c0, c1 = (NPR + PAST, NKEY) if kind == "k_grid" else (0, NPR + PAST)
                    m = nc.scalar.activation(Kh[0:NOPE, b, c0:c1], ps[0:NOPE, 7, 0:c1 - c0], ACT.Copy)
                m.then_inc(S["qk_free"], 1)

            def exponent(i):
                h, t = units[i]
                c0, c1 = keys(t)
                act.wait_ge(S["sc_neg"], i + 1)
                if i >= 2:
                    act.wait_ge(S["pt_ps"], i - 1)
                sc = ps[:, 2 * (i % 2):2 * (i % 2) + 2, :].rearrange("p a b -> p (a b)")
                nc.scalar.activation(pr[:, i % 2, 0:c1 - c0], sc[:, 0:c1 - c0], ACT.Exp, bias=negm[:, i:i + 1], scale=SCALE,
                                     accum_out=rsum[:, i:i + 1]).then_inc(S["sc_exp"], 1)

            for g in range(5):
                head_evacuate(0, g)
            exponent(0)
            for i, (h, t) in enumerate(units):
                if h + 1 < NH:
                    head_evacuate(h + 1, t)
                if i + 1 < U:
                    exponent(i + 1)
            for t in range(TILES):
                act.wait_ge(S["mo_ps"], t + 1)
                nc.scalar.activation(e.mixT[:, 0:4, t * P:(t + 1) * P], ps[:, t % 4, :].rearrange("p (k n) -> p k n", k=4),
                                     ACT.Copy).then_inc(S["mo_ev"], 1)
            e.done("act", a)

        @block.gpsimd
        def _(pool):
            pool.wait_ge(S["k_rope0"], 1)
            nc.gpsimd.tensor_copy(Kh[NOPE:QK, 1, :], Kh[NOPE:QK, 0, :]).then_inc(S["k_rope"], 1)

        @block.vector
        def _(dve):
            v = e.chain("dve", dve)
            dve.wait_ge(S["rms"], 1)
            v.link(nc.vector.reciprocal(st[:, :], st[:, :]))
            for t in range(TILES):
                nc.vector.tensor_scalar(tok[:, t, 0:QR], tok[:, t, 0:QR], st[:, t:t + 1], None, ALU.mult).then_inc(S["q_norm"], 1)
            for t in range(TILES):
                nc.vector.scalar_tensor_tensor(tok[:, t, QR:QR + KVR], tok[:, t, QR:QR + KVR], st[:, TILES + t:TILES + t + 1],
                                               e.prow[:, 0, :], ALU.mult, ALU.mult).then_inc(S["kv_norm"], 1)
            for t in range(KT):
                dve.wait_ge(S["tk_ps"], t + 1)
                at = 0 if t == 0 else (NPR + PAST + (t - 1) * P if t < TILES else NPR + (t - TILES) * P)
                v.add(nc.vector.tensor_copy(Kh[NOPE:QK, 0, at:at + P], ps[0:ROPE, 2 * (t % 4) + 1, 2 * P:3 * P]))
                nc.vector.tensor_copy(ckvT[:, :, at:at + P], ps[:, 2 * (t % 4) + 1, 0:2 * P].rearrange("p (k n) -> p k n", k=2)
                                      ).then_inc(S["tk_ev"], 1)
            g0 = NPR + PAST
            v.join()
            v.link(nc.vector.tensor_tensor(rt[:, 0:NSM], Kh[NOPE:QK, 0, g0:], e.rope[NOPE:QK, 0, :], ALU.mult))
            dve.wait_ge(S["krot_ps"], 1)
            v.link(nc.vector.tensor_tensor(r1, ps[NOPE:QK, 6, :], e.rope[NOPE:QK, 1, :], ALU.mult))
            nc.vector.tensor_tensor(Kh[NOPE:QK, 0, g0:], rt[:, 0:NSM], r1, ALU.add).then_inc(S["k_rope0"], 1)

            def rotate(h):
                b = h % 2
                dve.wait_ge(S["k_rope0"], 1)
                if h:
                    dve.wait_ge(S["qk_free"], 5 * h - 3)
                dve.wait_ge(S["qk_ps"], 5 * h + 2)
                v.link(nc.vector.tensor_tensor(r1, ps[NOPE:QK, 7, :], e.rope[NOPE:QK, 1, :], ALU.mult))
                v.link(nc.vector.tensor_tensor(QT[NOPE:QK, b, NPR:NTOK], QT[NOPE:QK, b, NPR:NTOK], e.rope[NOPE:QK, 0, :], ALU.mult))
                nc.vector.tensor_tensor(QT[NOPE:QK, b, NPR:NTOK], QT[NOPE:QK, b, NPR:NTOK], r1, ALU.add).then_inc(S["qk_free"], 1)

            def row_max(i):
                c0, c1 = keys(units[i][1])
                dve.wait_ge(S["sc_ps"], i + 1)
                sc = ps[:, 2 * (i % 2):2 * (i % 2) + 2, :].rearrange("p a b -> p (a b)")
                v.link(nc.vector.reduce_max(negm[:, i:i + 1], sc[:, 0:c1 - c0], AX))
                nc.vector.tensor_scalar(negm[:, i:i + 1], negm[:, i:i + 1], -SCALE, None, ALU.mult).then_inc(S["sc_neg"], 1)

            def output(i):
                h, t = units[i]
                dve.wait_ge(S["sc_exp"], i + 1)
                v.link(nc.vector.reciprocal(rinv[:, i:i + 1], rsum[:, i:i + 1]))
                dve.wait_ge(S["pv_ps"], i + 1)
                nc.vector.tensor_scalar(tok[:, t, h * DV:(h + 1) * DV], ps[:, 6, (i % 2) * DV:(i % 2 + 1) * DV],
                                        rinv[:, i:i + 1], None, ALU.mult).then_inc(S["pv_o"], 1)

            rotate(0)
            row_max(0)
            dve.wait_ge(S["st_cache"], 32)
            for i, (h, t) in enumerate(units):
                if t == 1 and h + 1 < NH:
                    rotate(h + 1)
                if i + 1 < U:
                    row_max(i + 1)
                if i:
                    output(i - 1)
                c0, c1 = keys(t)
                dve.wait_ge(S["pt_ps"], i + 1)
                if i >= 2:
                    dve.wait_ge(S["pv_ps"], i - 1)
                src = ps[:, 4:6, :].rearrange("p a b -> p (a b)")
                nc.vector.tensor_copy(pT[:, i % 2, 0:c1 - c0], src[:, 0:c1 - c0]).then_inc(S["pt_sb"], 1)
            output(U - 1)
            e.done("dve", v)


HGRN_SEMS = (
    "st_state", "ld_hg", "hg_q", "hg_z", "hg_e", "hg_prep", "lv0", "lv1", "at_ps", "at_sb", "oh_ps", "ou_sb",
    "kr_ps", "kr_sb", "kv_ps", "st_new", "hg_state", "hg_o", "hg_sq", "hg_ss", "hg_rt", "hg_on", "ho_ps", "ho_ev",
)


def phase_hgrn(e):
    nc, d, o, l, S, ps, tok = e.nc, e.d, e.o, e.l, e.S, e.ps, e.tok
    q = e.hgT[:, 0:2, :]
    f = e.hgT[:, 2:6, :]
    vcol, gcol = MLA_COLS, MLA_COLS + HH * HD
    kT, z = e.part(e.FREE, 4, NTOK)
    QL, KL, Pb, Rb, KRt, Sst = [], [], [], [], [], []
    for _ in range(2):
        v, z = e.part(z, LV + 1, 2, P); QL.append(v)
        v, z = e.part(z, LV, 2, P); KL.append(v)
        v, z = e.part(z, 2, P); Pb.append(v)
        v, z = e.part(z, 2, P); Rb.append(v)
        v, z = e.part(z, 2, P); KRt.append(v)
        v, z = e.part(z, 2, 2, HD); Sst.append(v)
    Sfin, z = e.part(z, 2, 2, HD)
    Ft, z = e.part(z, 2 * TILES, 2)
    am, z = e.part(z, 2, (LV + 1) * P)
    oS, z = e.part(z, TILES, HH * HD)
    ssq, z = e.part(z, TILES * HH)
    assert z <= 40600, z
    units = [(0, 0), (0, 1), (1, 0), (4, 1), (2, 0), (3, 1), (3, 0), (2, 1), (4, 0), (1, 1)]
    U = len(units)
    last = ((4, 0), (1, 1))

    def levels(eng, c, u):
        t, dr = units[u]
        cols = slice(t * P, (t + 1) * P)
        Pd, Rd = Pb[dr], Rb[dr]
        c.add(eng.tensor_copy(Pd, f[:, 2 * dr:2 * dr + 2, cols]))
        c.link(eng.memset(Rd, 1.0))
        near, far = (0, 1) if dr == 0 else (1, 0)
        yield
        for j in range(LV + 1):
            h = 1 << j
            i = c.add(eng.tensor_tensor(QL[dr][:, j], q[:, :, cols], Pd, ALU.mult))
            yield
            if j:
                c.add(eng.tensor_tensor(KL[dr][:, j - 1], kT[:, 2 * dr:2 * dr + 2, cols], Rd, ALU.mult))
                yield
            c.join()
            if j == LV:
                end = P - 1 if dr == 0 else 0
                c.link(eng.tensor_copy(Ft[:, u, :], Pd[:, :, end:end + 1].rearrange("p a b -> p (a b)")))
                break
            Pv = Pd.rearrange("p a (n s h) -> p a n s h", s=2, h=h)
            Rv = Rd.rearrange("p a (n s h) -> p a n s h", s=2, h=h)
            n = P // (2 * h)
            edge = h - 1 if dr == 0 else 0
            c.link(eng.tensor_tensor(Rv[:, :, :, near, :], Rv[:, :, :, near, :],
                                     Pv[:, :, :, far, edge:edge + 1].to_broadcast([P, 2, n, h]), ALU.mult))
            yield
            c.link(eng.tensor_tensor(Pv[:, :, :, far, :], Pv[:, :, :, far, :],
                                     Pv[:, :, :, near, edge:edge + 1].to_broadcast([P, 2, n, h]), ALU.mult))
            yield

    with nc.Block() as block:
        @block.sync
        def _(sp):
            e.clear_last(sp)
            for dr in range(2):
                sp.dma_start(Sst[dr][:, 1], d["s_hg"][l, dr].rearrange("a p v -> p a v")).then_inc(S["ld_hg"], 16)
            sp.wait_ge(S["hg_state"], 2)
            for dr in range(2):
                sp.dma_start(o["n_hg"][0, l, dr].rearrange("(a b) k v -> a (b k) v", a=2).rearrange("a p v -> p a v"),
                             Sfin[:, dr]).then_inc(S["st_state"], 16)
            sp.wait_ge(S["st_state"], 32)

        @block.scalar
        def _(act):
            a = e.chain("act", act)
            nc.scalar.activation(q, q, ACT.Silu).then_inc(S["hg_q"], 1)
            a.add(nc.scalar.activation(tok[:, :, gcol:gcol + HH * HD], tok[:, :, gcol:gcol + HH * HD], ACT.Silu))
            act.wait_ge(S["hg_z"], 1)
            nc.scalar.activation(kT, f, ACT.Exp, scale=-1.0).then_inc(S["hg_e"], 1)
            for u, (t, dr) in enumerate(units):
                if (t, dr) in last:
                    continue
                act.wait_ge(S["kr_ps"], u + 1)
                if u >= 2:
                    act.wait_ge(S["kv_ps"], u - 1)
                nc.scalar.activation(KRt[dr], ps[:, 6, 0:2 * P].rearrange("p (a b) -> p a b", a=2), ACT.Copy
                                     ).then_inc(S["kr_sb"], 1)
            act.wait_ge(S["hg_o"], 1)
            nc.scalar.activation(QL[0][:, 0:5].rearrange("p a b c -> p (a b c)"), oS.rearrange("p a b -> p (a b)"),
                                 ACT.Square).then_inc(S["hg_sq"], 1)
            act.wait_ge(S["hg_ss"], 1)
            nc.scalar.activation(ssq, ssq, ACT.Sqrt, bias=e.eps[:, 0:1], scale=1.0 / HD).then_inc(S["hg_rt"], 1)
            for t in range(TILES):
                act.wait_ge(S["ho_ps"], t + 1)
                nc.scalar.activation(e.mixT[:, 4:6, t * P:(t + 1) * P], ps[:, t % 4, 0:2 * P].rearrange("p (k n) -> p k n", k=2),
                                     ACT.Copy).then_inc(S["ho_ev"], 1)
            e.done("act", a)

        @block.gpsimd
        def _(pool):
            c = e.chain("pool", pool)
            pool.wait_ge(S["hg_prep"], 1)
            pool.wait_ge(S["hg_q"], 1)
            k = 0
            for u, (t, dr) in enumerate(units):
                if dr == 0:
                    continue
                if k:
                    pool.wait_ge(S["oh_ps"], HH * (u - 1))
                for _ in levels(nc.gpsimd, c, u):
                    pass
                k += 1
                nc.gpsimd.memset(Rb[1][:, 0, 0:1], 1.0).then_inc(S["lv1"], 1)
                pool.wait_ge(S["lv1"], k)
            e.done("pool", c)

        @block.tensor
        def _(pe):
            kr = [0]

            def att(i):
                u, h = divmod(i, HH)
                t, dr = units[u]
                cols = slice(t * P, (t + 1) * P)
                hp, r = h // 2, slice(HD * (h % 2), HD * (h % 2) + HD)
                if h == 0:
                    pe.wait_ge(S[f"lv{dr}"], u // 2 + 1)
                if i >= 2:
                    pe.wait_ge(S["at_sb"], i - 1)
                for j in range(LV + 1):
                    lhs = kT[r, 2 * dr + hp, cols] if j <= 1 else KL[dr][r, j - 2, hp, :]
                    rhs = q[r, hp, cols] if j == 0 else QL[dr][r, j - 1, hp, :]
                    m = nc.tensor.matmul(ps[:, 2 * (i % 2) + j // 4, (j % 4) * P:(j % 4 + 1) * P], lhs, rhs, start=True, stop=True)
                m.then_inc(S["at_ps"], 1)

            def out(i):
                u, h = divmod(i, HH)
                t, dr = units[u]
                hp, r = h // 2, slice(HD * (h % 2), HD * (h % 2) + HD)
                if h == 0 and u:
                    pe.wait_ge(S["ou_sb"], 2 * u)
                dst = ps[:, 4 + h % 2, hp * HD:(hp + 1) * HD]
                pe.wait_ge(S["at_sb"], i + 1)
                for j in range(LV + 1):
                    m = nc.tensor.matmul(dst, am[:, i % 2, j * P:(j + 1) * P], tok[:, t, vcol + h * HD:vcol + (h + 1) * HD],
                                         start=j == 0, stop=j == LV and t == 0)
                if t:
                    k = u // 2
                    if h == 0:
                        if k == 1:
                            pe.wait_ge(S["ld_hg"], 32)
                        else:
                            pe.wait_ge(S["st_new"], u - 1)
                    m = nc.tensor.matmul(dst, QL[dr][r, LV, hp, :], Sst[dr][r, k % 2, hp, :], start=False, stop=True)
                m.then_inc(S["oh_ps"], 1)

            for i in range(U * HH):
                u, h = divmod(i, HH)
                t, dr = units[u]
                att(i)
                if h == 0 and (t, dr) not in last:
                    if kr[0]:
                        pe.wait_ge(S["kr_sb"], kr[0])
                    for a in range(2):
                        m = nc.tensor.transpose(ps[:, 6, a * P:(a + 1) * P], KL[dr][:, LV - 1, a, :], e.ident[:, :])
                    m.then_inc(S["kr_ps"], 1)
                if i:
                    out(i - 1)
                if h == 1 and (t, dr) not in last:
                    kr[0] += 1
                    pe.wait_ge(S["kr_sb"], kr[0])
                    if kr[0] > 1:
                        pe.wait_ge(S["st_new"], kr[0] - 1)
                    for hh in range(HH):
                        m = nc.tensor.matmul(ps[HD * (hh % 2):HD * (hh % 2) + HD, 7, (hh // 2) * HD:(hh // 2 + 1) * HD],
                                             KRt[dr][:, hh // 2, HD * (hh % 2):HD * (hh % 2) + HD],
                                             tok[:, t, vcol + hh * HD:vcol + (hh + 1) * HD], start=True, stop=True)
                    m.then_inc(S["kv_ps"], 1)
            out(U * HH - 1)
            for t in range(TILES):
                pe.wait_ge(S["hg_on"], 1)
                if t >= 4:
                    pe.wait_ge(S["ho_ev"], t - 3)
                for k in range(2):
                    m = nc.tensor.transpose(ps[:, t % 4, k * P:(k + 1) * P], oS[:, t, k * P:(k + 1) * P], e.ident[:, :])
                m.then_inc(S["ho_ps"], 1)

        @block.vector
        def _(dve):
            v = e.chain("dve", dve)
            nc.vector.tensor_scalar(f, f, 60.0, -60.0, ALU.min, ALU.max).then_inc(S["hg_z"], 1)
            dve.wait_ge(S["hg_e"], 1)
            v.link(nc.vector.tensor_scalar(f, kT, 1.0, None, ALU.add))
            v.link(nc.vector.reciprocal(f, f))
            v.link(nc.vector.tensor_tensor(kT, kT, f, ALU.mult))
            for c in range(4):
                v.add(nc.vector.scalar_tensor_tensor(f[:, c, :], kT[:, c, :], e.lb[:, c:c + 1], f[:, c, :], ALU.mult, ALU.add))
            v.join()
            for c in range(4):
                m = nc.vector.tensor_scalar(kT[:, c, :], kT[:, c, :], e.oml[:, c:c + 1], None, ALU.mult)
                if c < 3:
                    v.add(m)
            v.join()
            m.then_inc(S["hg_prep"], 1)
            dve.wait_ge(S["hg_prep"], 1)
            dve.wait_ge(S["hg_q"], 1)

            def run_levels(u):
                if u:
                    dve.wait_ge(S["oh_ps"], HH * (u - 1))
                for _ in levels(nc.vector, v, u):
                    yield
                nc.vector.memset(Rb[0][:, 0, 0:1], 1.0).then_inc(S["lv0"], 1)
                dve.wait_ge(S["lv0"], u // 2 + 1)

            def collect(u):
                t, dr = units[u]
                dve.wait_ge(S["oh_ps"], HH * (u + 1))
                seen = t in [x for x, _ in units[:u]]
                if seen:
                    dve.wait_ge(S["ou_sb"], 2 * u)
                for b in range(2):
                    src = ps[:, 4 + b, 0:2 * HD].rearrange("p (a v) -> p a v", a=2)
                    dst = oS[:, t, :].rearrange("p (a b v) -> p a b v", a=2, b=2)[:, :, b, :]
                    if seen:
                        nc.vector.tensor_tensor(dst, dst, src, ALU.add).then_inc(S["ou_sb"], 1)
                    else:
                        nc.vector.tensor_copy(dst, src).then_inc(S["ou_sb"], 1)

            for _ in run_levels(0):
                pass
            ns = 0
            for u, (t, dr) in enumerate(units):
                nxt = run_levels(u + 1) if dr == 1 and u + 1 < U else None
                for h in range(HH):
                    i = u * HH + h
                    dve.wait_ge(S["at_ps"], i + 1)
                    if i >= 2:
                        dve.wait_ge(S["oh_ps"], i - 1)
                    nc.vector.tensor_tensor(am[:, i % 2, :], ps[:, 2 * (i % 2):2 * (i % 2) + 2, :].rearrange("p a b -> p (a b)"),
                                            e.hgm[:, dr, :], ALU.mult).then_inc(S["at_sb"], 1)
                    if h == 0 and u:
                        collect(u - 1)
                    if h == 2 and (t, dr) not in last:
                        ns += 1
                        dve.wait_ge(S["kv_ps"], ns)
                        v.join()
                        if dr == 0:
                            dve.wait_ge(S["lv0"], u // 2 + 1)
                        else:
                            dve.wait_ge(S["lv1"], u // 2 + 1)
                        k = u // 2
                        src = ps[:, 7, 0:2 * HD].rearrange("p (a b) -> p a b", a=2)
                        if t == 0:
                            m = nc.vector.tensor_copy(Sfin[:, dr], src)
                            m.then_inc(S["st_new"], 1)
                            dve.wait_ge(S["st_new"], ns)
                            dve.sem_inc(S["hg_state"], 1)
                        else:
                            dve.wait_ge(S["ld_hg"], 32)
                            dve.wait_ge(S["st_new"], ns - 1)
                            for a in range(2):
                                m = nc.vector.scalar_tensor_tensor(Sst[dr][:, (k + 1) % 2, a], Sst[dr][:, k % 2, a],
                                                                   Ft[:, u, a:a + 1], src[:, a], ALU.mult, ALU.add)
                                if a == 0:
                                    v.add(m)
                            v.join()
                            m.then_inc(S["st_new"], 1)
                    if nxt and h < HH - 1:
                        for _ in range(12):
                            if next(nxt, "end") == "end":
                                nxt = None
                                break
                if nxt:
                    for _ in nxt:
                        pass
            collect(U - 1)
            dve.wait_ge(S["ou_sb"], 2 * U)
            dve.sem_inc(S["hg_o"], 1)
            ov = oS.rearrange("p t (h v) -> p (t h) v", v=HD)
            dve.wait_ge(S["hg_sq"], 1)
            nc.vector.reduce_sum(ssq, QL[0][:, 0:5].rearrange("p a b c -> p (a b c)").rearrange("p (n v) -> p n v", v=HD), AX
                                 ).then_inc(S["hg_ss"], 1)
            v.link(nc.vector.tensor_tensor(oS, oS, e.prow[:, 1:2, :].to_broadcast([P, TILES, HH * HD]), ALU.mult))
            v.link(nc.vector.tensor_tensor(oS, oS, tok[:, :, gcol:gcol + HH * HD], ALU.mult))
            dve.wait_ge(S["hg_rt"], 1)
            v.link(nc.vector.reciprocal(ssq, ssq))
            nc.vector.tensor_tensor(ov, ov, ssq.rearrange("p (n o) -> p n o", o=1).to_broadcast([P, TILES * HH, HD]), ALU.mult
                                    ).then_inc(S["hg_on"], 1)
            e.done("dve", v)


RWKV_SEMS = (
    "ld_rw", "rw_om", "rw_f0", "rw_feat", "rw_th", "rw_k0", "rw_ksq", "lo_ps", "lo_ev", "vt_ps", "vt_ev", "kn_ps",
    "rw_kmax", "rw_krt", "rw_kn", "rw_kd", "rw_bon", "rw_E", "rw_ex", "rw_pre", "rw_G0", "rw_G", "m_ps", "l_ps",
    "kb_ps", "kb_sb", "mj", "x_new", "t1_ps", "t1_sb", "dy_ps", "dx_ps", "y_fin", "sm", "vz", "rh_ps", "rh_sb",
    "u_ps", "u_sb", "rs_ps", "rs_ev", "y_ps", "y_ev", "rw_sfin", "fin_ps", "rw_fin", "st_rw", "gn_c", "gn_sq",
    "gn_var", "gn_rt", "bo_ps", "ga_ps", "rw_out", "ro_ps", "ro_ev",
)


def phase_rwkv(e):
    nc, d, o, l, S, ps = e.nc, e.d, e.o, e.l, e.S, e.ps
    R = slice(0, NTOK)
    HI, LO = slice(C, P), slice(0, C)
    kk, z = e.part(e.a0, 2, NTOK)
    T, z = e.part(z, 3, NTOK)
    assert z <= e.a1
    KB, z = e.part(e.a1, 4, NCH, 2, C)
    assert z <= e.a2
    F, z = e.part(e.a2, NRW, NTOK)
    AR, z = e.part(z, 4, 2, NTOK)
    Vc, z = e.part(z, NCH, HH * HD, rows=C)
    ys, z = e.part(z, NCH, HH * HD, rows=C)
    VU, z = e.part(z, 2, 8, HD)
    KBt, z = e.part(z, 2, 2, P)
    M, z = e.part(z, 8, P)
    Mj, z = e.part(z, 5, 8, C)
    sq = Mj[LO].rearrange("p a b c -> p (a b c)")
    X, z = e.part(z, 8, C)
    Y, z = e.part(z, 8, C)
    T1, z = e.part(z, 8, C)
    RH, z = e.part(z, 8, C)
    Sm, z = e.part(z, 4, HD)
    Sn, z = e.part(z, 4, HD)
    S0, z = e.part(z, 4, HD)
    Sfin, z = e.part(z, 4, HD)
    So, z = e.part(z, 2, 2, P, rows=C)
    mid, z = e.part(z, 4, NCH)
    end, z = e.part(z, 4, NCH)
    G, z = e.part(z, 4, NCH)
    om, z = e.part(z, NRW)
    mu, z = e.part(z, NCH * HH, rows=C)
    rs, z = e.part(z, NCH * HH, rows=C)
    wwa, z = e.part(z, 2, HH * HD)
    g2, z = e.part(z, HH * HD)
    assert z <= 40600, z
    cut = ((NPR, NTOK), (0, NPR))
    DECAY = -float(np.exp(-0.5))
    units = [(par, dr, pair) for par in range(2) for dr in range(2) for pair in range(2)]
    steps = [(0, 1), (1, 0)] + [(2 + i, NCH - 1 - i) for i in range(NCH - 2)]
    NS = len(steps)
    first = (True, False) + (True,) * 4 + (False,) * 4
    pc = e.pcol

    def col(name, i):
        return pc[:, PC[name] + i:PC[name] + i + 1]

    def ck(c):
        return slice(C * c, C * c + C)

    def by_chunk(a):
        return a.rearrange("p (c t) -> p c t", t=C)

    lora = [(w, dr, pair, i) for w in range(2) for dr in range(2) for pair in range(2) for i in range(2)]

    with nc.Block() as block:
        @block.sync
        def _(sp):
            e.clear_last(sp)
            sp.dma_start(wwa, d["w_wa"][l]).then_inc(S["ld_rw"], 16)
            sp.dma_start(g2, d["w_g2"][l]).then_inc(S["ld_rw"], 16)
            sp.dma_start(S0, d["s_rw"][l].rearrange("d a p v -> p (d a) v")).then_inc(S["ld_rw"], 16)
            sp.wait_ge(S["rw_fin"], 1)
            for dr in range(2):
                for par in range(2):
                    sp.dma_start(o["n_rw"][0, l, dr].rearrange("(a b) v k -> b v a k", a=2)[par],
                                 So[:, dr, :, par * HD:(par + 1) * HD]).then_inc(S["st_rw"], 16)
            sp.wait_ge(S["st_rw"], 64)

        @block.scalar
        def _(act):
            a = e.chain("act", act)
            act.wait_ge(S["rw_om"], 1)
            for c in range(NRW):
                for c0, c1 in cut:
                    q0 = pad_at(c0)
                    nc.scalar.activation(F[:, c, c0:c1], e.rwT[:, c, q0:q0 + c1 - c0], ACT.Copy, scale=om[:, c:c + 1]
                                         ).then_inc(S["rw_f0"], 1)
            act.wait_ge(S["rw_feat"], 1)
            nc.scalar.activation(F[:, 6, R], F[:, 6, R], ACT.Tanh).then_inc(S["rw_th"], 1)
            for p in range(2):
                act.wait_ge(S["rw_k0"], p + 1)
                nc.scalar.activation(T[:, p, R], kk[:, p, R], ACT.Square).then_inc(S["rw_ksq"], 1)
            for n, (w, dr, pair, i) in enumerate(lora):
                act.wait_ge(S["lo_ps"], n + 1)
                c0, c1 = cut[i]
                dst = by_chunk(AR[:, 2 * dr + pair, 0, c0:c1]) if w == 0 else KB[:, 2 * dr + pair, c0 // C:c1 // C, 1, :]
                nc.scalar.activation(dst, by_chunk(ps[:, n % 4 * 2 + dr, 0:c1 - c0]), ACT.Sigmoid, bias=col("a0" if w else "w0", 2 * dr + pair)
                                     ).then_inc(S["lo_ev"], 1)
            a.add(nc.scalar.activation(F[:, 8, R], F[:, 8, R], ACT.Sigmoid))
            for n in range(NCH // 2):
                act.wait_ge(S["vt_ps"], n + 1)
                nc.scalar.activation(Vc[:, 2 * n:2 * n + 2, :], ps[LO, 2 * (n % 2), :].rearrange("p (a b) -> p a b", a=2), ACT.Copy
                                     ).then_inc(S["vt_ev"], 1)
            for p in range(2):
                act.wait_ge(S["rw_kmax"], p + 1)
                nc.scalar.activation(T[:, p, R], T[:, p, R], ACT.Sqrt).then_inc(S["rw_krt"], 1)
            for dp in range(4):
                act.wait_ge(S["rw_E"], dp + 1)
                nc.scalar.activation(T[:, 2, R], T[:, 0, R], ACT.Exp, scale=-1.0).then_inc(S["rw_ex"], 1)
                nc.scalar.activation(AR[:, dp, 1, R], T[:, 0, R], ACT.Exp).then_inc(S["rw_ex"], 1)
                nc.scalar.activation(AR[:, dp, 0, R], AR[:, dp, 0, R], ACT.Exp).then_inc(S["rw_ex"], 1)
            act.wait_ge(S["rw_G0"], 1)
            a.link(nc.scalar.activation(G, G, ACT.Exp))
            nc.scalar.activation(mid, mid, ACT.Exp).then_inc(S["rw_G"], 1)
            for s in range(NS):
                act.wait_ge(S["kb_ps"], s + 1)
                if s:
                    act.wait_ge(S["rs_ps"], s)
                nc.scalar.activation(KBt, ps[:, 4, :].rearrange("p (a b c) -> p a b c", a=2, b=2), ACT.Copy).then_inc(S["kb_sb"], 1)
                for j in range(5):
                    n = 5 * s + j
                    act.wait_ge(S["t1_ps"], n + 1)
                    nc.scalar.activation(T1[HI], ps[HI, 5, :].rearrange("p (a b) -> p a b", a=8), ACT.Copy).then_inc(S["t1_sb"], 1)
                act.wait_ge(S["u_ps"], s + 1)
                nc.scalar.activation(VU[HI, s % 2], ps[HI, 5, :].rearrange("p (a b) -> p a b", a=8), ACT.Copy, scale=-1.0
                                     ).then_inc(S["u_sb"], 1)
            act.wait_ge(S["fin_ps"], 1)
            nc.scalar.activation(So.rearrange("p a b c -> p (a b c)"), ps[LO, 6, :], ACT.Copy).then_inc(S["rw_fin"], 1)
            act.wait_ge(S["gn_c"], 1)
            nc.scalar.activation(sq, ys.rearrange("p a b -> p (a b)"), ACT.Square).then_inc(S["gn_sq"], 1)
            act.wait_ge(S["gn_var"], 1)
            nc.scalar.activation(rs, rs, ACT.Sqrt, bias=e.eps[LO, 2:3], scale=1.0 / HD).then_inc(S["gn_rt"], 1)
            for k in range(2):
                act.wait_ge(S["ro_ps"], k + 1)
                nc.scalar.activation(e.mixT[:, 6 + k, :], ps[:, 2 * k:2 * k + 2, :].rearrange("p a b -> p (a b)")[:, 0:NTOK],
                                     ACT.Copy).then_inc(S["ro_ev"], 1)
            e.done("act", a)

        @block.gpsimd
        def _(pool):
            c = e.chain("pool", pool)
            for dp in range(4):
                dr, p = divmod(dp, 2)
                if dp == 0:
                    pool.wait_ge(S["lo_ev"], len(lora))
                    pool.wait_ge(S["rw_kn"], 2)
                c.link(nc.gpsimd.tensor_scalar(by_chunk(T[:, 1, R]), KB[:, dp, :, 1, :], -1.0, col("ka", p), ALU.add, ALU.mult))
                c.link(nc.gpsimd.tensor_scalar(T[:, 1, R], T[:, 1, R], 1.0, None, ALU.add))
                c.link(nc.gpsimd.tensor_tensor(KB[:, dp, :, 0, :], by_chunk(T[:, 1, R]), by_chunk(F[:, 2 + p, R]), ALU.mult))
                if dr == 0:
                    c.link(nc.gpsimd.tensor_copy(by_chunk(F[:, 6 + p, R]), KB[:, dp, :, 0, :]))
                else:
                    c.link(nc.gpsimd.tensor_tensor(by_chunk(F[:, 6 + p, R]), by_chunk(F[:, 6 + p, R]), KB[:, dp, :, 0, :], ALU.add))
                nc.gpsimd.tensor_tensor(KB[:, dp, :, 1, :], KB[:, dp, :, 1, :], by_chunk(kk[:, p, R]), ALU.mult).then_inc(S["rw_kd"], 1)
                pool.wait_ge(S["rw_kd"], dp + 1)
            for p in range(2):
                c.link(nc.gpsimd.tensor_tensor(F[:, 6 + p, R], F[:, 6 + p, R], F[:, p, R], ALU.mult))
                nc.gpsimd.tensor_scalar(F[:, 6 + p, R], F[:, 6 + p, R], col("rk", p), None, ALU.mult).then_inc(S["rw_bon"], 1)
            pool.wait_ge(S["vt_ev"], NCH // 2)
            for s, chunks in enumerate(steps):
                if s >= 2:
                    pool.wait_ge(S["y_ps"], 2 * (s - 1))
                for dr in range(2):
                    for par in range(2):
                        c.add(nc.gpsimd.tensor_copy(
                            VU[LO, s % 2, 4 * par + 2 * dr:4 * par + 2 * dr + 2, :],
                            Vc[:, chunks[dr], :].rearrange("p (a b v) -> p a b v", a=2, b=2)[:, :, par, :]))
                c.join()
                nc.gpsimd.memset(VU[HI, s % 2], 0.0).then_inc(S["vz"], 1)
            e.done("pool", c)

        @block.tensor
        def _(pe):
            pe.wait_ge(S["ld_rw"], 48)
            pe.wait_ge(S["rw_th"], 1)
            for n, (w, dr, pair, i) in enumerate(lora):
                if n >= 4:
                    pe.wait_ge(S["lo_ev"], n - 3)
                c0, c1 = cut[i]
                r = slice(C * dr, C * dr + C)
                nc.tensor.matmul(ps[:, n % 4 * 2 + dr, 0:c1 - c0], wwa[r, w, pair * P:(pair + 1) * P], F[r, 6 + w, c0:c1],
                                 start=True, stop=True).then_inc(S["lo_ps"], 1)
            pe.wait_ge(S["lo_ev"], len(lora))
            for n in range(NCH // 2):
                if n >= 2:
                    pe.wait_ge(S["vt_ev"], n - 1)
                for i in range(2):
                    for p in range(2):
                        m = nc.tensor.transpose(ps[LO, 2 * (n % 2), i * 256 + p * P:i * 256 + (p + 1) * P], F[:, 4 + p, ck(2 * n + i)],
                                                e.ident[:, :])
                m.then_inc(S["vt_ps"], 1)
            for p in range(2):
                pe.wait_ge(S["rw_ksq"], p + 1)
                for i, (c0, c1) in enumerate(cut):
                    m = nc.tensor.matmul(ps[:, 4 + 2 * p + i, 0:c1 - c0], e.blk[:, :], T[:, p, c0:c1], start=True, stop=True)
                    m.then_inc(S["kn_ps"], 1)
            pe.wait_ge(S["rw_pre"], 4)
            pe.wait_ge(S["rw_G"], 1)
            for s, chunks in enumerate(steps):
                if s:
                    pe.wait_ge(S["y_ev"], s)
                    pe.wait_ge(S["rh_sb"], s)
                for u, (par, dr, pair) in enumerate(units):
                    r, cc, dp = slice(HD * par, HD * par + HD), ck(chunks[dr]), 2 * dr + pair
                    m = nc.tensor.matmul(ps[:, par, (u % 4) * P:(u % 4 + 1) * P], KB[r, dp, chunks[dr]].rearrange("p a b -> p (a b)"), AR[r, dp, :, cc],
                                         start=True, stop=True)
                    if u == 3:
                        m.then_inc(S["m_ps"], 1)
                m.then_inc(S["m_ps"], 1)
                for u, (par, dr, pair) in enumerate(units):
                    r, cc, dp = slice(HD * par, HD * par + HD), ck(chunks[dr]), 2 * dr + pair
                    m = nc.tensor.matmul(ps[HI, 2 + par, (u % 4) * C:(u % 4 + 1) * C], AR[r, dp, 0, cc], KB[r, dp, chunks[dr], 1, :],
                                         start=True, stop=True)
                    if u == 3:
                        m.then_inc(S["l_ps"], 1)
                m.then_inc(S["l_ps"], 1)
                if s:
                    pe.wait_ge(S["rs_ev"], s)
                for dp in range(4):
                    m = nc.tensor.transpose(ps[:, 4, dp * P:(dp + 1) * P], KB[:, dp, chunks[dp // 2]].rearrange("p a b -> p (a b)"), e.ident[:, :])
                m.then_inc(S["kb_ps"], 1)
                for j in range(5):
                    n = 5 * s + j
                    pe.wait_ge(S["x_new"], n + 1)
                    pe.wait_ge(S["mj"], n + 1)
                    if s and j == 0:
                        pe.wait_ge(S["u_sb"], s)
                    for u in range(8):
                        m = nc.tensor.matmul(ps[HI, 5, u * C:(u + 1) * C], Mj[HI, j, u, :], X[HI, u, :], start=True, stop=True)
                    m.then_inc(S["t1_ps"], 1)
                    pe.wait_ge(S["t1_sb"], n + 1)
                    for u in range(8):
                        m = nc.tensor.matmul(ps[HI, 7, u * C:(u + 1) * C], T1[HI, u, :], Y[HI, u, :], start=True, stop=True)
                    m.then_inc(S["dy_ps"], 1)
                    if j < 4:
                        for u in range(8):
                            m = nc.tensor.matmul(ps[HI, 6, u * C:(u + 1) * C], Y[HI, u, :], T1[HI, u, :], start=True, stop=True)
                        m.then_inc(S["dx_ps"], 1)
                pe.wait_ge(S["sm"], s + 1)
                pe.wait_ge(S["vz"], s + 1)
                pe.wait_ge(S["y_fin"], s + 1)
                for u, (par, dr, pair) in enumerate(units):
                    r, cc, dp = slice(HD * par, HD * par + HD), ck(chunks[dr]), 2 * dr + pair
                    dst = ps[HI, 2 + par, (u % 4) * C:(u % 4 + 1) * C]
                    nc.tensor.matmul(dst, AR[r, dp, 0, cc], Sm[r, dp, :], start=True, stop=False)
                    m = nc.tensor.matmul(dst, M[:, u, 0:C], VU[:, s % 2, u, :], start=False, stop=True)
                    if u == 3:
                        m.then_inc(S["rh_ps"], 1)
                m.then_inc(S["rh_ps"], 1)
                pe.wait_ge(S["rh_sb"], s + 1)
                for u in range(8):
                    m = nc.tensor.matmul(ps[HI, 5, u * C:(u + 1) * C], Y[HI, u, :], RH[HI, u, :], start=True, stop=True)
                m.then_inc(S["u_ps"], 1)
                pe.wait_ge(S["u_sb"], s + 1)
                pe.wait_ge(S["kb_sb"], s + 1)
                for u, (par, dr, pair) in enumerate(units):
                    dp = 2 * dr + pair
                    m = nc.tensor.matmul(ps[HD * par:HD * par + HD, 4, dp * HD:(dp + 1) * HD], KBt[:, dr, pair, par * HD:(par + 1) * HD],
                                         VU[:, s % 2, u, :], start=True, stop=True)
                m.then_inc(S["rs_ps"], 1)
                for u, (par, dr, pair) in enumerate(units):
                    r, cc, dp = slice(HD * par, HD * par + HD), ck(chunks[dr]), 2 * dr + pair
                    dst = ps[LO, par, (u % 4) * C:(u % 4 + 1) * C]
                    nc.tensor.matmul(dst, AR[r, dp, 1, cc], Sm[r, dp, :], start=True, stop=False)
                    m = nc.tensor.matmul(dst, M[:, u, C:P], VU[:, s % 2, u, :], start=False, stop=True)
                    if u == 3:
                        m.then_inc(S["y_ps"], 1)
                m.then_inc(S["y_ps"], 1)
            pe.wait_ge(S["rw_sfin"], 1)
            for dp in range(4):
                m = nc.tensor.transpose(ps[LO, 6, dp * P:(dp + 1) * P], Sfin[:, dp, :], e.ident[:, :])
            m.then_inc(S["fin_ps"], 1)
            pe.wait_ge(S["rw_bon"], 2)
            pe.wait_ge(S["y_ev"], NS)
            pe.wait_ge(S["rs_ev"], NS)
            for c in range(NCH):
                for p in range(2):
                    m = nc.tensor.matmul(ps[LO, 7, c * HH + 2 * p:c * HH + 2 * p + 2], F[:, 6 + p, ck(c)], e.blk[:, 0:P:C],
                                         start=True, stop=True)
            m.then_inc(S["bo_ps"], 1)
            for c in range(NCH):
                m = nc.tensor.matmul(ps[LO, c // 2, (c % 2) * 256:(c % 2 + 1) * 256], F[:, 8, ck(c)], g2, start=True, stop=True)
            m.then_inc(S["ga_ps"], 1)
            pe.wait_ge(S["rw_out"], 1)
            for k in range(2):
                for c in range(NCH):
                    m = nc.tensor.transpose(ps[:, 2 * k + c // 8, (c % 8) * C:(c % 8 + 1) * C], ys[:, c, k * P:(k + 1) * P],
                                            e.ident[LO, LO])
                m.then_inc(S["ro_ps"], 1)

        @block.vector
        def _(dve):
            v = e.chain("dve", dve)
            mu0, mu1 = (pc[:, PC[n]:PC[n] + NRW] for n in ("mu0", "mu1"))
            v.link(nc.vector.tensor_tensor(om, mu0, mu1, ALU.add))
            nc.vector.tensor_scalar(om, om, -1.0, 1.0, ALU.mult, ALU.add).then_inc(S["rw_om"], 1)
            for c in range(NRW):
                dve.wait_ge(S["rw_f0"], 2 * (c + 1))
                for c0, c1 in cut:
                    q0 = pad_at(c0) - 1
                    v.add(nc.vector.scalar_tensor_tensor(F[:, c, c0:c1], e.rwT[:, c, q0:q0 + c1 - c0], col("mu0", c), F[:, c, c0:c1],
                                                         ALU.mult, ALU.add))
            v.join()
            for c in range(NRW):
                for c0, c1 in cut:
                    q0 = pad_at(c0) + 1
                    v.add(nc.vector.scalar_tensor_tensor(F[:, c, c0:c1], e.rwT[:, c, q0:q0 + c1 - c0], col("mu1", c), F[:, c, c0:c1],
                                                         ALU.mult, ALU.add))
            v.join()
            dve.sem_inc(S["rw_feat"], 1)
            dve.wait_ge(S["rw_feat"], 1)
            for p in range(2):
                nc.vector.tensor_scalar(kk[:, p, R], F[:, 2 + p, R], col("kk", p), None, ALU.mult).then_inc(S["rw_k0"], 1)
            for p in range(2):
                dve.wait_ge(S["kn_ps"], 2 * p + 2)
                for i, (c0, c1) in enumerate(cut):
                    m = nc.vector.tensor_scalar(T[:, p, c0:c1], ps[:, 4 + 2 * p + i, 0:c1 - c0], 1e-12, None, ALU.max)
                    if i == 0:
                        v.link(m)
                m.then_inc(S["rw_kmax"], 1)
            for p in range(2):
                dve.wait_ge(S["rw_krt"], p + 1)
                v.link(nc.vector.reciprocal(T[:, p, R], T[:, p, R]))
                dve.wait_ge(S["rw_k0"], p + 1)
                nc.vector.tensor_tensor(kk[:, p, R], kk[:, p, R], T[:, p, R], ALU.mult).then_inc(S["rw_kn"], 1)
            dve.wait_ge(S["rw_kn"], 2)
            dve.wait_ge(S["lo_ev"], len(lora))
            for dp in range(4):
                dr, p = divmod(dp, 2)
                lw = AR[:, dp, 0, R]
                v.link(nc.vector.tensor_scalar(lw, lw, DECAY, None, ALU.mult))
                if dp:
                    dve.wait_ge(S["rw_ex"], 3 * dp)
                a, b, c = e.reset[:, dr, R], lw, T[:, 0, R]
                if dr:
                    a, b, c = a[:, ::-1], b[:, ::-1], c[:, ::-1]
                v.link(nc.vector.tensor_tensor_scan(c, a, b, 0.0, ALU.mult, ALU.add))
                m0, e0 = (C // 2 - 1, C - 1) if dr == 0 else (C // 2, 0)
                g = by_chunk(T[:, 0, R])
                per = lambda a: a[:, dp, :].rearrange("p (c o) -> p c o", o=1)
                v.add(nc.vector.tensor_copy(per(mid), g[:, :, m0:m0 + 1]))
                v.link(nc.vector.tensor_copy(per(end), g[:, :, e0:e0 + 1]))
                v.link(nc.vector.tensor_tensor(g, g, per(mid).to_broadcast([P, NCH, C]), ALU.subtract))
                nc.vector.tensor_tensor(lw, T[:, 0, R], lw, ALU.subtract).then_inc(S["rw_E"], 1)
                dve.wait_ge(S["rw_E"], dp + 1)
                dve.wait_ge(S["rw_kd"], dp + 1)
                dve.wait_ge(S["rw_ex"], 3 * dp + 1)
                for w in range(2):
                    v.add(nc.vector.tensor_tensor(KB[:, dp, :, w, :], KB[:, dp, :, w, :], by_chunk(T[:, 2, R]), ALU.mult))
                dve.wait_ge(S["rw_ex"], 3 * dp + 2)
                v.add(nc.vector.tensor_tensor(AR[:, dp, 1, R], AR[:, dp, 1, R], F[:, p, R], ALU.mult))
                dve.wait_ge(S["rw_ex"], 3 * dp + 3)
                m = nc.vector.tensor_tensor(lw, lw, kk[:, p, R], ALU.mult)
                v.link(m)
                dve.sem_inc(S["rw_pre"], 1)
            v.link(nc.vector.tensor_tensor(G, end, mid, ALU.subtract))
            for dst, src, rows in ((slice(0, 1), slice(1, 2), (0, 2)), (slice(2, NCH - 1), slice(3, NCH), (0, 2)),
                                   (slice(1, 2), slice(0, 1), (2, 4)), (slice(3, NCH), slice(2, NCH - 1), (2, 4))):
                q = slice(*rows)
                v.link(nc.vector.tensor_tensor(G[:, q, dst], G[:, q, dst], mid[:, q, src], ALU.add))
            dve.sem_inc(S["rw_G0"], 1)
            v.link(nc.vector.memset(Sm, 0.0))
            dve.wait_ge(S["rw_G"], 1)
            dve.wait_ge(S["ld_rw"], 48)
            for dr, c in ((0, 2), (1, NCH - 1)):
                v.link(nc.vector.tensor_tensor(S0[:, 2 * dr:2 * dr + 2, :], S0[:, 2 * dr:2 * dr + 2, :],
                                               mid[:, 2 * dr:2 * dr + 2, c:c + 1].to_broadcast([P, 2, HD]), ALU.mult))
            dve.sem_inc(S["sm"], 1)
            for s, chunks in enumerate(steps):
                for par in range(2):
                    dve.wait_ge(S["m_ps"], 2 * s + par + 1)
                    m = nc.vector.tensor_tensor(M[:, 4 * par:4 * par + 4, :].rearrange("p (a b) c -> p a b c", a=2),
                                                ps[:, par, :].rearrange("p (a b c) -> p a b c", a=2, b=2),
                                                e.rwm[:, :, :].rearrange("p a (o c) -> p a o c", o=1).to_broadcast([P, 2, 2, P]), ALU.mult)
                    v.add(m)
                v.join()
                Mv = M[HI, :, 0:C]

                def level(dr, j):
                    return e.rwl[HI, dr, j:j + 1, :].to_broadcast([C, 2, C])

                for j in range(5):
                    for par in range(2):
                        for dr in range(2):
                            us = slice(4 * par + 2 * dr, 4 * par + 2 * dr + 2)
                            m = nc.vector.tensor_tensor(Mj[HI, j, us, :], M[HI, us, 0:C], level(dr, j + 1), ALU.mult)
                            v.add(m)
                    v.join()
                    dve.sem_inc(S["mj"], 1)
                    if j == 0:
                        for par in range(2):
                            for dr in range(2):
                                us = slice(4 * par + 2 * dr, 4 * par + 2 * dr + 2)
                                dve.wait_ge(S["l_ps"], 2 * s + par + 1)
                                lp = ps[HI, 2 + par, 2 * dr * C:(2 * dr + 2) * C].rearrange("p (a b) -> p a b", a=2)
                                v.add(nc.vector.tensor_tensor(X[HI, us, :], lp, level(1 - dr, 0), ALU.mult))
                                v.add(nc.vector.tensor_tensor(Y[HI, us, :], M[HI, us, 0:C], level(dr, 0), ALU.mult))
                        v.join()
                        idn = e.ident[HI, C:P].rearrange("p (o c) -> p o c", o=1).to_broadcast([C, 8, C])
                        v.link(nc.vector.tensor_tensor(X[HI], idn, X[HI], ALU.subtract))
                        v.link(nc.vector.tensor_tensor(Y[HI], idn, Y[HI], ALU.subtract))
                        dve.sem_inc(S["x_new"], 1)
                for j in range(5):
                    n = 5 * s + j
                    dve.wait_ge(S["dy_ps"], n + 1)
                    if j < 4:
                        dve.wait_ge(S["dx_ps"], 4 * s + j + 1)
                        v.add(nc.vector.tensor_tensor(X[HI], X[HI], ps[HI, 6, :].rearrange("p (a b) -> p a b", a=8), ALU.subtract))
                    v.link(nc.vector.tensor_tensor(Y[HI], Y[HI], ps[HI, 7, :].rearrange("p (a b) -> p a b", a=8), ALU.subtract))
                    dve.sem_inc(S["x_new" if j < 4 else "y_fin"], 1)
                for par in range(2):
                    dve.wait_ge(S["rh_ps"], 2 * s + par + 1)
                    v.add(nc.vector.tensor_copy(RH[HI, 4 * par:4 * par + 4, :], ps[HI, 2 + par, 0:4 * C].rearrange("p (a b) -> p a b", a=4)))
                v.join()
                dve.sem_inc(S["rh_sb"], 1)
                dve.wait_ge(S["rs_ps"], s + 1)
                v.link(nc.vector.tensor_tensor(Sn, Sm, ps[:, 4, 0:4 * HD].rearrange("p (a b) -> p a b", a=4), ALU.add))
                dve.sem_inc(S["rs_ev"], 1)
                for par in range(2):
                    dve.wait_ge(S["y_ps"], 2 * s + par + 1)
                    for dr in range(2):
                        dst = ys[:, chunks[dr], :].rearrange("p (a b v) -> p a b v", a=2, b=2)[:, :, par, :]
                        src = ps[LO, par, 2 * dr * C:(2 * dr + 2) * C].rearrange("p (a b) -> p a b", a=2)
                        if first[s]:
                            v.add(nc.vector.tensor_copy(dst, src))
                        else:
                            v.add(nc.vector.tensor_tensor(dst, dst, src, ALU.add))
                v.join()
                dve.sem_inc(S["y_ev"], 1)
                to = Sfin if s == 1 else Sm
                for dr in range(2):
                    q = slice(2 * dr, 2 * dr + 2)
                    v.add(nc.vector.tensor_tensor(to[:, q, :], Sn[:, q, :], G[:, q, chunks[dr]:chunks[dr] + 1].to_broadcast([P, 2, HD]),
                                                  ALU.mult))
                v.join()
                if s == 1:
                    v.link(nc.vector.tensor_copy(Sm, S0))
                    dve.sem_inc(S["rw_sfin"], 1)
                dve.sem_inc(S["sm"], 1)
            yv = ys.rearrange("p c (h v) -> p (c h) v", v=HD)
            col3 = lambda a: a.rearrange("p (n o) -> p n o", o=1).to_broadcast([C, NCH * HH, HD])
            row3 = lambda i: e.prow[LO, i:i + 1, :].to_broadcast([C, NCH, HH * HD])
            v.link(nc.vector.reduce_sum(mu, yv, AX))
            v.link(nc.vector.tensor_scalar(mu, mu, 1.0 / HD, None, ALU.mult))
            v.link(nc.vector.tensor_tensor(yv, yv, col3(mu), ALU.subtract))
            dve.sem_inc(S["gn_c"], 1)
            dve.wait_ge(S["gn_sq"], 1)
            v.link(nc.vector.reduce_sum(rs, sq.rearrange("p (n v) -> p n v", v=HD), AX))
            dve.sem_inc(S["gn_var"], 1)
            dve.wait_ge(S["gn_rt"], 1)
            v.link(nc.vector.reciprocal(rs, rs))
            v.link(nc.vector.tensor_tensor(yv, yv, col3(rs), ALU.mult))
            v.link(nc.vector.tensor_tensor(ys, ys, row3(2), ALU.mult))
            v.link(nc.vector.tensor_tensor(ys, ys, row3(3), ALU.add))
            dve.wait_ge(S["bo_ps"], 1)
            v.link(nc.vector.tensor_copy(mu, ps[LO, 7, 0:NCH * HH]))
            Vv = Vc.rearrange("p c (h v) -> p (c h) v", v=HD)
            v.link(nc.vector.tensor_tensor(Vv, Vv, col3(mu), ALU.mult))
            v.link(nc.vector.tensor_tensor(ys, ys, Vc, ALU.add))
            dve.wait_ge(S["ga_ps"], 1)
            v.link(nc.vector.tensor_tensor(ys.rearrange("p c v -> p (c v)"), ys.rearrange("p c v -> p (c v)"),
                                           ps[LO, 0:5, :].rearrange("p a b -> p (a b)"), ALU.mult))
            dve.sem_inc(S["rw_out"], 1)
            e.done("dve", v)


def norm_steps(e, pre, src, brow, gb, y, st, src_ready, src_sem):
    nc, S, x = e.nc, e.S, e.x

    def vector(dve, v):
        dve.wait_ge(S[pre + "ld"], 32)
        for t in range(TILES):
            g = 1 if t else 0
            b = t % 2
            src_ready(dve, t)
            if t >= 2:
                dve.wait_ge(S[pre + "xn"], t - 1)
            for n in range(2):
                m = nc.vector.tensor_tensor(y[:, b, n * 512:(n + 1) * 512], src(t, n), brow[:, g, n * 512:(n + 1) * 512], ALU.mult)
                v.add(m)
            v.join()
            if src_sem:
                dve.sem_inc(S[src_sem], 1)
            v.link(nc.vector.scalar_tensor_tensor(y[:, b, :], x[:, t, :], ALPHA, y[:, b, :], ALU.mult, ALU.add))
            for n in range(2):
                v.add(nc.vector.bn_stats(st[:, t, 6 * n:6 * n + 6], y[:, b, n * 512:(n + 1) * 512]))
            v.join()
            v.link(nc.vector.bn_aggr(st[:, t, 12:14], st[:, t, 0:12]))
            dve.sem_inc(S[pre + "var"], 1)
            dve.wait_ge(S[pre + "sd"], t + 1)
            v.link(nc.vector.reciprocal(st[:, t, 14:15], st[:, t, 14:15]))
            v.link(nc.vector.tensor_scalar(st[:, t, 15:16], st[:, t, 12:13], st[:, t, 14:15], -1.0, ALU.mult, ALU.mult))
            dve.sem_inc(S[pre + "nm"], 1)

    def scalar(act):
        for t in range(TILES):
            act.wait_ge(S[pre + "var"], t + 1)
            nc.scalar.activation(st[:, t, 14:15], st[:, t, 13:14], ACT.Sqrt, bias=e.eps[:, 1:2]).then_inc(S[pre + "sd"], 1)
            act.wait_ge(S[pre + "nm"], t + 1)
            nc.scalar.activation(x[:, t, :], y[:, t % 2, :], ACT.Identity, bias=st[:, t, 15:16], scale=st[:, t, 14:15]
                                 ).then_inc(S[pre + "xn"], 1)

    def pool(pl, c):
        pl.wait_ge(S[pre + "ld"], 32)
        for t in range(TILES):
            pl.wait_ge(S[pre + "xn"], t + 1)
            c.link(nc.gpsimd.tensor_tensor(x[:, t, :], x[:, t, :], gb[:, 0, :], ALU.mult))
            nc.gpsimd.tensor_tensor(x[:, t, :], x[:, t, :], gb[:, 1, :], ALU.add).then_inc(S[pre + "x"], 1)

    def loads(sp, which):
        d, l = e.d, e.l
        for g in range(2):
            sp.dma_start(brow[:, g, :], e.mod_d[g, 2 + 3 * which].rearrange("k p -> (k p)").rearrange("(o n) -> o n", o=1)
                         .to_broadcast([P, DM])).then_inc(S[pre + "ldg"], 16)
        sp.dma_start(gb[:, 0, :], d["ln_g"][l, which].rearrange("(o n) -> o n", o=1).to_broadcast([P, DM])).then_inc(S[pre + "ldg"], 16)
        sp.dma_start(gb[:, 1, :], d["ln_b"][l, which].rearrange("(o n) -> o n", o=1).to_broadcast([P, DM])).then_inc(S[pre + "ldg"], 16)
        sp.wait_ge(S[pre + "ldg"], 64)
        sp.sem_inc(S[pre + "ld"], 32)

    return vector, scalar, pool, loads


OUTPUT_SEMS = (
    "n1x", "op_ps", "op_ev", "st_x", "n1ld", "n1ldg", "n1var", "n1sd", "n1nm", "n1xn", "ld_wo0", "ld_wo1",
)


def phase_output(e):
    nc, d, l, S, ps = e.nc, e.d, e.l, e.S, e.ps
    z = e.a0
    wo, z = e.part(z, 2, KD, 512)
    brow, z = e.part(z, 2, DM)
    gb, z = e.part(z, 2, DM)
    y, z = e.part(z, 2, DM)
    st, z = e.part(z, TILES, 16)

    def ready(dve, t):
        dve.wait_ge(S["op_ps"], 2 * t + 2)

    vector, scalar, pool, loads = norm_steps(
        e, "n1", lambda t, n: ps[:, 2 * (t % 4) + n, :], brow, gb, y, st, ready, "op_ev")
    with nc.Block() as block:
        @block.sync
        def _(sp):
            e.clear_last(sp)
            for n in range(2):
                sp.dma_start(wo[:, n], d["w_out"][l].rearrange("(k p) n -> p k n", p=P)[:, :, n * 512:(n + 1) * 512]
                             ).then_inc(S[f"ld_wo{n}"], 16)
            loads(sp, 0)
            for t in range(TILES):
                sp.wait_ge(S["n1x"], t + 1)
                sp.dma_start(e.h2_d[t * P:(t + 1) * P, :], e.x[:, t, :]).then_inc(S["st_x"], 16)
            sp.wait_ge(S["st_x"], 16 * TILES)

        @block.tensor
        def _(pe):
            for t in range(TILES):
                if t >= 4:
                    pe.wait_ge(S["op_ev"], t - 3)
                for n in range(2):
                    if t == 0:
                        pe.wait_ge(S[f"ld_wo{n}"], 16)
                    for k in range(KD):
                        m = nc.tensor.matmul(ps[:, 2 * (t % 4) + n, :], e.mixT[:, k, t * P:(t + 1) * P], wo[:, n, k, :],
                                             start=k == 0, stop=k == KD - 1)
                    m.then_inc(S["op_ps"], 1)

        @block.vector
        def _(dve):
            v = e.chain("dve", dve)
            vector(dve, v)
            e.done("dve", v)

        @block.scalar
        def _(act):
            scalar(act)

        @block.gpsimd
        def _(pl):
            c = e.chain("pool", pl)
            pool(pl, c)
            e.done("pool", c)


def expert_memory(e):
    z = 0
    r = {}
    r["w"], z = e.part(z, 12, 2048)
    r["yacc"], z = e.part(z, TILES, DM)
    r["xe"], z = e.part(z, 2, DM, rows=CAP)
    r["xT"], z = e.part(z, KD, CAP)
    r["hs"], z = e.part(z, 2, CAP)
    r["hT"], z = e.part(z, KD, CAP)
    r["ye"], z = e.part(z, 2, DM, rows=CAP)
    r["Gm"], z = e.part(z, 2, NTOK, rows=CAP)
    r["idx"], z = e.part(z, NE, rows=CAP)
    r["gate"], z = e.part(z, NE, rows=CAP)
    r["iu"], z = e.part(z, NE, rows=CAP, dt=U32)
    r["ic"], z = e.part(z, 2, rows=CAP, dt=U32)
    r["iota"], z = e.part(z, NTOK, rows=CAP)
    assert z <= 40600, z
    return r


ROUTE_SEMS = (
    "ld_rt", "rx_ps", "rx_act", "rx_dve", "lg_ps", "lg_c", "lg_e", "aff", "af_ps", "top", "ti_ps",
)


def phase_route(e):
    nc, d, l, S, ps = e.nc, e.d, e.l, e.S, e.ps
    mem = expert_memory(e)
    idx, gate, iu, iota = mem["idx"], mem["gate"], mem["iu"], mem["iota"]
    hT, z = e.part(0, KD, NTOK)
    rt, z = e.part(z, KD, NE)
    lg, z = e.part(z, TILES, NE)
    mx, z = e.part(z, TILES)
    aT, z = e.part(z, NTOK, rows=NE)
    val, z = e.part(z, CAP, rows=NE)
    pos, z = e.part(z, CAP, rows=NE, dt=U32)
    pf, z = e.part(z, CAP, rows=NE)
    base, z = e.part(z, CAP, rows=NE)
    assert z <= 12 * 2048
    NG = 2 * TILES
    with nc.Block() as block:
        @block.sync
        def _(sp):
            e.clear_last(sp)
            sp.dma_start(rt, d["router"][l]).then_inc(S["ld_rt"], 16)
            sp.dma_start(base, d["base"]).then_inc(S["ld_rt"], 16)
            sp.dma_start(iota, d["iota"][0:CAP, :]).then_inc(S["ld_rt"], 16)
            sp.wait_ge(S["ld_rt"], 48)

        @block.tensor
        def _(pe):
            for n in range(NG):
                t, b = divmod(n, 2)
                if n >= 8:
                    pe.wait_ge(S["rx_dve" if n % 2 else "rx_act"], (n - 8) // 2 + 1)
                for k in range(4):
                    kk = 4 * b + k
                    m = nc.tensor.transpose(ps[:, n % 8, k * P:(k + 1) * P], e.x[:, t, kk * P:(kk + 1) * P], e.ident[:, :])
                m.then_inc(S["rx_ps"], 1)
            pe.wait_ge(S["rx_act"], TILES)
            pe.wait_ge(S["rx_dve"], TILES)
            pe.wait_ge(S["ld_rt"], 48)
            for t in range(TILES):
                for k in range(KD):
                    m = nc.tensor.matmul(ps[:, 0, t * NE:(t + 1) * NE], hT[:, k, t * P:(t + 1) * P], rt[:, k, :],
                                         start=k == 0, stop=k == KD - 1)
            m.then_inc(S["lg_ps"], 1)
            pe.wait_ge(S["aff"], 1)
            for t in range(TILES):
                m = nc.tensor.transpose(ps[0:NE, 1 + t // 4, (t % 4) * P:(t % 4 + 1) * P], lg[:, t, :], e.ident[:, :])
            m.then_inc(S["af_ps"], 1)
            pe.wait_ge(S["top"], 1)
            nc.tensor.transpose(ps[0:CAP, 3, 0:NE], pf, e.ident[0:NE, 0:NE])
            nc.tensor.transpose(ps[0:CAP, 3, NE:2 * NE], val, e.ident[0:NE, 0:NE]).then_inc(S["ti_ps"], 1)

        @block.scalar
        def _(act):
            for n in range(0, NG, 2):
                t, b = divmod(n, 2)
                g = 1 if t else 0
                act.wait_ge(S["rx_ps"], n + 1)
                for k in range(4):
                    kk = 4 * b + k
                    m = nc.scalar.activation(hT[:, kk, t * P:(t + 1) * P], ps[:, n % 8, k * P:(k + 1) * P], ACT.Identity,
                                             bias=e.modc[:, g, 3, kk:kk + 1], scale=e.modc[:, g, 4, kk:kk + 1])
                m.then_inc(S["rx_act"], 1)
            act.wait_ge(S["lg_c"], 1)
            nc.scalar.activation(lg, lg, ACT.Exp).then_inc(S["lg_e"], 1)

        @block.vector
        def _(dve):
            v = e.chain("dve", dve)
            for n in range(1, NG, 2):
                t, b = divmod(n, 2)
                g = 1 if t else 0
                dve.wait_ge(S["rx_ps"], n + 1)
                for k in range(4):
                    kk = 4 * b + k
                    m = nc.vector.tensor_scalar(hT[:, kk, t * P:(t + 1) * P], ps[:, n % 8, k * P:(k + 1) * P],
                                                e.modc[:, g, 4, kk:kk + 1], e.modc[:, g, 3, kk:kk + 1], ALU.mult, ALU.add)
                m.then_inc(S["rx_dve"], 1)
            dve.wait_ge(S["lg_ps"], 1)
            v.link(nc.vector.tensor_copy(lg, ps[:, 0, 0:TILES * NE].rearrange("p (a b) -> p a b", a=TILES)))
            m3 = mx.rearrange("p (n o) -> p n o", o=1).to_broadcast([P, TILES, NE])
            v.link(nc.vector.reduce_max(mx, lg, AX))
            v.link(nc.vector.tensor_tensor(lg, lg, m3, ALU.subtract))
            dve.sem_inc(S["lg_c"], 1)
            dve.wait_ge(S["lg_e"], 1)
            v.link(nc.vector.reduce_sum(mx, lg, AX))
            v.link(nc.vector.reciprocal(mx, mx))
            v.link(nc.vector.tensor_tensor(lg, lg, m3, ALU.mult))
            dve.sem_inc(S["aff"], 1)
            dve.wait_ge(S["af_ps"], 1)
            v.link(nc.vector.tensor_copy(aT, ps[0:NE, 1:3, :].rearrange("p a b -> p (a b)")[:, 0:NTOK]))
            for c0, c1, k0, k1 in ((NPR, NTOK, 0, CAPS), (0, NPR, CAPS, CAP)):
                for k in range(k0, k1, 8):
                    v.link(nc.vector.max(val[:, k:k + 8], aT[:, c0:c1]))
                    v.link(nc.vector.max_index(pos[:, k:k + 8], val[:, k:k + 8], aT[:, c0:c1]))
                    v.link(nc.vector.match_replace(aT[:, c0:c1], val[:, k:k + 8], aT[:, c0:c1], -1.0))
            v.link(nc.vector.tensor_copy(pf, pos))
            dve.wait_ge(S["ld_rt"], 48)
            v.link(nc.vector.tensor_tensor(pf, pf, base, ALU.add))
            dve.sem_inc(S["top"], 1)
            dve.wait_ge(S["ti_ps"], 1)
            v.add(nc.vector.tensor_copy(idx, ps[0:CAP, 3, 0:NE]))
            v.add(nc.vector.tensor_copy(gate, ps[0:CAP, 3, NE:2 * NE]))
            v.join()
            v.link(nc.vector.tensor_copy(iu, idx))
            e.done("dve", v)


EXPERTS_SEMS = (
    "turn",
    "ic", "xe_used", "xt_ps", "xt_sb", "xm", "xa", "g_sb", "ye_sb", "sc_ev", "sp_ps", "he", "hs", "h_ps", "w_used",
    "ld_e0", "ld_e1", "ld_e2", "ld_e3", "ld_f0", "ld_f1", "ld_f2", "ld_f3",
)


def phase_experts(e):
    nc, d, l, S, ps = e.nc, e.d, e.l, e.S, e.ps
    mem = expert_memory(e)
    w, yacc, xe, xT, hs, hT, ye, Gm, idx, gate, iu, ic, iota = (mem[k] for k in (
        "w", "yacc", "xe", "xT", "hs", "hT", "ye", "Gm", "idx", "gate", "iu", "ic", "iota"))
    w13 = w[:, 0:8, :].rearrange("p s (k n) -> p s k n", k=KD)
    w2 = w[:, 8:12, :].rearrange("p s (k n) -> p s k n", k=2)
    NI = NE // 2
    v0, p0 = e.count["dve"], e.count["pool"]
    groups = ((0, CAPS, 1), (CAPS, CAP, 0))

    with nc.Block() as block:
        @block.sync
        def _(sp):
            e.clear_last(sp)
            def load(x, j, second):
                if not second:
                    for a, name in enumerate(("ex_w1", "ex_w3")):
                        sp.dma_start(w13[:, 4 * a + j], d[name][l, x].rearrange("(k p) n -> p k n", p=P)[:, :, j * 256:(j + 1) * 256]
                                     ).then_inc(S[f"ld_e{j}"], 16)
                else:
                    sp.dma_start(w2[:, j], d["ex_w2"][l, x, j * 256:(j + 1) * 256].rearrange("(k p) n -> p k n", p=P)
                                 ).then_inc(S[f"ld_f{j}"], 16)

            for second in range(2):
                for j in range(4):
                    load(0, j, second)
            with sp.Fori(1, NE) as x:
                for second in range(2):
                    for j in range(4):
                        if second:
                            sp.wait_ge(S["w_used"], x * 4 + (j + 1 - 4))
                        else:
                            sp.wait_ge(S["h_ps"], x * 8 + (2 * j + 2 - 8))
                        load(x, j, second)

        @block.gpsimd
        def _(pool):
            with pool.Fori(0, NI) as i:
                for b in range(2):
                    pool.wait_ge(S["xe_used"], i * 2 + (b + 1))
                    pool.sem_inc(S["turn"], 1)
                    nc.gpsimd.tensor_copy(ic[:, b:b + 1], iu[:, bass.ds(i * 2 + b, 1)]).then_inc(S["ic"], 1)
                    pool.wait_ge(S["ic"], i * 2 + (b + 1))
                    pool.sem_inc(S["turn"], 1)
                    nc.gpsimd.indirect_dma_start(xe[:, b, :], None, e.h2_d, bass.IndirectOffsetOnAxis(ap=ic[:, b:b + 1], axis=0)
                                                 ).then_inc(S[f"ld_x{b}"], 16)

        @block.tensor
        def _(pe):
            def scatter(n, b):
                pe.wait_ge(S["ye_sb"], n + 1)
                pe.wait_ge(S["g_sb"], n + 1)
                for t in range(TILES):
                    for h in range(2):
                        k = 2 * t + h
                        pe.wait_ge(S["sc_ev"], n * 10 + (k + 1))
                        m = nc.tensor.matmul(ps[:, 6 + h, :], Gm[:, b, t * P:(t + 1) * P], ye[:, b, h * 512:(h + 1) * 512],
                                             start=True, stop=True)
                        m.then_inc(S["sp_ps"], 1)

            with pe.Fori(0, NI) as i:
                for b in range(2):
                    x = i * 2 + b
                    pe.wait_ge(S[f"ld_x{b}"], l * (16 * NI) + (i * 16 + 16))
                    for k in range(KD):
                        m = nc.tensor.transpose(ps[:, k // 4, (k % 4) * CAP:(k % 4 + 1) * CAP], xe[:, b, k * P:(k + 1) * P],
                                                e.ident[0:CAP, 0:CAP])
                    m.then_inc(S["xt_ps"], 1)
                    for f in range(KD):
                        j = f // 2
                        if f % 2 == 0:
                            pe.wait_ge(S[f"ld_e{j}"], x * 32 + 32)
                        if f == 0:
                            pe.wait_ge(S["xt_sb"], x + 1)
                        pe.wait_ge(S["he"], x * 8 + (f + 1))
                        for a in range(2):
                            for k in range(KD):
                                m = nc.tensor.matmul(ps[:, 2 + f % 2, a * CAP:(a + 1) * CAP], w13[:, 4 * a + j, k, (f % 2) * P:(f % 2 + 1) * P],
                                                     xT[:, k, :], start=k == 0, stop=k == KD - 1)
                        m.then_inc(S["h_ps"], 1)
                    scatter(x, 1 - b)
                    pe.wait_ge(S["he"], x * 8 + 10)
                    for f in range(KD):
                        if f % 2 == 0:
                            pe.wait_ge(S[f"ld_f{f // 2}"], x * 16 + 16)
                        for h in range(2):
                            m = nc.tensor.matmul(ps[0:CAP, 4 + h, :], hT[:, f, :], w2[:, f // 2, f % 2, h * 512:(h + 1) * 512],
                                                 start=f == 0, stop=f == KD - 1)
                        if f % 2:
                            m.then_inc(S["w_used"], 1)
            scatter(NE, 1)

        @block.scalar
        def _(act):
            with act.Fori(0, NI) as i:
                for b in range(2):
                    x = i * 2 + b
                    for f in range(KD):
                        act.wait_ge(S["h_ps"], x * 8 + (f + 1))
                        act.wait_ge(S["he"], x * 8 + (f + 1))
                        nc.scalar.activation(hs[:, f % 2, :], ps[:, 2 + f % 2, 0:CAP], ACT.Silu).then_inc(S["hs"], 1)
                    act.wait_ge(S["w_used"], x * 4 + 4)
                    act.wait_ge(S["sp_ps"], x * 10 + 10)
                    nc.scalar.activation(ye[:, b, :], ps[0:CAP, 4:6, :].rearrange("p a b -> p (a b)"), ACT.Copy).then_inc(S["ye_sb"], 1)

        @block.vector
        def _(dve):
            v = e.chain("dve", dve)
            v.add(nc.vector.memset(yacc, 0.0))
            v.add(nc.vector.memset(ye[:, 1, :], 0.0))
            v.link(nc.vector.memset(Gm[:, 1, :], 0.0))
            for name, n in (("ye_sb", 1), ("g_sb", 1), ("sc_ev", 2), ("he", 2), ("xe_used", 2)):
                dve.sem_inc(S[name], n)

            def add(n):
                for t in range(TILES):
                    for h in range(2):
                        dve.wait_ge(S["sp_ps"], n * 10 + (2 * t + h + 1))
                        nc.vector.tensor_tensor(yacc[:, t, h * 512:(h + 1) * 512], yacc[:, t, h * 512:(h + 1) * 512], ps[:, 6 + h, :],
                                                ALU.add).then_inc(S["sc_ev"], 1)

            with dve.Fori(0, NI) as i:
                for b in range(2):
                    x = i * 2 + b
                    dve.wait_ge(S["xt_ps"], x + 1)
                    for c0, c1, g in groups:
                        for q in range(2):
                            s3 = lambda a: e.modc[:, g, a, 4 * q:4 * q + 4].rearrange("p (n o) -> p n o", o=1).to_broadcast([P, 4, c1 - c0])
                            nc.vector.tensor_tensor(xT[:, 4 * q:4 * q + 4, c0:c1],
                                                    ps[:, q, 0:4 * CAP].rearrange("p (a b) -> p a b", a=4)[:, :, c0:c1],
                                                    s3(4), ALU.mult).then_inc(S["xm"], 1)
                    dve.wait_ge(S["xm"], x * 4 + 4)
                    dve.sem_inc(S["xe_used"], 1)
                    for c0, c1, g in groups:
                        s3 = lambda a: e.modc[:, g, a, :].rearrange("p (n o) -> p n o", o=1).to_broadcast([P, KD, c1 - c0])
                        nc.vector.tensor_tensor(xT[:, :, c0:c1], xT[:, :, c0:c1], s3(3), ALU.add).then_inc(S["xa"], 1)
                    dve.wait_ge(S["xa"], x * 2 + 2)
                    dve.sem_inc(S["xt_sb"], 1)
                    nc.vector.tensor_scalar(Gm[:, b, :], iota, idx[:, bass.ds(x, 1)], gate[:, bass.ds(x, 1)], ALU.is_equal, ALU.mult
                                            ).then_inc(S["g_sb"], 1)
                    for f in range(KD):
                        dve.wait_ge(S["hs"], x * 8 + (f + 1))
                        nc.vector.tensor_tensor(hT[:, f, :], hs[:, f % 2, :], ps[:, 2 + f % 2, CAP:2 * CAP], ALU.mult
                                                ).then_inc(S["he"], 1)
                    add(x)
            add(NE)
            e.done("dve", v)


NORM2_SEMS = (
    "n2ld", "n2ldg", "n2var", "n2sd", "n2nm", "n2xn", "n2x",
)


def phase_norm2(e):
    nc, S = e.nc, e.S
    yacc = expert_memory(e)["yacc"]
    brow, z = e.part(0, 2, DM)
    gb, z = e.part(z, 2, DM)
    y, z = e.part(z, 2, DM)
    st, z = e.part(z, TILES, 16)
    vector, scalar, pool, loads = norm_steps(
        e, "n2", lambda t, n: yacc[:, t, n * 512:(n + 1) * 512], brow, gb, y, st, lambda dve, t: None, None)
    with nc.Block() as block:
        @block.sync
        def _(sp):
            e.clear_last(sp)
            loads(sp, 1)

        @block.vector
        def _(dve):
            v = e.chain("dve", dve)
            vector(dve, v)
            e.done("dve", v)

        @block.scalar
        def _(act):
            scalar(act)

        @block.gpsimd
        def _(pl):
            c = e.chain("pool", pl)
            pool(pl, c)
            e.done("pool", c)


PHASES = [
    (phase_modulation, MODULATION_SEMS), (phase_project, PROJECT_SEMS), (phase_attention, ATTENTION_SEMS),
    (phase_hgrn, HGRN_SEMS), (phase_rwkv, RWKV_SEMS), (phase_output, OUTPUT_SEMS), (phase_route, ROUTE_SEMS),
    (phase_experts, EXPERTS_SEMS), (phase_norm2, NORM2_SEMS),
]


def kernel(**inputs):
    import numpy as _np
    import concourse.bacc as _bacc
    from concourse import mybir as _mybir
    from concourse.bass_utils import run_bass_kernel_spmd as _run

    nc = _bacc.Bacc("TRN2", target_bir_lowering=False, num_devices=1)
    arrays, d, o = {}, {}, {}
    for name, a in layout(inputs).items():
        arrays[f"in_{name}"] = a
        d[name] = nc.dram_tensor(f"in_{name}", a.shape, _mybir.dt.from_np(a.dtype), kind="ExternalInput").ap()
    for name, shape in OUTS:
        o[name] = nc.dram_tensor(f"out_{name}", shape, _mybir.dt.float32, kind="ExternalOutput").ap()
    program(nc, d, o)
    r = _run(nc, [arrays], core_ids=[0])
    return tuple(r.results[0][f"out_{name}"] for name, _ in OUTS)
```

```python
from contextlib import ExitStack

import numpy as np
import concourse.bass as bass
from concourse import mybir

F32 = mybir.dt.float32
U32 = mybir.dt.uint32
ALU = mybir.AluOpType
ACT = mybir.ActivationFunctionType
AX = mybir.AxisListType.X

P = 128
DEPTH, DM, NPR, NSM = 2, 1024, 128, 512
NTOK = NPR + NSM
TILES = NTOK // P
KD = DM // P
PAST = 256
GRID_W = 64
NH, NOPE, ROPE, DV = 8, 64, 32, 64
QK = NOPE + ROPE
QR, KVR = 384, 256
MLA_COLS = QR + KVR + ROPE
HH, HD = 4, 64
HG0 = MLA_COLS
RW0 = HG0 + 5 * HH * HD
NRW = 9
NE, FF = 16, 1024
CAPS, CAPP = 2 * NSM // NE, 2 * NPR // NE
CAP = CAPS + CAPP
WIDE = 96
ORDER = (((0, CAPS, 0, 1), (CAPS, CAP, CAPS, 0)), ((0, CAPS, WIDE - CAPS, 1), (CAPS, CAP, 0, 0)))
C = 64
NCH = NTOK // C
LV = 7
ALPHA = float((2 * DEPTH) ** 0.25)
SCALE = float(QK) ** -0.5
PAD = NTOK + 3
TOKC = MLA_COLS + 2 * HH * HD
HGT = 6
WRING = 6


def pad_at(n):
    return n + 1 + (n >= NPR)


def constants():
    i = np.arange(P)
    s, t = i[:, None], i[None, :]
    m = np.zeros((2, LV + 1, P, P), np.float32)
    m[:, 0] = np.eye(P)
    for j in range(LV):
        h = 1 << j
        same = s // (2 * h) == t // (2 * h)
        m[0, j + 1] = same & (s % (2 * h) < h) & (t % (2 * h) >= h)
        m[1, j + 1] = m[0, j + 1].T
    hgm = m.transpose(2, 0, 1, 3).reshape(P, 2 * (LV + 1) * P)
    rwm = np.zeros((P, 2, P), np.float32)
    a, b = np.arange(C)[:, None], np.arange(C)[None, :]
    for d in range(2):
        strict, incl = ((a < b), (a <= b)) if d == 0 else ((a > b), (a >= b))
        for r in range(2):
            rwm[r * C:(r + 1) * C, d, :C] = strict
            rwm[r * C:(r + 1) * C, d, C:] = incl
    bds = m[:, 1:7].sum(1).transpose(2, 0, 1)
    blk = (s // C == t // C).astype(np.float32)
    quarter = ROPE // 4
    pos = np.stack([np.arange(NSM) // GRID_W, np.arange(NSM) % GRID_W], -1).astype(np.float32)
    inv = (np.float32(10000.0) ** (-np.arange(quarter, dtype=np.float32) / np.float32(quarter))).astype(np.float32)
    ang = pos[:, :, None] * inv
    rope = np.zeros((QK, 2, NSM), np.float32)
    rope[:NOPE, 0] = 1.0
    rot = np.zeros((QK, ROPE), np.float32)
    for ax in range(2):
        for half in range(2):
            for q in range(quarter):
                c = ax * 2 * quarter + half * quarter + q
                rope[NOPE + c, 0] = np.cos(ang[:, ax, q])
                rope[NOPE + c, 1] = np.sin(ang[:, ax, q])
                o = ax * 2 * quarter + (1 - half) * quarter + q
                rot[NOPE + o, c] = 1.0 if half else -1.0
    reset = np.ones((P, 2, NTOK), np.float32)
    reset[:, 0, 0::C] = 0
    reset[:, 1, C - 1::C] = 0
    iota = np.broadcast_to(np.arange(NTOK, dtype=np.float32), (P, NTOK))
    base = np.broadcast_to(np.where(np.arange(CAP) < CAPS, NPR, 0).astype(np.float32), (NE, CAP))
    return {
        "ident": np.eye(P, dtype=np.float32), "hgm": hgm, "rwm": rwm.reshape(P, -1), "bds": bds.reshape(P, -1),
        "blk": blk, "rope": rope.reshape(QK, -1), "rot": rot, "reset": reset.reshape(P, -1), "iota": iota,
        "base": base,
    }


PC = {}
_n = 0
for _name, _w in (("qn", 3), ("mu0", 9), ("mu1", 9), ("w0", 4), ("a0", 4), ("kk", 2), ("ka", 2), ("rk", 2)):
    PC[_name] = _n
    _n += _w
NPC = _n


def layout(i):
    f = lambda n: np.asarray(i[n])
    cols = lambda a: a.reshape(DEPTH, -1, P).transpose(0, 2, 1)
    w = f("w_in").reshape(DEPTH, KD, P, -1)
    tch = [HG0 + P * n for n in (0, 1)] + [HG0 + 2 * HH * HD + P * n for n in range(4)] + [RW0 + P * n for n in range(NRW)]
    w_t = np.stack([w[:, :, :, c:c + P] for c in tch], 1).transpose(0, 1, 3, 2, 4)
    tok = np.concatenate([w[..., :MLA_COLS], w[..., HG0 + 256:HG0 + 512], w[..., HG0 + 1024:HG0 + 1280]], -1)
    ukv = f("mla_w_ukv").reshape(DEPTH, 2, P, NH, 2, NOPE)
    out = {
        "x": np.concatenate([f("x_prompt").reshape(NPR, DM), f("x_sample").reshape(NSM, DM)], 0),
        "cvec": np.stack([f("c_ctx").reshape(KD, P), f("c").reshape(KD, P)], -1).transpose(1, 0, 2),
        "ada_w": f("ada_w"), "ada_b": f("ada_b"),
        "w_t": w_t, "w_tok": tok.transpose(0, 2, 1, 3),
        "w_uq": f("mla_w_uq").reshape(DEPTH, 3, P, NH * QK).transpose(0, 2, 1, 3),
        "w_uk": ukv[..., 0, :].reshape(DEPTH, 2, P, NH * NOPE).transpose(0, 2, 1, 3),
        "w_uv": ukv[..., 1, :].reshape(DEPTH, 2, P, NH * DV).transpose(0, 2, 1, 3),
        "c_ckv": f("cache_ckv").reshape(DEPTH, PAST, KVR), "c_kr": f("cache_krope").reshape(DEPTH, PAST, ROPE),
        "lb": f("hg_lb_logits").reshape(DEPTH * 4, P).T,
        "pcol": np.concatenate([cols(f(n)) for n in
                                ("mla_q_norm",)] + [cols(f("rw_mu")[:, 0]), cols(f("rw_mu")[:, 1])] +
                               [cols(f(n)) for n in ("rw_w0", "rw_a0", "rw_k_k", "rw_k_a", "rw_r_k")], -1),
        "prow": np.concatenate([f(n) for n in ("mla_kv_norm", "hg_norm", "rw_gn_w", "rw_gn_b")], -1),
        "w_wa": np.stack([f("rw_w2"), f("rw_a2")], 1).reshape(DEPTH, 2, P, HH * HD).transpose(0, 2, 1, 3),
        "w_g2": f("rw_g2"),
        "s_hg": f("state_hgrn").reshape(DEPTH, 2, 2, P, HD),
        "s_rw": f("state_rwkv").reshape(DEPTH, 2, HH, HD, HD).transpose(0, 1, 2, 4, 3).reshape(DEPTH, 2, 2, P, HD),
        "w_out": f("w_out"), "ln_g": f("ln_g"), "ln_b": f("ln_b"),
        "router": f("router").reshape(DEPTH, KD, P, NE).transpose(0, 2, 1, 3),
        "ex_w1": f("ex_w1"), "ex_w3": f("ex_w3"), "ex_w2": f("ex_w2"),
    }
    out.update(constants())
    return {k: np.ascontiguousarray(v) for k, v in out.items()}


OUTS = [("y_p", (1, NPR, DM)), ("y_s", (1, NSM, DM)), ("n_ckv", (1, DEPTH, NPR, KVR)), ("n_kr", (1, DEPTH, NPR, ROPE)),
        ("n_hg", (1, DEPTH, 2, HH, HD, HD)), ("n_rw", (1, DEPTH, 2, HH, HD, HD))]


class Shared:
    pass


class Chain:

    def __init__(self, eng, sem, at=0):
        self.eng, self.sem, self.n = eng, sem, at

    def add(self, ins):
        self.n += 1
        ins.then_inc(self.sem, 1)
        return self.n

    def join(self):
        self.eng.wait_ge(self.sem, self.n)

    def link(self, ins):
        self.add(ins)
        self.join()


def program(nc, d, o, taps=(), depth=DEPTH, stop=99):
    ctx = ExitStack()
    used = []
    with ctx:
        def sb(name, shape, dt=F32):
            return ctx.enter_context(nc.sbuf_tensor(name, shape, dt))

        def sem(name):
            s = ctx.enter_context(nc.semaphore(name))
            used.append(s)
            return s

        x = sb("x_sb", [P, TILES, DM])
        ident = sb("ident_sb", [P, P])
        hgm = sb("hgm_sb", [P, 2, (LV + 1) * P])
        rwm = sb("rwm_sb", [P, 2, P])
        bds = sb("bds_sb", [P, 2, P])
        blk = sb("blk_sb", [P, P])
        rope = sb("rope_sb", [QK, 2, NSM])
        rot = sb("rot_sb", [QK, ROPE])
        reset = sb("reset_sb", [P, 2, NTOK])
        scT = sb("scT", [P, KD, 2])
        lball = sb("lball", [P, DEPTH, 4])
        lb = sb("lb_sb", [P, 4])
        oml = sb("oml", [P, 4])
        modc = sb("modc", [P, 2, 6, KD])
        pcol = sb("pcol_sb", [P, NPC])
        prow = sb("prow_sb", [P, 4, 256])
        eps = sb("eps_sb", [P, 3])
        arena = sb("arena", [P, 40600])
        ps = ctx.enter_context(nc.psum_tensor("ps", [P, 8, 512], F32))
        mod_d = nc.dram_tensor("mod_d", (2, 6, KD, P), F32, kind="Internal").ap()
        h2_d = nc.dram_tensor("h2_d", (NTOK, DM), F32, kind="Internal").ap()

        def part(at, *shape, rows=P, dt=F32):
            n = int(np.prod(shape))
            v = arena[0:rows, at:at + n]
            if dt != F32:
                v = v.bitcast(dt)
            if len(shape) > 1:
                names = "abcdef"[:len(shape)]
                v = v.rearrange(f"p ({' '.join(names)}) -> p {' '.join(names)}", **dict(zip(names, shape)))
            return v, at + n

        hT, a0 = part(0, KD, NTOK)
        mixT = hT
        hgT, a1 = part(a0, HGT, NTOK)
        rwT, a2 = part(a1, NRW, PAD)
        tok, FREE = part(a2, TILES, TOKC)

        chains = {k: sem(k + "_chain") for k in ("dve", "act", "pool", "pe")}
        count = dict.fromkeys(chains, 0)

        def chain(kind, eng):
            c = Chain(eng, chains[kind], count[kind])
            return c

        def done(kind, c):
            count[kind] = c.n

        S = {n: sem(n) for n in ("ld_const", "tap", "st_y")}
        S.update({n: ctx.enter_context(nc.semaphore(n)) for n in ("ld_x0", "ld_x1")})

        with nc.Block() as block:
            cv, z = part(0, KD, 2)
            lg, z = part(z, DEPTH, 4)
            tmp, z = part(z, 8, 4)

            @block.sync
            def _(sp):
                for dst, src in ((ident, "ident"), (blk, "blk"), (rot, "rot")):
                    sp.dma_start(dst[:, :], d[src]).then_inc(S["ld_const"], 16)
                sp.dma_start(hgm[:, :, :].rearrange("p a b -> p (a b)"), d["hgm"]).then_inc(S["ld_const"], 16)
                sp.dma_start(rwm[:, :, :].rearrange("p a b -> p (a b)"), d["rwm"]).then_inc(S["ld_const"], 16)
                sp.dma_start(bds[:, :, :].rearrange("p a b -> p (a b)"), d["bds"]).then_inc(S["ld_const"], 16)
                sp.dma_start(rope[:, :, :].rearrange("p a b -> p (a b)"), d["rope"]).then_inc(S["ld_const"], 16)
                sp.dma_start(reset[:, :, :].rearrange("p a b -> p (a b)"), d["reset"]).then_inc(S["ld_const"], 16)
                sp.dma_start(cv, d["cvec"]).then_inc(S["ld_const"], 16)
                sp.dma_start(lg.rearrange("p a b -> p (a b)"), d["lb"]).then_inc(S["ld_const"], 16)
                sp.dma_start(x[:, :, :], d["x"].rearrange("(t p) n -> p t n", p=P)).then_inc(S["ld_const"], 16)
                sp.wait_ge(S["ld_const"], 16 * 11)

            @block.scalar
            def _(act):
                a = chain("act", act)
                act.wait_ge(S["ld_const"], 176)
                a.add(nc.scalar.activation(scT[:, :, :], cv, ACT.Silu))
                act.wait_ge(chains["dve"], 2)
                a.link(nc.scalar.activation(tmp[:, 1:1 + DEPTH, :], tmp[:, 4:4 + DEPTH, :], ACT.Exp))
                done("act", a)

            @block.vector
            def _(dve):
                v = chain("dve", dve)
                dve.wait_ge(S["ld_const"], 176)
                v.link(nc.vector.tensor_tensor(tmp[:, 0, :], lg[:, 0, :], lg[:, 1, :], ALU.max))
                v.link(nc.vector.tensor_tensor(tmp[:, 4:4 + DEPTH, :], lg, tmp[:, 0:1, :].to_broadcast([P, DEPTH, 4]),
                                               ALU.subtract))
                dve.wait_ge(chains["act"], 2)
                v.link(nc.vector.tensor_tensor(tmp[:, 3, :], tmp[:, 1, :], tmp[:, 2, :], ALU.add))
                v.link(nc.vector.reciprocal(tmp[:, 3, :], tmp[:, 3, :]))
                v.link(nc.vector.tensor_tensor(tmp[:, 1:1 + DEPTH, :], tmp[:, 1:1 + DEPTH, :],
                                               tmp[:, 3:4, :].to_broadcast([P, DEPTH, 4]), ALU.mult))
                v.link(nc.vector.tensor_tensor(tmp[:, 6, :], tmp[:, 1, :], tmp[:, 1, :], ALU.subtract))
                v.link(nc.vector.tensor_scalar(lball[:, 0, :], tmp[:, 6, :], 0.0, None, ALU.max))
                v.link(nc.vector.tensor_tensor(tmp[:, 7, :], tmp[:, 1, :], tmp[:, 2, :], ALU.add))
                v.link(nc.vector.tensor_tensor(tmp[:, 7, :], tmp[:, 7, :], tmp[:, 1, :], ALU.subtract))
                v.link(nc.vector.tensor_scalar(lball[:, 1, :], tmp[:, 7, :], 0.0, None, ALU.max))
                v.add(nc.vector.memset(eps[:, 0:1], 1e-6))
                v.add(nc.vector.memset(eps[:, 1:2], 1e-5))
                v.link(nc.vector.memset(eps[:, 2:3], 64e-5))
                done("dve", v)

        def clear_all():
            nc.all_engine_barrier()
            with nc.Block() as block:
                @block.sync
                def _(sp):
                    for s in used:
                        sp.sem_clear(s)
            nc.all_engine_barrier()
            for k in count:
                count[k] = 0

        e = Shared()
        e.nc, e.d, e.o, e.x, e.ident, e.hgm = nc, d, o, x, ident, hgm
        e.rwm, e.bds, e.blk, e.rope, e.rot, e.reset = rwm, bds, blk, rope, rot, reset
        e.scT, e.lball, e.lb, e.oml, e.modc, e.pcol = scT, lball, lb, oml, modc, pcol
        e.prow, e.eps, e.ps, e.mod_d, e.h2_d, e.part = prow, eps, ps, mod_d, h2_d, part
        e.hT, e.mixT, e.hgT, e.rwT, e.tok, e.a0 = hT, mixT, hgT, rwT, tok, a0
        e.a1, e.a2, e.FREE, e.chains, e.count, e.chain = a1, a2, FREE, chains, count, chain
        e.done = done
        clear_all()
        with nc.Fori(0, depth) as l:
            e.l = l
            last = []

            def clear_last(sp):
                for s in last:
                    sp.sem_clear(s)

            e.clear_last = clear_last
            for n, (f, names) in enumerate(PHASES):
                if n >= stop:
                    break
                own = {name: nc.alloc_semaphore(name=f"{name}") for name in names}
                e.S = {**S, **own}
                f(e)
                for s in last:
                    nc.release_semaphore(s)
                last[:] = own.values()
            if taps:
                with nc.Block() as block:
                    @block.sync
                    def _(sp):
                        for k, (name, f) in enumerate(taps):
                            sp.dma_start(o[name][l], f(e)).then_inc(S["tap"], 16)
                        sp.wait_ge(S["tap"], 16 * len(taps))
            used.extend(last)
            clear_all()
        with nc.Block() as block:
            @block.sync
            def _(sp):
                sp.dma_start(o["y_p"][0], x[:, 0, :]).then_inc(S["st_y"], 16)
                sp.dma_start(o["y_s"][0].rearrange("(t p) n -> p t n", p=P), x[:, 1:TILES, :]).then_inc(S["st_y"], 16)
                sp.wait_ge(S["st_y"], 32)


MODULATION_SEMS = (
    "ld_adab",
    "mod_out", "mod_in", "ada_ps", "ada_row", "modt", "ld_par", "ld_ada0", "ld_ada1", "ld_ada2", "ld_ada3",
)


def phase_modulation(e):
    nc, d, l, S = e.nc, e.d, e.l, e.S
    NB = 6 * DM // 512
    RING = 4
    slot, z = e.part(0, RING, KD, 512)
    brow, z = e.part(z, 6 * DM, rows=2)
    mrow, z = e.part(z, 6 * DM, rows=2)
    mt, z = e.part(z, P, rows=96)
    ps = e.ps
    with nc.Block() as block:
        @block.sync
        def _(sp):
            e.clear_last(sp)
            sp.dma_start(brow, d["ada_b"][l].rearrange("(o n) -> o n", o=1).to_broadcast([2, 6 * DM])).then_inc(S["ld_adab"], 16)
            for n in range(NB):
                if n >= RING:
                    sp.wait_ge(S["ada_ps"], n - RING + 1)
                sp.dma_start(slot[:, n % RING], d["ada_w"][l].rearrange("(k p) n -> p k n", p=P)[:, :, n * 512:(n + 1) * 512]
                             ).then_inc(S[f"ld_ada{n % RING}"], 16)
            sp.dma_start(e.pcol[:, :], d["pcol"][l]).then_inc(S["ld_par"], 16)
            sp.dma_start(e.prow[:, :, :].rearrange("p a b -> p (a b)"),
                         d["prow"][l].rearrange("(o n) -> o n", o=1).to_broadcast([P, 1024])).then_inc(S["ld_par"], 16)
            sp.wait_ge(S["ada_row"], NB)
            sp.dma_start(e.mod_d.rearrange("g s k p -> g (s k p)"), mrow).then_inc(S["mod_out"], 16)
            sp.wait_ge(S["mod_out"], 16)
            sp.dma_start(mt, e.mod_d.rearrange("g s k p -> (g s k) p")).then_inc(S["mod_in"], 16)
            sp.wait_ge(S["ld_par"], 32)

        @block.tensor
        def _(pe):
            for n in range(NB):
                pe.wait_ge(S[f"ld_ada{n % RING}"], 16 * (n // RING + 1))
                if n >= 8:
                    pe.wait_ge(S["ada_row"], n - 7)
                for k in range(KD):
                    i = nc.tensor.matmul(ps[0:2, n % 8, :], e.scT[:, k, :], slot[:, n % RING, k, :],
                                         start=k == 0, stop=k == KD - 1)
                i.then_inc(S["ada_ps"], 1)
            pe.wait_ge(S["mod_in"], 16)
            pe.wait_ge(S["ada_row"], NB)
            nc.tensor.transpose(ps[:, 0, 0:96], mt, e.ident[0:96, 0:96]).then_inc(S["modt"], 1)

        @block.vector
        def _(dve):
            v = e.chain("dve", dve)
            dve.wait_ge(S["ld_adab"], 16)
            for n in range(NB):
                dve.wait_ge(S["ada_ps"], n + 1)
                nc.vector.tensor_tensor(mrow[:, n * 512:(n + 1) * 512], ps[0:2, n % 8, :], brow[:, n * 512:(n + 1) * 512],
                                        ALU.add).then_inc(S["ada_row"], 1)
            dve.wait_ge(S["modt"], 1)
            v.link(nc.vector.tensor_copy(e.modc[:, :, :, :].rearrange("p g s k -> p (g s k)"), ps[:, 0, 0:96]))
            for s in (1, 4):
                v.add(nc.vector.tensor_scalar(e.modc[:, :, s, :], e.modc[:, :, s, :], 1.0, None, ALU.add))
            v.link(nc.vector.tensor_copy(e.lb[:, :], e.lball[:, bass.ds(l, 1), :].rearrange("p a b -> p (a b)")))
            v.link(nc.vector.tensor_scalar(e.oml[:, :], e.lb[:, :], -1.0, 1.0, ALU.mult, ALU.add))
            e.done("dve", v)


PROJECT_SEMS = (
    "ld_tokw", "pj_ps", "pj_act", "pj_dve", "ld_wt0", "ld_wt1", "ld_wt2", "ld_wt3", "ld_wt4", "ld_wt5",
)


def phase_project(e):
    nc, d, l, S, ps = e.nc, e.d, e.l, e.S, e.ps
    tokw, z = e.part(e.FREE, KD, TOKC)
    ring, z = e.part(z, WRING, KD, P)
    NT = HGT + NRW
    spans = ((0, 512), (512, MLA_COLS), (MLA_COLS, TOKC))
    groups = [("x", t, h) for t in range(TILES) for h in range(2)]
    NX = len(groups)
    groups += [("T", c, g) for c in range(NT) for g in (1, 0)]
    groups += [("tok", t, s) for t in range(TILES) for s in range(3)]

    with nc.Block() as block:
        @block.sync
        def _(sp):
            e.clear_last(sp)
            for c in range(NT):
                if c >= WRING:
                    sp.wait_ge(S["pj_ps"], NX + 2 * (c - WRING + 1))
                sp.dma_start(ring[:, c % WRING], d["w_t"][l, c]).then_inc(S[f"ld_wt{c % WRING}"], 16)
                if c == WRING - 1:
                    sp.dma_start(tokw, d["w_tok"][l]).then_inc(S["ld_tokw"], 16)

        @block.tensor
        def _(pe):
            for n, (kind, a, b) in enumerate(groups):
                if n >= 8:
                    pe.wait_ge(S["pj_dve" if n % 2 else "pj_act"], (n - 8) // 2 + 1)
                if n == NX:
                    pe.wait_ge(S["pj_act"], NX // 2)
                    pe.wait_ge(S["pj_dve"], NX // 2)
                if kind == "x":
                    for k in range(4):
                        kk = 4 * b + k
                        i = nc.tensor.transpose(ps[:, n % 8, k * P:(k + 1) * P], e.x[:, a, kk * P:(kk + 1) * P], e.ident[:, :])
                elif kind == "T":
                    pe.wait_ge(S[f"ld_wt{a % WRING}"], 16 * (a // WRING + 1))
                    c0, c1 = (NPR, NTOK) if b else (0, NPR)
                    for k in range(KD):
                        i = nc.tensor.matmul(ps[:, n % 8, 0:c1 - c0], ring[:, a % WRING, k, :], e.hT[:, k, c0:c1],
                                             start=k == 0, stop=k == KD - 1)
                else:
                    pe.wait_ge(S["ld_tokw"], 16)
                    c0, c1 = spans[b]
                    for k in range(KD):
                        i = nc.tensor.matmul(ps[:, n % 8, 0:c1 - c0], e.hT[:, k, a * P:(a + 1) * P], tokw[:, k, c0:c1],
                                             start=k == 0, stop=k == KD - 1)
                i.then_inc(S["pj_ps"], 1)

        def place(n):
            kind, a, b = groups[n]
            if kind == "T":
                c0, c1 = (NPR, NTOK) if b else (0, NPR)
                dst = e.hgT[:, a, c0:c1] if a < HGT else e.rwT[:, a - HGT, pad_at(c0):pad_at(c0) + c1 - c0]
            else:
                c0, c1 = spans[b]
                dst = e.tok[:, a, c0:c1]
            return dst, ps[:, n % 8, 0:c1 - c0]

        @block.scalar
        def _(act):
            for n in range(0, len(groups), 2):
                act.wait_ge(S["pj_ps"], n + 1)
                kind, a, b = groups[n]
                if kind == "x":
                    g = 1 if a else 0
                    for k in range(4):
                        kk = 4 * b + k
                        i = nc.scalar.activation(e.hT[:, kk, a * P:(a + 1) * P], ps[:, n % 8, k * P:(k + 1) * P], ACT.Identity,
                                                 bias=e.modc[:, g, 0, kk:kk + 1], scale=e.modc[:, g, 1, kk:kk + 1])
                else:
                    dst, src = place(n)
                    i = nc.scalar.activation(dst, src, ACT.Copy)
                i.then_inc(S["pj_act"], 1)

        @block.vector
        def _(dve):
            v = e.chain("dve", dve)
            for col in (0, pad_at(NPR) - 1, PAD - 1):
                v.add(nc.vector.memset(e.rwT[:, :, col:col + 1], 0.0))
            for n in range(1, len(groups), 2):
                dve.wait_ge(S["pj_ps"], n + 1)
                kind, a, b = groups[n]
                if kind == "x":
                    g = 1 if a else 0
                    for k in range(4):
                        kk = 4 * b + k
                        i = nc.vector.tensor_scalar(e.hT[:, kk, a * P:(a + 1) * P], ps[:, n % 8, k * P:(k + 1) * P],
                                                    e.modc[:, g, 1, kk:kk + 1], e.modc[:, g, 0, kk:kk + 1], ALU.mult, ALU.add)
                else:
                    dst, src = place(n)
                    i = nc.vector.tensor_copy(dst, src)
                i.then_inc(S["pj_dve"], 1)
            e.done("dve", v)


ATTENTION_SEMS = (
    "st_cache", "ld_mla", "q_norm", "kv_norm", "rms", "tq_ps", "tq_ev", "tk_ps", "tk_ev", "v_ps", "v_ev", "krot_ps",
    "k_rope0", "k_rope", "qk_ps", "qk_free", "sc_ps", "sc_neg", "sc_exp", "pt_ps", "pt_sb", "pv_ps", "pv_o", "mo_ps",
    "mo_ev",
)


def phase_attention(e):
    nc, d, o, l, S, ps, tok = e.nc, e.d, e.o, e.l, e.S, e.ps, e.tok
    NKEY = NTOK + PAST
    KT = NKEY // P
    uq, z = e.part(e.FREE, 3, NH * QK)
    uk, z = e.part(z, 2, NH * NOPE)
    uv, z = e.part(z, 2, NH * DV)
    cqT, z = e.part(z, 3, NTOK)
    ckvT, z = e.part(z, 2, NKEY)
    V, z = e.part(z, KT, NH * DV)
    cache, z = e.part(z, 2, KVR + ROPE)
    QT, z = e.part(z, 2, NTOK, rows=QK)
    Kh, z = e.part(z, 2, NKEY, rows=QK)
    pr, z = e.part(z, 2, PAST + NSM)
    pT, z = e.part(z, 2, PAST + NSM)
    st, z = e.part(z, 2 * TILES)
    negm, z = e.part(z, NH * TILES)
    rsum, z = e.part(z, NH * TILES)
    rinv, z = e.part(z, NH * TILES)
    assert z <= 40600
    rt = pT[NOPE:QK].rearrange("p a b -> p (a b)")
    units = [(h, t) for h in range(NH) for t in range(TILES)]
    U = len(units)
    r1, z = e.part(z, NSM)
    assert z <= 40600, z
    r1 = r1[NOPE:QK]
    proj = ("q_grid", "rot", "q_ctx", "k_grid", "k_rest")

    with nc.Block() as block:
        @block.sync
        def _(sp):
            e.clear_last(sp)
            for dst, src in ((uq, d["w_uq"][l]), (uk, d["w_uk"][l]), (uv, d["w_uv"][l]),
                             (cache[:, :, 0:KVR], d["c_ckv"][l].rearrange("(t p) n -> p t n", p=P)),
                             (cache[:, :, KVR:], d["c_kr"][l].rearrange("(t p) n -> p t n", p=P))):
                sp.dma_start(dst, src).then_inc(S["ld_mla"], 16)
            sp.wait_ge(S["kv_norm"], 1)
            sp.dma_start(o["n_ckv"][0, l], tok[:, 0, QR:QR + KVR]).then_inc(S["st_cache"], 16)
            sp.dma_start(o["n_kr"][0, l], tok[:, 0, QR + KVR:MLA_COLS]).then_inc(S["st_cache"], 16)
            sp.wait_ge(S["st_cache"], 32)

        def head_product(pe, h, g):
            n = 5 * h + g
            if n:
                pe.wait_ge(S["qk_free"], n)
            if h >= 2 and g == 0:
                pe.wait_ge(S["sc_ps"], TILES * (h - 1))
            b = h % 2
            kind = proj[g]
            if kind in ("q_grid", "q_ctx"):
                c0, c1 = (NPR, NTOK) if kind == "q_grid" else (0, NPR)
                for k in range(3):
                    i = nc.tensor.matmul(ps[0:QK, 7, 0:c1 - c0], uq[:, k, h * QK:(h + 1) * QK], cqT[:, k, c0:c1],
                                         start=k == 0, stop=k == 2)
            elif kind == "rot":
                i = nc.tensor.matmul(ps[NOPE:QK, 7, :], e.rot[NOPE:QK, :], QT[NOPE:QK, b, NPR:NTOK], start=True, stop=True)
            else:
                c0, c1 = (NPR + PAST, NKEY) if kind == "k_grid" else (0, NPR + PAST)
                for k in range(2):
                    i = nc.tensor.matmul(ps[0:NOPE, 7, 0:c1 - c0], uk[:, k, h * NOPE:(h + 1) * NOPE], ckvT[:, k, c0:c1],
                                         start=k == 0, stop=k == 1)
            i.then_inc(S["qk_ps"], 1)

        def keys(t):
            return (0, NPR) if t == 0 else (NPR, NKEY)

        @block.tensor
        def _(pe):
            for t in range(TILES):
                pe.wait_ge(S["q_norm"], t + 1)
                if t >= 4:
                    pe.wait_ge(S["tq_ev"], t - 3)
                for k in range(3):
                    i = nc.tensor.transpose(ps[:, 2 * (t % 4), k * P:(k + 1) * P], tok[:, t, k * P:(k + 1) * P], e.ident[:, :])
                i.then_inc(S["tq_ps"], 1)
            pe.wait_ge(S["ld_mla"], 80)
            for t in range(KT):
                if t < TILES:
                    pe.wait_ge(S["kv_norm"], t + 1)
                    src = tok[:, t, QR:MLA_COLS]
                else:
                    src = cache[:, t - TILES, :]
                if t >= 4:
                    pe.wait_ge(S["tk_ev"], t - 3)
                for k in range(2):
                    nc.tensor.transpose(ps[:, 2 * (t % 4) + 1, k * P:(k + 1) * P], src[:, k * P:(k + 1) * P], e.ident[:, :])
                nc.tensor.transpose(ps[0:ROPE, 2 * (t % 4) + 1, 2 * P:3 * P], src[:, KVR:KVR + ROPE],
                                    e.ident[:, :]).then_inc(S["tk_ps"], 1)
            pe.wait_ge(S["tk_ev"], KT)
            pe.wait_ge(S["tq_ev"], TILES)
            for t in range(KT):
                if t >= 4:
                    pe.wait_ge(S["v_ev"], t - 3)
                for k in range(2):
                    i = nc.tensor.matmul(ps[:, t % 4, :], ckvT[:, k, t * P:(t + 1) * P], uv[:, k, :], start=k == 0, stop=k == 1)
                i.then_inc(S["v_ps"], 1)
            nc.tensor.matmul(ps[NOPE:QK, 6, :], e.rot[NOPE:QK, :], Kh[NOPE:QK, 0, NPR + PAST:], start=True, stop=True
                             ).then_inc(S["krot_ps"], 1)
            for g in range(5):
                if g == 1:
                    pe.wait_ge(S["qk_free"], 1)
                head_product(pe, 0, g)

            def scores(i):
                h, t = units[i]
                if t == 0:
                    pe.wait_ge(S["qk_free"], 5 * (h + 1))
                    pe.wait_ge(S["k_rope"], 1)
                if i >= 2:
                    pe.wait_ge(S["sc_exp"], i - 1)
                elif i == 0:
                    pe.wait_ge(S["v_ev"], KT)
                c0, c1 = keys(t)
                m = nc.tensor.matmul(ps[:, 2 * (i % 2), 0:min(512, c1 - c0)], QT[:, h % 2, t * P:(t + 1) * P],
                                     Kh[:, h % 2, c0:min(c0 + 512, c1)], start=True, stop=True)
                if c1 - c0 > 512:
                    m = nc.tensor.matmul(ps[:, 2 * (i % 2) + 1, 0:c1 - c0 - 512], QT[:, h % 2, t * P:(t + 1) * P],
                                         Kh[:, h % 2, c0 + 512:c1], start=True, stop=True)
                m.then_inc(S["sc_ps"], 1)

            def attend(i):
                h, t = units[i]
                c0, c1 = keys(t)
                pe.wait_ge(S["pt_sb"], i + 1)
                if i >= 2:
                    pe.wait_ge(S["pv_o"], i - 1)
                n = (c1 - c0) // P
                for k in range(n):
                    m = nc.tensor.matmul(ps[:, 6, (i % 2) * DV:(i % 2 + 1) * DV], pT[:, i % 2, k * P:(k + 1) * P],
                                         V[:, c0 // P + k, h * DV:(h + 1) * DV], start=k == 0, stop=k == n - 1)
                m.then_inc(S["pv_ps"], 1)

            scores(0)
            for i, (h, t) in enumerate(units):
                if h + 1 < NH:
                    head_product(pe, h + 1, t)
                if i + 1 < U:
                    scores(i + 1)
                if i == 1:
                    pe.wait_ge(S["k_rope"], 1)
                if i:
                    attend(i - 1)
                pe.wait_ge(S["sc_exp"], i + 1)
                if i:
                    pe.wait_ge(S["pt_sb"], i)
                c0, c1 = keys(t)
                for k in range((c1 - c0) // P):
                    m = nc.tensor.transpose(ps[:, 4 + k // 4, (k % 4) * P:(k % 4 + 1) * P], pr[:, i % 2, k * P:(k + 1) * P],
                                            e.ident[:, :])
                m.then_inc(S["pt_ps"], 1)
            attend(U - 1)
            for t in range(TILES):
                pe.wait_ge(S["pv_o"], U)
                pe.wait_ge(S["sc_exp"], U)
                if t >= 4:
                    pe.wait_ge(S["mo_ev"], t - 3)
                for k in range(4):
                    m = nc.tensor.transpose(ps[:, t % 4, k * P:(k + 1) * P], tok[:, t, k * P:(k + 1) * P], e.ident[:, :])
                m.then_inc(S["mo_ps"], 1)

        @block.scalar
        def _(act):
            a = e.chain("act", act)
            for t in range(TILES):
                a.add(nc.scalar.activation(pr[:, 0, 0:QR], tok[:, t, 0:QR], ACT.Square, accum_out=st[:, t:t + 1]))
                a.link(nc.scalar.activation(pr[:, 1, 0:KVR], tok[:, t, QR:QR + KVR], ACT.Square,
                                            accum_out=st[:, TILES + t:TILES + t + 1]))
            a.add(nc.scalar.activation(st[:, 0:TILES], st[:, 0:TILES], ACT.Sqrt, bias=e.eps[:, 0:1], scale=1.0 / QR))
            nc.scalar.activation(st[:, TILES:], st[:, TILES:], ACT.Sqrt, bias=e.eps[:, 0:1], scale=1.0 / KVR).then_inc(S["rms"], 1)
            for t in range(TILES):
                act.wait_ge(S["tq_ps"], t + 1)
                for k in range(3):
                    m = nc.scalar.activation(cqT[:, k, t * P:(t + 1) * P], ps[:, 2 * (t % 4), k * P:(k + 1) * P], ACT.Copy,
                                             scale=e.pcol[:, PC["qn"] + k:PC["qn"] + k + 1])
                m.then_inc(S["tq_ev"], 1)
            for t in range(KT):
                act.wait_ge(S["v_ps"], t + 1)
                nc.scalar.activation(V[:, t, :], ps[:, t % 4, :], ACT.Copy).then_inc(S["v_ev"], 1)

            def head_evacuate(h, g):
                kind, b = proj[g], h % 2
                if kind == "rot":
                    return
                act.wait_ge(S["qk_ps"], 5 * h + g + 1)
                if kind[0] == "q":
                    c0, c1 = (NPR, NTOK) if kind == "q_grid" else (0, NPR)
                    m = nc.scalar.activation(QT[:, b, c0:c1], ps[0:QK, 7, 0:c1 - c0], ACT.Copy)
                else:
                    c0, c1 = (NPR + PAST, NKEY) if kind == "k_grid" else (0, NPR + PAST)
                    m = nc.scalar.activation(Kh[0:NOPE, b, c0:c1], ps[0:NOPE, 7, 0:c1 - c0], ACT.Copy)
                m.then_inc(S["qk_free"], 1)

            def exponent(i):
                h, t = units[i]
                c0, c1 = keys(t)
                act.wait_ge(S["sc_neg"], i + 1)
                if i >= 2:
                    act.wait_ge(S["pt_ps"], i - 1)
                sc = ps[:, 2 * (i % 2):2 * (i % 2) + 2, :].rearrange("p a b -> p (a b)")
                nc.scalar.activation(pr[:, i % 2, 0:c1 - c0], sc[:, 0:c1 - c0], ACT.Exp, bias=negm[:, i:i + 1], scale=SCALE,
                                     accum_out=rsum[:, i:i + 1]).then_inc(S["sc_exp"], 1)

            for g in range(5):
                head_evacuate(0, g)
            exponent(0)
            for i, (h, t) in enumerate(units):
                if h + 1 < NH:
                    head_evacuate(h + 1, t)
                if i + 1 < U:
                    exponent(i + 1)
            for t in range(TILES):
                act.wait_ge(S["mo_ps"], t + 1)
                nc.scalar.activation(e.mixT[:, 0:4, t * P:(t + 1) * P], ps[:, t % 4, :].rearrange("p (k n) -> p k n", k=4),
                                     ACT.Copy).then_inc(S["mo_ev"], 1)
            e.done("act", a)

        @block.gpsimd
        def _(pool):
            pool.wait_ge(S["k_rope0"], 1)
            nc.gpsimd.tensor_copy(Kh[NOPE:QK, 1, :], Kh[NOPE:QK, 0, :]).then_inc(S["k_rope"], 1)

        @block.vector
        def _(dve):
            v = e.chain("dve", dve)
            dve.wait_ge(S["rms"], 1)
            v.link(nc.vector.reciprocal(st[:, :], st[:, :]))
            for t in range(TILES):
                nc.vector.tensor_scalar(tok[:, t, 0:QR], tok[:, t, 0:QR], st[:, t:t + 1], None, ALU.mult).then_inc(S["q_norm"], 1)
            for t in range(TILES):
                nc.vector.scalar_tensor_tensor(tok[:, t, QR:QR + KVR], tok[:, t, QR:QR + KVR], st[:, TILES + t:TILES + t + 1],
                                               e.prow[:, 0, :], ALU.mult, ALU.mult).then_inc(S["kv_norm"], 1)
            for t in range(KT):
                dve.wait_ge(S["tk_ps"], t + 1)
                at = 0 if t == 0 else (NPR + PAST + (t - 1) * P if t < TILES else NPR + (t - TILES) * P)
                v.add(nc.vector.tensor_copy(Kh[NOPE:QK, 0, at:at + P], ps[0:ROPE, 2 * (t % 4) + 1, 2 * P:3 * P]))
                nc.vector.tensor_copy(ckvT[:, :, at:at + P], ps[:, 2 * (t % 4) + 1, 0:2 * P].rearrange("p (k n) -> p k n", k=2)
                                      ).then_inc(S["tk_ev"], 1)
            g0 = NPR + PAST
            v.join()
            v.link(nc.vector.tensor_tensor(rt[:, 0:NSM], Kh[NOPE:QK, 0, g0:], e.rope[NOPE:QK, 0, :], ALU.mult))
            dve.wait_ge(S["krot_ps"], 1)
            v.link(nc.vector.tensor_tensor(r1, ps[NOPE:QK, 6, :], e.rope[NOPE:QK, 1, :], ALU.mult))
            nc.vector.tensor_tensor(Kh[NOPE:QK, 0, g0:], rt[:, 0:NSM], r1, ALU.add).then_inc(S["k_rope0"], 1)

            def rotate(h):
                b = h % 2
                dve.wait_ge(S["k_rope0"], 1)
                if h:
                    dve.wait_ge(S["qk_free"], 5 * h - 3)
                dve.wait_ge(S["qk_ps"], 5 * h + 2)
                v.link(nc.vector.tensor_tensor(r1, ps[NOPE:QK, 7, :], e.rope[NOPE:QK, 1, :], ALU.mult))
                v.link(nc.vector.tensor_tensor(QT[NOPE:QK, b, NPR:NTOK], QT[NOPE:QK, b, NPR:NTOK], e.rope[NOPE:QK, 0, :], ALU.mult))
                nc.vector.tensor_tensor(QT[NOPE:QK, b, NPR:NTOK], QT[NOPE:QK, b, NPR:NTOK], r1, ALU.add).then_inc(S["qk_free"], 1)

            def row_max(i):
                c0, c1 = keys(units[i][1])
                dve.wait_ge(S["sc_ps"], i + 1)
                sc = ps[:, 2 * (i % 2):2 * (i % 2) + 2, :].rearrange("p a b -> p (a b)")
                v.link(nc.vector.reduce_max(negm[:, i:i + 1], sc[:, 0:c1 - c0], AX))
                nc.vector.tensor_scalar(negm[:, i:i + 1], negm[:, i:i + 1], -SCALE, None, ALU.mult).then_inc(S["sc_neg"], 1)

            def output(i):
                h, t = units[i]
                dve.wait_ge(S["sc_exp"], i + 1)
                v.link(nc.vector.reciprocal(rinv[:, i:i + 1], rsum[:, i:i + 1]))
                dve.wait_ge(S["pv_ps"], i + 1)
                nc.vector.tensor_scalar(tok[:, t, h * DV:(h + 1) * DV], ps[:, 6, (i % 2) * DV:(i % 2 + 1) * DV],
                                        rinv[:, i:i + 1], None, ALU.mult).then_inc(S["pv_o"], 1)

            rotate(0)
            row_max(0)
            dve.wait_ge(S["st_cache"], 32)
            for i, (h, t) in enumerate(units):
                if t == 1 and h + 1 < NH:
                    rotate(h + 1)
                if i + 1 < U:
                    row_max(i + 1)
                if i:
                    output(i - 1)
                c0, c1 = keys(t)
                dve.wait_ge(S["pt_ps"], i + 1)
                if i >= 2:
                    dve.wait_ge(S["pv_ps"], i - 1)
                src = ps[:, 4:6, :].rearrange("p a b -> p (a b)")
                nc.vector.tensor_copy(pT[:, i % 2, 0:c1 - c0], src[:, 0:c1 - c0]).then_inc(S["pt_sb"], 1)
            output(U - 1)
            e.done("dve", v)


HGRN_SEMS = (
    "st_state", "ld_hg", "hg_q", "hg_z", "hg_e", "hg_prep", "lv0", "lv1", "at_ps", "at_sb", "oh_ps", "ou_sb",
    "kr_ps", "kr_sb", "kv_ps", "st_new", "hg_state", "hg_o", "hg_sq", "hg_ss", "hg_rt", "hg_on", "ho_ps", "ho_ev",
)


def phase_hgrn(e):
    nc, d, o, l, S, ps, tok = e.nc, e.d, e.o, e.l, e.S, e.ps, e.tok
    q = e.hgT[:, 0:2, :]
    f = e.hgT[:, 2:6, :]
    vcol, gcol = MLA_COLS, MLA_COLS + HH * HD
    kT, z = e.part(e.FREE, 4, NTOK)
    QL, KL, Pb, Rb, KRt, Sst = [], [], [], [], [], []
    for _ in range(2):
        v, z = e.part(z, LV + 1, 2, P); QL.append(v)
        v, z = e.part(z, LV, 2, P); KL.append(v)
        v, z = e.part(z, 2, P); Pb.append(v)
        v, z = e.part(z, 2, P); Rb.append(v)
        v, z = e.part(z, 2, P); KRt.append(v)
        v, z = e.part(z, 2, 2, HD); Sst.append(v)
    Sfin, z = e.part(z, 2, 2, HD)
    Ft, z = e.part(z, 2 * TILES, 2)
    am, z = e.part(z, 2, (LV + 1) * P)
    oS, z = e.part(z, TILES, HH * HD)
    ssq, z = e.part(z, TILES * HH)
    assert z <= 40600, z
    units = [(0, 0), (0, 1), (1, 0), (4, 1), (2, 0), (3, 1), (3, 0), (2, 1), (4, 0), (1, 1)]
    U = len(units)
    last = ((4, 0), (1, 1))

    def levels(eng, c, u):
        t, dr = units[u]
        cols = slice(t * P, (t + 1) * P)
        Pd, Rd = Pb[dr], Rb[dr]
        c.add(eng.tensor_copy(Pd, f[:, 2 * dr:2 * dr + 2, cols]))
        c.link(eng.memset(Rd, 1.0))
        near, far = (0, 1) if dr == 0 else (1, 0)
        yield
        for j in range(LV + 1):
            h = 1 << j
            i = c.add(eng.tensor_tensor(QL[dr][:, j], q[:, :, cols], Pd, ALU.mult))
            yield
            if j:
                c.add(eng.tensor_tensor(KL[dr][:, j - 1], kT[:, 2 * dr:2 * dr + 2, cols], Rd, ALU.mult))
                yield
            c.join()
            if j == LV:
                end = P - 1 if dr == 0 else 0
                c.link(eng.tensor_copy(Ft[:, u, :], Pd[:, :, end:end + 1].rearrange("p a b -> p (a b)")))
                break
            Pv = Pd.rearrange("p a (n s h) -> p a n s h", s=2, h=h)
            Rv = Rd.rearrange("p a (n s h) -> p a n s h", s=2, h=h)
            n = P // (2 * h)
            edge = h - 1 if dr == 0 else 0
            c.link(eng.tensor_tensor(Rv[:, :, :, near, :], Rv[:, :, :, near, :],
                                     Pv[:, :, :, far, edge:edge + 1].to_broadcast([P, 2, n, h]), ALU.mult))
            yield
            c.link(eng.tensor_tensor(Pv[:, :, :, far, :], Pv[:, :, :, far, :],
                                     Pv[:, :, :, near, edge:edge + 1].to_broadcast([P, 2, n, h]), ALU.mult))
            yield

    with nc.Block() as block:
        @block.sync
        def _(sp):
            e.clear_last(sp)
            for dr in range(2):
                sp.dma_start(Sst[dr][:, 1], d["s_hg"][l, dr].rearrange("a p v -> p a v")).then_inc(S["ld_hg"], 16)
            sp.wait_ge(S["hg_state"], 2)
            for dr in range(2):
                sp.dma_start(o["n_hg"][0, l, dr].rearrange("(a b) k v -> a (b k) v", a=2).rearrange("a p v -> p a v"),
                             Sfin[:, dr]).then_inc(S["st_state"], 16)
            sp.wait_ge(S["st_state"], 32)

        @block.scalar
        def _(act):
            a = e.chain("act", act)
            nc.scalar.activation(q, q, ACT.Silu).then_inc(S["hg_q"], 1)
            a.add(nc.scalar.activation(tok[:, :, gcol:gcol + HH * HD], tok[:, :, gcol:gcol + HH * HD], ACT.Silu))
            act.wait_ge(S["hg_z"], 1)
            nc.scalar.activation(kT, f, ACT.Exp, scale=-1.0).then_inc(S["hg_e"], 1)
            for u, (t, dr) in enumerate(units):
                if (t, dr) in last:
                    continue
                act.wait_ge(S["kr_ps"], u + 1)
                if u >= 2:
                    act.wait_ge(S["kv_ps"], u - 1)
                nc.scalar.activation(KRt[dr], ps[:, 6, 0:2 * P].rearrange("p (a b) -> p a b", a=2), ACT.Copy
                                     ).then_inc(S["kr_sb"], 1)
            act.wait_ge(S["hg_o"], 1)
            nc.scalar.activation(QL[0][:, 0:5].rearrange("p a b c -> p (a b c)"), oS.rearrange("p a b -> p (a b)"),
                                 ACT.Square).then_inc(S["hg_sq"], 1)
            act.wait_ge(S["hg_ss"], 1)
            nc.scalar.activation(ssq, ssq, ACT.Sqrt, bias=e.eps[:, 0:1], scale=1.0 / HD).then_inc(S["hg_rt"], 1)
            for t in range(TILES):
                act.wait_ge(S["ho_ps"], t + 1)
                nc.scalar.activation(e.mixT[:, 4:6, t * P:(t + 1) * P], ps[:, t % 4, 0:2 * P].rearrange("p (k n) -> p k n", k=2),
                                     ACT.Copy).then_inc(S["ho_ev"], 1)
            e.done("act", a)

        @block.gpsimd
        def _(pool):
            c = e.chain("pool", pool)
            pool.wait_ge(S["hg_prep"], 1)
            pool.wait_ge(S["hg_q"], 1)
            k = 0
            for u, (t, dr) in enumerate(units):
                if dr == 0:
                    continue
                if k:
                    pool.wait_ge(S["oh_ps"], HH * (u - 1))
                for _ in levels(nc.gpsimd, c, u):
                    pass
                k += 1
                nc.gpsimd.memset(Rb[1][:, 0, 0:1], 1.0).then_inc(S["lv1"], 1)
                pool.wait_ge(S["lv1"], k)
            e.done("pool", c)

        @block.tensor
        def _(pe):
            kr = [0]

            def att(i):
                u, h = divmod(i, HH)
                t, dr = units[u]
                cols = slice(t * P, (t + 1) * P)
                hp, r = h // 2, slice(HD * (h % 2), HD * (h % 2) + HD)
                if h == 0:
                    pe.wait_ge(S[f"lv{dr}"], u // 2 + 1)
                if i >= 2:
                    pe.wait_ge(S["at_sb"], i - 1)
                for j in range(LV + 1):
                    lhs = kT[r, 2 * dr + hp, cols] if j <= 1 else KL[dr][r, j - 2, hp, :]
                    rhs = q[r, hp, cols] if j == 0 else QL[dr][r, j - 1, hp, :]
                    m = nc.tensor.matmul(ps[:, 2 * (i % 2) + j // 4, (j % 4) * P:(j % 4 + 1) * P], lhs, rhs, start=True, stop=True)
                m.then_inc(S["at_ps"], 1)

            def out(i):
                u, h = divmod(i, HH)
                t, dr = units[u]
                hp, r = h // 2, slice(HD * (h % 2), HD * (h % 2) + HD)
                if h == 0 and u:
                    pe.wait_ge(S["ou_sb"], 2 * u)
                dst = ps[:, 4 + h % 2, hp * HD:(hp + 1) * HD]
                pe.wait_ge(S["at_sb"], i + 1)
                for j in range(LV + 1):
                    m = nc.tensor.matmul(dst, am[:, i % 2, j * P:(j + 1) * P], tok[:, t, vcol + h * HD:vcol + (h + 1) * HD],
                                         start=j == 0, stop=j == LV and t == 0)
                if t:
                    k = u // 2
                    if h == 0:
                        if k == 1:
                            pe.wait_ge(S["ld_hg"], 32)
                        else:
                            pe.wait_ge(S["st_new"], u - 1)
                    m = nc.tensor.matmul(dst, QL[dr][r, LV, hp, :], Sst[dr][r, k % 2, hp, :], start=False, stop=True)
                m.then_inc(S["oh_ps"], 1)

            for i in range(U * HH):
                u, h = divmod(i, HH)
                t, dr = units[u]
                att(i)
                if h == 0 and (t, dr) not in last:
                    if kr[0]:
                        pe.wait_ge(S["kr_sb"], kr[0])
                    for a in range(2):
                        m = nc.tensor.transpose(ps[:, 6, a * P:(a + 1) * P], KL[dr][:, LV - 1, a, :], e.ident[:, :])
                    m.then_inc(S["kr_ps"], 1)
                if i:
                    out(i - 1)
                if h == 1 and (t, dr) not in last:
                    kr[0] += 1
                    pe.wait_ge(S["kr_sb"], kr[0])
                    if kr[0] > 1:
                        pe.wait_ge(S["st_new"], kr[0] - 1)
                    for hh in range(HH):
                        m = nc.tensor.matmul(ps[HD * (hh % 2):HD * (hh % 2) + HD, 7, (hh // 2) * HD:(hh // 2 + 1) * HD],
                                             KRt[dr][:, hh // 2, HD * (hh % 2):HD * (hh % 2) + HD],
                                             tok[:, t, vcol + hh * HD:vcol + (hh + 1) * HD], start=True, stop=True)
                    m.then_inc(S["kv_ps"], 1)
            out(U * HH - 1)
            for t in range(TILES):
                pe.wait_ge(S["hg_on"], 1)
                if t >= 4:
                    pe.wait_ge(S["ho_ev"], t - 3)
                for k in range(2):
                    m = nc.tensor.transpose(ps[:, t % 4, k * P:(k + 1) * P], oS[:, t, k * P:(k + 1) * P], e.ident[:, :])
                m.then_inc(S["ho_ps"], 1)

        @block.vector
        def _(dve):
            v = e.chain("dve", dve)
            nc.vector.tensor_scalar(f, f, 60.0, -60.0, ALU.min, ALU.max).then_inc(S["hg_z"], 1)
            dve.wait_ge(S["hg_e"], 1)
            v.link(nc.vector.tensor_scalar(f, kT, 1.0, None, ALU.add))
            v.link(nc.vector.reciprocal(f, f))
            v.link(nc.vector.tensor_tensor(kT, kT, f, ALU.mult))
            for c in range(4):
                v.add(nc.vector.scalar_tensor_tensor(f[:, c, :], kT[:, c, :], e.lb[:, c:c + 1], f[:, c, :], ALU.mult, ALU.add))
            v.join()
            for c in range(4):
                m = nc.vector.tensor_scalar(kT[:, c, :], kT[:, c, :], e.oml[:, c:c + 1], None, ALU.mult)
                if c < 3:
                    v.add(m)
            v.join()
            m.then_inc(S["hg_prep"], 1)
            dve.wait_ge(S["hg_prep"], 1)
            dve.wait_ge(S["hg_q"], 1)

            def run_levels(u):
                if u:
                    dve.wait_ge(S["oh_ps"], HH * (u - 1))
                for _ in levels(nc.vector, v, u):
                    yield
                nc.vector.memset(Rb[0][:, 0, 0:1], 1.0).then_inc(S["lv0"], 1)
                dve.wait_ge(S["lv0"], u // 2 + 1)

            def collect(u):
                t, dr = units[u]
                dve.wait_ge(S["oh_ps"], HH * (u + 1))
                seen = t in [x for x, _ in units[:u]]
                if seen:
                    dve.wait_ge(S["ou_sb"], 2 * u)
                for b in range(2):
                    src = ps[:, 4 + b, 0:2 * HD].rearrange("p (a v) -> p a v", a=2)
                    dst = oS[:, t, :].rearrange("p (a b v) -> p a b v", a=2, b=2)[:, :, b, :]
                    if seen:
                        nc.vector.tensor_tensor(dst, dst, src, ALU.add).then_inc(S["ou_sb"], 1)
                    else:
                        nc.vector.tensor_copy(dst, src).then_inc(S["ou_sb"], 1)

            for _ in run_levels(0):
                pass
            ns = 0
            for u, (t, dr) in enumerate(units):
                nxt = run_levels(u + 1) if dr == 1 and u + 1 < U else None
                for h in range(HH):
                    i = u * HH + h
                    dve.wait_ge(S["at_ps"], i + 1)
                    if i >= 2:
                        dve.wait_ge(S["oh_ps"], i - 1)
                    nc.vector.tensor_tensor(am[:, i % 2, :], ps[:, 2 * (i % 2):2 * (i % 2) + 2, :].rearrange("p a b -> p (a b)"),
                                            e.hgm[:, dr, :], ALU.mult).then_inc(S["at_sb"], 1)
                    if h == 0 and u:
                        collect(u - 1)
                    if h == 2 and (t, dr) not in last:
                        ns += 1
                        dve.wait_ge(S["kv_ps"], ns)
                        v.join()
                        if dr == 0:
                            dve.wait_ge(S["lv0"], u // 2 + 1)
                        else:
                            dve.wait_ge(S["lv1"], u // 2 + 1)
                        k = u // 2
                        src = ps[:, 7, 0:2 * HD].rearrange("p (a b) -> p a b", a=2)
                        if t == 0:
                            m = nc.vector.tensor_copy(Sfin[:, dr], src)
                            m.then_inc(S["st_new"], 1)
                            dve.wait_ge(S["st_new"], ns)
                            dve.sem_inc(S["hg_state"], 1)
                        else:
                            dve.wait_ge(S["ld_hg"], 32)
                            dve.wait_ge(S["st_new"], ns - 1)
                            for a in range(2):
                                m = nc.vector.scalar_tensor_tensor(Sst[dr][:, (k + 1) % 2, a], Sst[dr][:, k % 2, a],
                                                                   Ft[:, u, a:a + 1], src[:, a], ALU.mult, ALU.add)
                                if a == 0:
                                    v.add(m)
                            v.join()
                            m.then_inc(S["st_new"], 1)
                    if nxt and h < HH - 1:
                        for _ in range(12):
                            if next(nxt, "end") == "end":
                                nxt = None
                                break
                if nxt:
                    for _ in nxt:
                        pass
            collect(U - 1)
            dve.wait_ge(S["ou_sb"], 2 * U)
            dve.sem_inc(S["hg_o"], 1)
            ov = oS.rearrange("p t (h v) -> p (t h) v", v=HD)
            dve.wait_ge(S["hg_sq"], 1)
            nc.vector.reduce_sum(ssq, QL[0][:, 0:5].rearrange("p a b c -> p (a b c)").rearrange("p (n v) -> p n v", v=HD), AX
                                 ).then_inc(S["hg_ss"], 1)
            v.link(nc.vector.tensor_tensor(oS, oS, e.prow[:, 1:2, :].to_broadcast([P, TILES, HH * HD]), ALU.mult))
            v.link(nc.vector.tensor_tensor(oS, oS, tok[:, :, gcol:gcol + HH * HD], ALU.mult))
            dve.wait_ge(S["hg_rt"], 1)
            v.link(nc.vector.reciprocal(ssq, ssq))
            nc.vector.tensor_tensor(ov, ov, ssq.rearrange("p (n o) -> p n o", o=1).to_broadcast([P, TILES * HH, HD]), ALU.mult
                                    ).then_inc(S["hg_on"], 1)
            e.done("dve", v)


RWKV_SEMS = (
    "ld_rw", "rw_om", "rw_f0", "rw_feat", "rw_th", "rw_k0", "rw_ksq", "lo_ps", "lo_ev", "vt_ps", "vt_ev", "kn_ps",
    "rw_kmax", "rw_krt", "rw_kn", "rw_kd", "rw_bon", "rw_E", "rw_ex", "rw_pre", "rw_G0", "rw_G", "m_ps", "l_ps",
    "kb_ps", "kb_sb", "mj", "t1_ps", "t1_sb", "sm", "vz", "rh_ps", "rh_sb", "u_ps", "u_sb", "rs_ps", "y_ps", "y_ev",
    "rw_sfin", "fin_ps", "rw_fin", "st_rw", "gn_c", "gn_sq", "gn_var", "gn_rt", "bo_ps", "ga_ps", "rw_out", "ro_ps",
    "ro_ev", "dxy_ps", "ls", "m_sb", "mt_ps", "mt_sb", "xy", "xy1",
)


def phase_rwkv(e):
    nc, d, o, l, S, ps = e.nc, e.d, e.o, e.l, e.S, e.ps
    R = slice(0, NTOK)
    HI, LO = slice(C, P), slice(0, C)
    kk, z = e.part(e.a0, 2, NTOK)
    T, z = e.part(z, 3, NTOK)
    assert z <= e.a1
    KB, z = e.part(e.a1, 4, NCH, 2, C)
    assert z <= e.a2
    F, z = e.part(e.a2, NRW, NTOK)
    AR, z = e.part(z, 4, 2, NTOK)
    Vc, z = e.part(z, NCH, HH * HD, rows=C)
    VU, z = e.part(z, 2, 8, HD)
    KBt, z = e.part(z, 2, 4, P)
    RH, z = e.part(z, HH, HD)
    Sm, z = e.part(z, 4, 2, HD)
    Sn, z = e.part(z, 4, 2, HD)
    S0, z = e.part(z, 4, HD)
    S0b, z = e.part(z, 4, 2, HD)
    Sfin, z = e.part(z, 4, 2, HD)
    yst0 = z
    Yst, z = e.part(z, 2, TILES, HH, P)
    sq, _ = e.part(yst0, NCH * HH * HD, rows=C)
    Ms, z1 = e.part(e.a0, 2, HH, P)
    Mj, z1 = e.part(z1, 2, 2, HH, P)
    assert z1 <= e.a1
    M, z1 = e.part(e.a0, 2, 8, P)
    So, z1 = e.part(z1, 4, P)
    assert z1 <= e.a1
    X, z1 = e.part(e.a2, 2, HH, P)
    T1, z1 = e.part(z1, 2, HH, P)
    ys, _ = e.part(e.a2, NCH, HH * HD, rows=C)
    mid, z = e.part(z, 4, NCH)
    end, z = e.part(z, 4, NCH)
    G, z = e.part(z, 4, NCH)
    Gb, z = e.part(z, 4, NCH, 2)
    om, z = e.part(z, NRW)
    mu, z = e.part(z, NCH * HH, rows=C)
    rs, z = e.part(z, NCH * HH, rows=C)
    wwa, z = e.part(z, 2, HH * HD)
    g2, z = e.part(z, HH * HD)
    assert z <= 40600, z
    cut = ((NPR, NTOK), (0, NPR))
    DECAY = -float(np.exp(-0.5))
    steps = [(0, 1), (1, 0)] + [(2 + i, NCH - 1 - i) for i in range(NCH - 2)]
    NS = len(steps)
    LVC = 5

    def blockrow(c):
        return slice(C * (c % 2), C * (c % 2) + C)

    first = (True, False) + (True,) * 4 + (False,) * 4
    pc = e.pcol

    def col(name, i):
        return pc[:, PC[name] + i:PC[name] + i + 1]

    def ck(c):
        return slice(C * c, C * c + C)

    def by_chunk(a):
        return a.rearrange("p (c t) -> p c t", t=C)

    lora = [(w, dr, pair, i) for w in range(2) for dr in range(2) for pair in range(2) for i in range(2)]

    with nc.Block() as block:
        @block.sync
        def _(sp):
            e.clear_last(sp)
            sp.dma_start(wwa, d["w_wa"][l]).then_inc(S["ld_rw"], 16)
            sp.dma_start(g2, d["w_g2"][l]).then_inc(S["ld_rw"], 16)
            sp.dma_start(S0, d["s_rw"][l].rearrange("d a p v -> p (d a) v")).then_inc(S["ld_rw"], 16)
            sp.wait_ge(S["rw_fin"], 1)
            for dr in range(2):
                for par in range(2):
                    sp.dma_start(o["n_rw"][0, l, dr].rearrange("(a b) v k -> b v a k", a=2)[par],
                                 So[par * HD:(par + 1) * HD, 2 * dr:2 * dr + 2, par * HD:(par + 1) * HD]).then_inc(S["st_rw"], 16)
            sp.wait_ge(S["st_rw"], 64)

        @block.scalar
        def _(act):
            a = e.chain("act", act)
            act.wait_ge(S["rw_om"], 1)
            for c in range(NRW):
                for c0, c1 in cut:
                    q0 = pad_at(c0)
                    nc.scalar.activation(F[:, c, c0:c1], e.rwT[:, c, q0:q0 + c1 - c0], ACT.Copy, scale=om[:, c:c + 1]
                                         ).then_inc(S["rw_f0"], 1)
            act.wait_ge(S["rw_feat"], 1)
            nc.scalar.activation(F[:, 6, R], F[:, 6, R], ACT.Tanh).then_inc(S["rw_th"], 1)
            for p in range(2):
                act.wait_ge(S["rw_k0"], p + 1)
                nc.scalar.activation(T[:, p, R], kk[:, p, R], ACT.Square).then_inc(S["rw_ksq"], 1)
            for n, (w, dr, pair, i) in enumerate(lora):
                act.wait_ge(S["lo_ps"], n + 1)
                c0, c1 = cut[i]
                dst = by_chunk(AR[:, 2 * dr + pair, 0, c0:c1]) if w == 0 else KB[:, 2 * dr + pair, c0 // C:c1 // C, 1, :]
                nc.scalar.activation(dst, by_chunk(ps[:, n % 4 * 2 + dr, 0:c1 - c0]), ACT.Sigmoid, bias=col("a0" if w else "w0", 2 * dr + pair)
                                     ).then_inc(S["lo_ev"], 1)
            a.add(nc.scalar.activation(F[:, 8, R], F[:, 8, R], ACT.Sigmoid))
            for n in range(NCH // 2):
                act.wait_ge(S["vt_ps"], n + 1)
                nc.scalar.activation(Vc[:, 2 * n:2 * n + 2, :], ps[LO, 2 * (n % 2), :].rearrange("p (a b) -> p a b", a=2), ACT.Copy
                                     ).then_inc(S["vt_ev"], 1)
            for p in range(2):
                act.wait_ge(S["rw_kmax"], p + 1)
                nc.scalar.activation(T[:, p, R], T[:, p, R], ACT.Sqrt).then_inc(S["rw_krt"], 1)
            for dp in range(4):
                act.wait_ge(S["rw_E"], dp + 1)
                nc.scalar.activation(T[:, 2, R], T[:, 0, R], ACT.Exp, scale=-1.0).then_inc(S["rw_ex"], 1)
                nc.scalar.activation(AR[:, dp, 1, R], T[:, 0, R], ACT.Exp).then_inc(S["rw_ex"], 1)
                nc.scalar.activation(AR[:, dp, 0, R], AR[:, dp, 0, R], ACT.Exp).then_inc(S["rw_ex"], 1)
            act.wait_ge(S["rw_G0"], 1)
            a.link(nc.scalar.activation(G, G, ACT.Exp))
            nc.scalar.activation(mid, mid, ACT.Exp).then_inc(S["rw_G"], 1)
            for t in range(TILES):
                for ln in range(2):
                    act.wait_ge(S["mt_ps"], 2 * t + ln + 1)
                    if t:
                        act.wait_ge(S["mj"], 2 * LVC * t)
                    nc.scalar.activation(Ms[:, ln], ps[:, 6 + ln, :].rearrange("p (a b) -> p a b", a=HH), ACT.Copy
                                         ).then_inc(S["mt_sb"], 1)
                for j in range(LVC):
                    for ln in range(2):
                        act.wait_ge(S["t1_ps"], (LVC * t + j) * 2 + ln + 1)
                        nc.scalar.activation(T1[:, ln], ps[:, 4 + ln, :].rearrange("p (a b) -> p a b", a=HH), ACT.Copy
                                             ).then_inc(S["t1_sb"], 1)
            for s in range(-1, NS):
                if s >= 0:
                    for dr in range(2):
                        act.wait_ge(S["u_ps"], 2 * s + dr + 1)
                        nc.scalar.activation(VU[HI, s % 2, 4 * dr:4 * dr + 4], ps[HI, 5 + dr, 0:4 * HD].rearrange("p (a b) -> p a b", a=4),
                                             ACT.Copy, scale=-1.0).then_inc(S["u_sb"], 1)
                if s + 1 < NS:
                    act.wait_ge(S["kb_ps"], s + 2)
                    nc.scalar.activation(KBt[:, (s + 1) % 2], ps[:, 4, :].rearrange("p (a b) -> p a b", a=4), ACT.Copy
                                         ).then_inc(S["kb_sb"], 1)
            act.wait_ge(S["fin_ps"], 1)
            nc.scalar.activation(So.rearrange("p a b -> p (a b)"), ps[:, 6, :], ACT.Copy).then_inc(S["rw_fin"], 1)
            act.wait_ge(S["gn_c"], 1)
            nc.scalar.activation(sq, ys.rearrange("p a b -> p (a b)"), ACT.Square).then_inc(S["gn_sq"], 1)
            act.wait_ge(S["gn_var"], 1)
            nc.scalar.activation(rs, rs, ACT.Sqrt, bias=e.eps[LO, 2:3], scale=1.0 / HD).then_inc(S["gn_rt"], 1)
            for k in range(2):
                act.wait_ge(S["ro_ps"], k + 1)
                nc.scalar.activation(e.mixT[:, 6 + k, :], ps[:, 2 * k:2 * k + 2, :].rearrange("p a b -> p (a b)")[:, 0:NTOK],
                                     ACT.Copy).then_inc(S["ro_ev"], 1)
            e.done("act", a)

        @block.gpsimd
        def _(pool):
            c = e.chain("pool", pool)
            for dp in range(4):
                dr, p = divmod(dp, 2)
                if dp == 0:
                    pool.wait_ge(S["lo_ev"], len(lora))
                    pool.wait_ge(S["rw_kn"], 2)
                c.link(nc.gpsimd.tensor_scalar(by_chunk(T[:, 1, R]), KB[:, dp, :, 1, :], -1.0, col("ka", p), ALU.add, ALU.mult))
                c.link(nc.gpsimd.tensor_scalar(T[:, 1, R], T[:, 1, R], 1.0, None, ALU.add))
                c.link(nc.gpsimd.tensor_tensor(KB[:, dp, :, 0, :], by_chunk(T[:, 1, R]), by_chunk(F[:, 2 + p, R]), ALU.mult))
                if dr == 0:
                    c.link(nc.gpsimd.tensor_copy(by_chunk(F[:, 6 + p, R]), KB[:, dp, :, 0, :]))
                else:
                    c.link(nc.gpsimd.tensor_tensor(by_chunk(F[:, 6 + p, R]), by_chunk(F[:, 6 + p, R]), KB[:, dp, :, 0, :], ALU.add))
                nc.gpsimd.tensor_tensor(KB[:, dp, :, 1, :], KB[:, dp, :, 1, :], by_chunk(kk[:, p, R]), ALU.mult).then_inc(S["rw_kd"], 1)
                pool.wait_ge(S["rw_kd"], dp + 1)
            for p in range(2):
                c.link(nc.gpsimd.tensor_tensor(F[:, 6 + p, R], F[:, 6 + p, R], F[:, p, R], ALU.mult))
                nc.gpsimd.tensor_scalar(F[:, 6 + p, R], F[:, 6 + p, R], col("rk", p), None, ALU.mult).then_inc(S["rw_bon"], 1)
            pool.wait_ge(S["rw_pre"], 4)

            def masked(dst, src, dr, j):
                return nc.gpsimd.tensor_tensor(dst, src, e.hgm[:, dr, (j + 1) * P:(j + 2) * P].rearrange("p (o n) -> p o n", o=1)
                                               .to_broadcast([P, HH, P]), ALU.mult)

            def next_mask(t, j, ln):
                k = LVC * t + j
                if k >= 2:
                    pool.wait_ge(S["t1_ps"], 2 * (k - 2) + ln + 1)
                masked(Mj[:, ln, k % 2], Ms[:, ln], ln, j + 1).then_inc(S["mj"], 1)

            idn = e.ident[:, :].rearrange("p (o n) -> p o n", o=1).to_broadcast([P, HH, P])
            for t in range(TILES):
                for ln in range(2):
                    pool.wait_ge(S["mt_sb"], 2 * t + ln + 1)
                    c.add(masked(X[:, ln], T1[:, ln], 1 - ln, 0))
                    c.link(masked(Yst[:, ln, t], Ms[:, ln], ln, 0))
                    c.add(nc.gpsimd.tensor_tensor(X[:, ln], idn, X[:, ln], ALU.subtract))
                    c.link(nc.gpsimd.tensor_tensor(Yst[:, ln, t], idn, Yst[:, ln, t], ALU.subtract))
                    pool.sem_inc(S["xy1"], 1)
                    next_mask(t, 0, ln)
                for j in range(1, LVC):
                    for ln in range(2):
                        next_mask(t, j, ln)
            pool.wait_ge(S["vt_ev"], NCH // 2)
            for s, chunks in enumerate(steps):
                if s >= 2:
                    pool.wait_ge(S["y_ps"], s - 1)
                for dr in range(2):
                    c.add(nc.gpsimd.tensor_copy(VU[LO, s % 2, 4 * dr:4 * dr + 4, :],
                                                Vc[:, chunks[dr], :].rearrange("p (a v) -> p a v", a=4)))
                c.join()
                nc.gpsimd.memset(VU[HI, s % 2], 0.0).then_inc(S["vz"], 1)
            e.done("pool", c)

        @block.tensor
        def _(pe):
            pe.wait_ge(S["ld_rw"], 48)
            pe.wait_ge(S["rw_th"], 1)
            for n, (w, dr, pair, i) in enumerate(lora):
                if n >= 4:
                    pe.wait_ge(S["lo_ev"], n - 3)
                c0, c1 = cut[i]
                r = slice(C * dr, C * dr + C)
                nc.tensor.matmul(ps[:, n % 4 * 2 + dr, 0:c1 - c0], wwa[r, w, pair * P:(pair + 1) * P], F[r, 6 + w, c0:c1],
                                 start=True, stop=True).then_inc(S["lo_ps"], 1)
            pe.wait_ge(S["lo_ev"], len(lora))
            for n in range(NCH // 2):
                if n >= 2:
                    pe.wait_ge(S["vt_ev"], n - 1)
                for i in range(2):
                    for p in range(2):
                        m = nc.tensor.transpose(ps[LO, 2 * (n % 2), i * 256 + p * P:i * 256 + (p + 1) * P], F[:, 4 + p, ck(2 * n + i)],
                                                e.ident[:, :])
                m.then_inc(S["vt_ps"], 1)
            for p in range(2):
                pe.wait_ge(S["rw_ksq"], p + 1)
                for i, (c0, c1) in enumerate(cut):
                    m = nc.tensor.matmul(ps[:, 4 + 2 * p + i, 0:c1 - c0], e.blk[:, :], T[:, p, c0:c1], start=True, stop=True)
                    m.then_inc(S["kn_ps"], 1)
            pe.wait_ge(S["rw_pre"], 4)
            for t in range(TILES):
                for ln in range(2):
                    if t:
                        pe.wait_ge(S["xy"], 2 * (LVC * t - 1) + ln + 1)
                    for par in range(2):
                        for pair in range(2):
                            r, dp = slice(HD * par, HD * par + HD), 2 * ln + pair
                            m = nc.tensor.matmul(ps[:, 2 * ln + par, pair * P:(pair + 1) * P], AR[r, dp, 0, t * P:(t + 1) * P],
                                                 KB[r, dp, 2 * t:2 * t + 2, 1, :], start=True, stop=True)
                        m.then_inc(S["l_ps"], 1)
                for ln in range(2):
                    pe.wait_ge(S["ls"], 2 * t + ln + 1)
                    for h in range(HH):
                        m = nc.tensor.transpose(ps[:, 6 + ln, h * P:(h + 1) * P], T1[:, ln, h, :], e.ident[:, :])
                    m.then_inc(S["mt_ps"], 1)
                for j in range(LVC):
                    for ln in range(2):
                        n = (LVC * t + j) * 2 + ln
                        if j == 0:
                            pe.wait_ge(S["xy1"], 2 * t + ln + 1)
                        else:
                            pe.wait_ge(S["xy"], n - 1)
                        pe.wait_ge(S["mj"], n + 1)
                        for h in range(HH):
                            m = nc.tensor.matmul(ps[:, 4 + ln, h * P:(h + 1) * P], Mj[:, ln, (LVC * t + j) % 2, h, :], X[:, ln, h, :],
                                                 start=True, stop=True)
                        m.then_inc(S["t1_ps"], 1)
                    for ln in range(2):
                        pe.wait_ge(S["t1_sb"], (LVC * t + j) * 2 + ln + 1)
                        if j < LVC - 1:
                            for h in range(HH):
                                nc.tensor.matmul(ps[:, 2 * ln, h * P:(h + 1) * P], Yst[:, ln, t, h, :], T1[:, ln, h, :],
                                                 start=True, stop=True)
                        for h in range(HH):
                            m = nc.tensor.matmul(ps[:, 2 * ln + 1, h * P:(h + 1) * P], T1[:, ln, h, :], Yst[:, ln, t, h, :],
                                                 start=True, stop=True)
                        m.then_inc(S["dxy_ps"], 1)
            pe.wait_ge(S["rw_G"], 1)
            pe.wait_ge(S["xy"], 2 * LVC * TILES)

            def matrices(s):
                chunks = steps[s]
                if s:
                    pe.wait_ge(S["m_sb"], 4 * s)
                    pe.wait_ge(S["kb_sb"], s)
                for par in range(2):
                    for dp in range(4):
                        r, c = slice(HD * par, HD * par + HD), chunks[dp // 2]
                        m = nc.tensor.matmul(ps[:, par, dp * P:(dp + 1) * P], KB[r, dp, c].rearrange("p a b -> p (a b)"),
                                             AR[r, dp, :, ck(c)], start=True, stop=True)
                    m.then_inc(S["m_ps"], 1)
                for dp in range(4):
                    m = nc.tensor.transpose(ps[:, 4, dp * P:(dp + 1) * P], KB[:, dp, chunks[dp // 2]].rearrange("p a b -> p (a b)"),
                                            e.ident[:, :])
                m.then_inc(S["kb_ps"], 1)

            def with_state(dst, dp, c, w, s):
                nc.tensor.matmul(dst, AR[:, dp, w, ck(c)], Sm[:, dp].rearrange("p a b -> p (a b)"), start=True, stop=False,
                                 skip_group_check=True)
                for par in range(2):
                    u = 2 * dp + par
                    m = nc.tensor.matmul(dst[:, par * HD:(par + 1) * HD], M[:, s % 2, u, w * C:(w + 1) * C], VU[:, s % 2, u, :],
                                         start=False, stop=True, skip_group_check=True)
                return m

            matrices(0)
            for s, chunks in enumerate(steps):
                pe.wait_ge(S["sm"], s + 1)
                pe.wait_ge(S["vz"], s + 1)
                pe.wait_ge(S["m_sb"], 4 * s + 4)
                for dp in range(4):
                    c = chunks[dp // 2]
                    m = with_state(ps[blockrow(c), 2, (dp % 2) * P:(dp % 2 + 1) * P], dp, c, 0, s)
                m.then_inc(S["rh_ps"], 1)
                pe.wait_ge(S["rh_sb"], s + 1)
                if s:
                    pe.wait_ge(S["y_ev"], s)
                for dr in range(2):
                    c = chunks[dr]
                    for h in range(HH):
                        m = nc.tensor.matmul(ps[HI, 5 + dr, h * HD:(h + 1) * HD], Yst[blockrow(c), dr, c // 2, h, blockrow(c)],
                                             RH[blockrow(c), h, :], start=True, stop=True)
                    m.then_inc(S["u_ps"], 1)
                if s + 1 < NS:
                    matrices(s + 1)
                pe.wait_ge(S["u_sb"], 2 * s + 2)
                pe.wait_ge(S["kb_sb"], s + 1)
                for dp in range(4):
                    m = nc.tensor.matmul(ps[:, 7, dp * P:(dp + 1) * P], KBt[:, s % 2, dp, :],
                                         VU[:, s % 2, 2 * dp:2 * dp + 2, :].rearrange("p a b -> p (a b)"), start=True, stop=True)
                m.then_inc(S["rs_ps"], 1)
                for dp in range(4):
                    m = with_state(ps[LO, 5, dp * P:(dp + 1) * P], dp, chunks[dp // 2], 1, s)
                m.then_inc(S["y_ps"], 1)
            pe.wait_ge(S["rw_sfin"], 1)
            for dp in range(4):
                m = nc.tensor.transpose(ps[:, 6, dp * P:(dp + 1) * P], Sfin[:, dp].rearrange("p a b -> p (a b)"), e.ident[:, :])
            m.then_inc(S["fin_ps"], 1)
            pe.wait_ge(S["rw_bon"], 2)
            pe.wait_ge(S["y_ev"], NS)
            for c in range(NCH):
                for p in range(2):
                    m = nc.tensor.matmul(ps[LO, 7, c * HH + 2 * p:c * HH + 2 * p + 2], F[:, 6 + p, ck(c)], e.blk[:, 0:P:C],
                                         start=True, stop=True)
            m.then_inc(S["bo_ps"], 1)
            for c in range(NCH):
                m = nc.tensor.matmul(ps[LO, c // 2, (c % 2) * 256:(c % 2 + 1) * 256], F[:, 8, ck(c)], g2, start=True, stop=True)
            m.then_inc(S["ga_ps"], 1)
            pe.wait_ge(S["rw_out"], 1)
            for k in range(2):
                for c in range(NCH):
                    m = nc.tensor.transpose(ps[:, 2 * k + c // 8, (c % 8) * C:(c % 8 + 1) * C], ys[:, c, k * P:(k + 1) * P],
                                            e.ident[LO, LO])
                m.then_inc(S["ro_ps"], 1)

        @block.vector
        def _(dve):
            v = e.chain("dve", dve)
            mu0, mu1 = (pc[:, PC[n]:PC[n] + NRW] for n in ("mu0", "mu1"))
            v.link(nc.vector.tensor_tensor(om, mu0, mu1, ALU.add))
            nc.vector.tensor_scalar(om, om, -1.0, 1.0, ALU.mult, ALU.add).then_inc(S["rw_om"], 1)
            for c in range(NRW):
                dve.wait_ge(S["rw_f0"], 2 * (c + 1))
                for c0, c1 in cut:
                    q0 = pad_at(c0) - 1
                    v.add(nc.vector.scalar_tensor_tensor(F[:, c, c0:c1], e.rwT[:, c, q0:q0 + c1 - c0], col("mu0", c), F[:, c, c0:c1],
                                                         ALU.mult, ALU.add))
            v.join()
            for c in range(NRW):
                for c0, c1 in cut:
                    q0 = pad_at(c0) + 1
                    v.add(nc.vector.scalar_tensor_tensor(F[:, c, c0:c1], e.rwT[:, c, q0:q0 + c1 - c0], col("mu1", c), F[:, c, c0:c1],
                                                         ALU.mult, ALU.add))
            v.join()
            dve.sem_inc(S["rw_feat"], 1)
            dve.wait_ge(S["rw_feat"], 1)
            for p in range(2):
                nc.vector.tensor_scalar(kk[:, p, R], F[:, 2 + p, R], col("kk", p), None, ALU.mult).then_inc(S["rw_k0"], 1)
            for p in range(2):
                dve.wait_ge(S["kn_ps"], 2 * p + 2)
                for i, (c0, c1) in enumerate(cut):
                    m = nc.vector.tensor_scalar(T[:, p, c0:c1], ps[:, 4 + 2 * p + i, 0:c1 - c0], 1e-12, None, ALU.max)
                    if i == 0:
                        v.link(m)
                m.then_inc(S["rw_kmax"], 1)
            for p in range(2):
                dve.wait_ge(S["rw_krt"], p + 1)
                v.link(nc.vector.reciprocal(T[:, p, R], T[:, p, R]))
                dve.wait_ge(S["rw_k0"], p + 1)
                nc.vector.tensor_tensor(kk[:, p, R], kk[:, p, R], T[:, p, R], ALU.mult).then_inc(S["rw_kn"], 1)
            dve.wait_ge(S["rw_kn"], 2)
            dve.wait_ge(S["lo_ev"], len(lora))
            for dp in range(4):
                dr, p = divmod(dp, 2)
                lw = AR[:, dp, 0, R]
                v.link(nc.vector.tensor_scalar(lw, lw, DECAY, None, ALU.mult))
                if dp:
                    dve.wait_ge(S["rw_ex"], 3 * dp)
                a, b, c = e.reset[:, dr, R], lw, T[:, 0, R]
                if dr:
                    a, b, c = a[:, ::-1], b[:, ::-1], c[:, ::-1]
                v.link(nc.vector.tensor_tensor_scan(c, a, b, 0.0, ALU.mult, ALU.add))
                m0, e0 = (C // 2 - 1, C - 1) if dr == 0 else (C // 2, 0)
                g = by_chunk(T[:, 0, R])
                per = lambda a: a[:, dp, :].rearrange("p (c o) -> p c o", o=1)
                v.add(nc.vector.tensor_copy(per(mid), g[:, :, m0:m0 + 1]))
                v.link(nc.vector.tensor_copy(per(end), g[:, :, e0:e0 + 1]))
                v.link(nc.vector.tensor_tensor(g, g, per(mid).to_broadcast([P, NCH, C]), ALU.subtract))
                nc.vector.tensor_tensor(lw, T[:, 0, R], lw, ALU.subtract).then_inc(S["rw_E"], 1)
                dve.wait_ge(S["rw_E"], dp + 1)
                dve.wait_ge(S["rw_kd"], dp + 1)
                dve.wait_ge(S["rw_ex"], 3 * dp + 1)
                for w in range(2):
                    v.add(nc.vector.tensor_tensor(KB[:, dp, :, w, :], KB[:, dp, :, w, :], by_chunk(T[:, 2, R]), ALU.mult))
                dve.wait_ge(S["rw_ex"], 3 * dp + 2)
                v.add(nc.vector.tensor_tensor(AR[:, dp, 1, R], AR[:, dp, 1, R], F[:, p, R], ALU.mult))
                dve.wait_ge(S["rw_ex"], 3 * dp + 3)
                m = nc.vector.tensor_tensor(lw, lw, kk[:, p, R], ALU.mult)
                v.link(m)
                dve.sem_inc(S["rw_pre"], 1)
            v.link(nc.vector.tensor_tensor(G, end, mid, ALU.subtract))
            for dst, src, rows in ((slice(0, 1), slice(1, 2), (0, 2)), (slice(2, NCH - 1), slice(3, NCH), (0, 2)),
                                   (slice(1, 2), slice(0, 1), (2, 4)), (slice(3, NCH), slice(2, NCH - 1), (2, 4))):
                q = slice(*rows)
                v.link(nc.vector.tensor_tensor(G[:, q, dst], G[:, q, dst], mid[:, q, src], ALU.add))
            dve.sem_inc(S["rw_G0"], 1)
            v.add(nc.vector.memset(Sm, 0.0))
            v.add(nc.vector.memset(S0b, 0.0))
            v.link(nc.vector.memset(Gb, 0.0))
            dve.wait_ge(S["rw_G"], 1)
            dve.wait_ge(S["ld_rw"], 48)
            for par, r in enumerate((LO, HI)):
                v.add(nc.vector.tensor_copy(Gb[r, :, :, par:par + 1], G[r].rearrange("p a (c o) -> p a c o", o=1)))
                for dr, c in ((0, 2), (1, NCH - 1)):
                    v.add(nc.vector.tensor_tensor(S0b[r, 2 * dr:2 * dr + 2, par, :], S0[r, 2 * dr:2 * dr + 2, :],
                                                  mid[r, 2 * dr:2 * dr + 2, c:c + 1].to_broadcast([C, 2, HD]), ALU.mult))
            v.join()
            dve.sem_inc(S["sm"], 1)
            dve.wait_ge(S["rw_bon"], 2)
            for t in range(TILES):
                for ln in range(2):
                    strict = e.bds[:, ln:ln + 1, :].to_broadcast([P, 2, P])
                    for par in range(2):
                        dve.wait_ge(S["l_ps"], 4 * t + 2 * ln + par + 1)
                        dst = T1[:, ln].rearrange("p (a b) c -> p a b c", a=2)[:, :, par, :]
                        v.add(nc.vector.tensor_tensor(dst, ps[:, 2 * ln + par, 0:2 * P].rearrange("p (a b) -> p a b", a=2), strict,
                                                      ALU.mult))
                    v.join()
                    dve.sem_inc(S["ls"], 1)
                for j in range(LVC):
                    for ln in range(2):
                        dve.wait_ge(S["dxy_ps"], (LVC * t + j) * 2 + ln + 1)
                        if j < LVC - 1:
                            v.add(nc.vector.tensor_tensor(X[:, ln], X[:, ln], ps[:, 2 * ln, :].rearrange("p (a b) -> p a b", a=HH),
                                                          ALU.subtract))
                        v.link(nc.vector.tensor_tensor(Yst[:, ln, t], Yst[:, ln, t],
                                                       ps[:, 2 * ln + 1, :].rearrange("p (a b) -> p a b", a=HH), ALU.subtract))
                        dve.sem_inc(S["xy"], 1)

            def mask(s):
                for par in range(2):
                    dve.wait_ge(S["m_ps"], 2 * s + par + 1)
                    Mv = M[:, s % 2].rearrange("p (d a b) c -> p d a b c", d=2, a=2)
                    for dr in range(2):
                        nc.vector.tensor_tensor(Mv[:, dr, :, par, :], ps[:, par, dr * 2 * P:(dr + 1) * 2 * P].rearrange("p (a c) -> p a c", a=2),
                                                e.rwm[:, dr:dr + 1, :].to_broadcast([P, 2, P]), ALU.mult).then_inc(S["m_sb"], 1)

            mask(0)
            for s, chunks in enumerate(steps):
                dve.wait_ge(S["rh_ps"], s + 1)
                nc.vector.tensor_copy(RH, ps[:, 2, 0:4 * HD].rearrange("p (a b) -> p a b", a=4)).then_inc(S["rh_sb"], 1)
                if s + 1 < NS:
                    mask(s + 1)
                dve.wait_ge(S["rs_ps"], s + 1)
                v.link(nc.vector.tensor_tensor(Sn, Sm, ps[:, 7, :].rearrange("p (a b c) -> p a b c", a=4, b=2), ALU.add))
                dve.wait_ge(S["y_ps"], s + 1)
                to = Sfin if s == 1 else Sm
                for dr in range(2):
                    q = slice(2 * dr, 2 * dr + 2)
                    v.add(nc.vector.tensor_tensor(to[:, q], Sn[:, q], Gb[:, q, chunks[dr], :].rearrange("p a (b o) -> p a b o", o=1)
                                                  .to_broadcast([P, 2, 2, HD]), ALU.mult))
                v.join()
                if s == 1:
                    v.link(nc.vector.tensor_copy(Sm, S0b))
                    dve.sem_inc(S["rw_sfin"], 1)
                dve.sem_inc(S["sm"], 1)
                for dr in range(2):
                    dst = ys[:, chunks[dr], :]
                    src = ps[LO, 5, dr * 4 * HD:(dr + 1) * 4 * HD]
                    if first[s]:
                        v.add(nc.vector.tensor_copy(dst, src))
                    else:
                        v.add(nc.vector.tensor_tensor(dst, dst, src, ALU.add))
                v.join()
                dve.sem_inc(S["y_ev"], 1)
            yv = ys.rearrange("p c (h v) -> p (c h) v", v=HD)
            col3 = lambda a: a.rearrange("p (n o) -> p n o", o=1).to_broadcast([C, NCH * HH, HD])
            row3 = lambda i: e.prow[LO, i:i + 1, :].to_broadcast([C, NCH, HH * HD])
            v.link(nc.vector.reduce_sum(mu, yv, AX))
            v.link(nc.vector.tensor_scalar(mu, mu, 1.0 / HD, None, ALU.mult))
            v.link(nc.vector.tensor_tensor(yv, yv, col3(mu), ALU.subtract))
            dve.sem_inc(S["gn_c"], 1)
            dve.wait_ge(S["gn_sq"], 1)
            v.link(nc.vector.reduce_sum(rs, sq.rearrange("p (n v) -> p n v", v=HD), AX))
            dve.sem_inc(S["gn_var"], 1)
            dve.wait_ge(S["gn_rt"], 1)
            v.link(nc.vector.reciprocal(rs, rs))
            v.link(nc.vector.tensor_tensor(yv, yv, col3(rs), ALU.mult))
            v.link(nc.vector.tensor_tensor(ys, ys, row3(2), ALU.mult))
            v.link(nc.vector.tensor_tensor(ys, ys, row3(3), ALU.add))
            dve.wait_ge(S["bo_ps"], 1)
            v.link(nc.vector.tensor_copy(mu, ps[LO, 7, 0:NCH * HH]))
            Vv = Vc.rearrange("p c (h v) -> p (c h) v", v=HD)
            v.link(nc.vector.tensor_tensor(Vv, Vv, col3(mu), ALU.mult))
            v.link(nc.vector.tensor_tensor(ys, ys, Vc, ALU.add))
            dve.wait_ge(S["ga_ps"], 1)
            v.link(nc.vector.tensor_tensor(ys.rearrange("p c v -> p (c v)"), ys.rearrange("p c v -> p (c v)"),
                                           ps[LO, 0:5, :].rearrange("p a b -> p (a b)"), ALU.mult))
            dve.sem_inc(S["rw_out"], 1)
            e.done("dve", v)


def norm_steps(e, pre, src, brow, gb, y, st, src_ready, src_sem):
    nc, S, x = e.nc, e.S, e.x

    def vector(dve, v):
        dve.wait_ge(S[pre + "ld"], 32)
        for t in range(TILES):
            g = 1 if t else 0
            b = t % 2
            src_ready(dve, t)
            if t >= 2:
                dve.wait_ge(S[pre + "xn"], t - 1)
            for n in range(2):
                m = nc.vector.tensor_tensor(y[:, b, n * 512:(n + 1) * 512], src(t, n), brow[:, g, n * 512:(n + 1) * 512], ALU.mult)
                v.add(m)
            v.join()
            if src_sem:
                dve.sem_inc(S[src_sem], 1)
            v.link(nc.vector.scalar_tensor_tensor(y[:, b, :], x[:, t, :], ALPHA, y[:, b, :], ALU.mult, ALU.add))
            for n in range(2):
                v.add(nc.vector.bn_stats(st[:, t, 6 * n:6 * n + 6], y[:, b, n * 512:(n + 1) * 512]))
            v.join()
            v.link(nc.vector.bn_aggr(st[:, t, 12:14], st[:, t, 0:12]))
            dve.sem_inc(S[pre + "var"], 1)
            dve.wait_ge(S[pre + "sd"], t + 1)
            v.link(nc.vector.reciprocal(st[:, t, 14:15], st[:, t, 14:15]))
            v.link(nc.vector.tensor_scalar(st[:, t, 15:16], st[:, t, 12:13], st[:, t, 14:15], -1.0, ALU.mult, ALU.mult))
            dve.sem_inc(S[pre + "nm"], 1)

    def scalar(act):
        for t in range(TILES):
            act.wait_ge(S[pre + "var"], t + 1)
            nc.scalar.activation(st[:, t, 14:15], st[:, t, 13:14], ACT.Sqrt, bias=e.eps[:, 1:2]).then_inc(S[pre + "sd"], 1)
            act.wait_ge(S[pre + "nm"], t + 1)
            nc.scalar.activation(x[:, t, :], y[:, t % 2, :], ACT.Identity, bias=st[:, t, 15:16], scale=st[:, t, 14:15]
                                 ).then_inc(S[pre + "xn"], 1)

    def pool(pl, c):
        pl.wait_ge(S[pre + "ld"], 32)
        for t in range(TILES):
            pl.wait_ge(S[pre + "xn"], t + 1)
            c.link(nc.gpsimd.tensor_tensor(x[:, t, :], x[:, t, :], gb[:, 0, :], ALU.mult))
            nc.gpsimd.tensor_tensor(x[:, t, :], x[:, t, :], gb[:, 1, :], ALU.add).then_inc(S[pre + "x"], 1)

    def loads(sp, which):
        d, l = e.d, e.l
        for g in range(2):
            sp.dma_start(brow[:, g, :], e.mod_d[g, 2 + 3 * which].rearrange("k p -> (k p)").rearrange("(o n) -> o n", o=1)
                         .to_broadcast([P, DM])).then_inc(S[pre + "ldg"], 16)
        sp.dma_start(gb[:, 0, :], d["ln_g"][l, which].rearrange("(o n) -> o n", o=1).to_broadcast([P, DM])).then_inc(S[pre + "ldg"], 16)
        sp.dma_start(gb[:, 1, :], d["ln_b"][l, which].rearrange("(o n) -> o n", o=1).to_broadcast([P, DM])).then_inc(S[pre + "ldg"], 16)
        sp.wait_ge(S[pre + "ldg"], 64)
        sp.sem_inc(S[pre + "ld"], 32)

    return vector, scalar, pool, loads


OUTPUT_SEMS = (
    "n1x", "op_ps", "op_ev", "st_x", "n1ld", "n1ldg", "n1var", "n1sd", "n1nm", "n1xn", "ld_wo0", "ld_wo1",
)


def phase_output(e):
    nc, d, l, S, ps = e.nc, e.d, e.l, e.S, e.ps
    z = e.a0
    wo, z = e.part(z, 2, KD, 512)
    brow, z = e.part(z, 2, DM)
    gb, z = e.part(z, 2, DM)
    y, z = e.part(z, 2, DM)
    st, z = e.part(z, TILES, 16)

    def ready(dve, t):
        dve.wait_ge(S["op_ps"], 2 * t + 2)

    vector, scalar, pool, loads = norm_steps(
        e, "n1", lambda t, n: ps[:, 2 * (t % 4) + n, :], brow, gb, y, st, ready, "op_ev")
    with nc.Block() as block:
        @block.sync
        def _(sp):
            e.clear_last(sp)
            for n in range(2):
                sp.dma_start(wo[:, n], d["w_out"][l].rearrange("(k p) n -> p k n", p=P)[:, :, n * 512:(n + 1) * 512]
                             ).then_inc(S[f"ld_wo{n}"], 16)
            loads(sp, 0)
            for t in range(TILES):
                sp.wait_ge(S["n1x"], t + 1)
                sp.dma_start(e.h2_d[t * P:(t + 1) * P, :], e.x[:, t, :]).then_inc(S["st_x"], 16)
            sp.wait_ge(S["st_x"], 16 * TILES)

        @block.tensor
        def _(pe):
            for t in range(TILES):
                if t >= 4:
                    pe.wait_ge(S["op_ev"], t - 3)
                for n in range(2):
                    if t == 0:
                        pe.wait_ge(S[f"ld_wo{n}"], 16)
                    for k in range(KD):
                        m = nc.tensor.matmul(ps[:, 2 * (t % 4) + n, :], e.mixT[:, k, t * P:(t + 1) * P], wo[:, n, k, :],
                                             start=k == 0, stop=k == KD - 1)
                    m.then_inc(S["op_ps"], 1)

        @block.vector
        def _(dve):
            v = e.chain("dve", dve)
            vector(dve, v)
            e.done("dve", v)

        @block.scalar
        def _(act):
            scalar(act)

        @block.gpsimd
        def _(pl):
            c = e.chain("pool", pl)
            pool(pl, c)
            e.done("pool", c)


def expert_memory(e):
    z = 0
    r = {}
    r["w"], z = e.part(z, 12, 2048)
    r["yacc"], z = e.part(z, TILES, DM)
    r["xe"], z = e.part(z, 2, DM, rows=CAP)
    r["xT"], z = e.part(z, 2, KD, WIDE)
    r["hs"], z = e.part(z, 2, WIDE)
    r["hA"], z = e.part(z, KD, WIDE)
    r["hB"], z = e.part(z, KD, P)
    r["yP"], z = e.part(z, DM)
    r["yC"], z = e.part(z, DM)
    r["GP"], z = e.part(z, NSM)
    r["GC"], z = e.part(z, NPR)
    for n in ("iP", "gP", "iC", "gC"):
        r[n], z = e.part(z, NE // 2)
    r["iu"], z = e.part(z, NE, rows=CAP, dt=U32)
    r["ic"], z = e.part(z, 2, rows=CAP, dt=U32)
    r["iota"], z = e.part(z, NTOK)
    assert z <= 40600, z
    return r


ROUTE_SEMS = (
    "ld_rt", "rx_ps", "rx_act", "rx_dve", "lg_ps", "lg_c", "lg_e", "aff", "af_ps", "top", "ti_ps",
)


def phase_route(e):
    nc, d, l, S, ps = e.nc, e.d, e.l, e.S, e.ps
    mem = expert_memory(e)
    iu, iota, iP, gP, iC, gC = (mem[k] for k in ("iu", "iota", "iP", "gP", "iC", "gC"))
    hT, z = e.part(0, KD, NTOK)
    rt, z = e.part(z, KD, NE)
    lg, z = e.part(z, TILES, NE)
    mx, z = e.part(z, TILES)
    aT, z = e.part(z, NTOK, rows=NE)
    val, z = e.part(z, CAP, rows=NE)
    pos, z = e.part(z, CAP, rows=NE, dt=U32)
    pf, z = e.part(z, CAP, rows=NE)
    base, z = e.part(z, CAP, rows=NE)
    assert z <= 12 * 2048
    NG = 2 * TILES
    with nc.Block() as block:
        @block.sync
        def _(sp):
            e.clear_last(sp)
            sp.dma_start(rt, d["router"][l]).then_inc(S["ld_rt"], 16)
            sp.dma_start(base, d["base"]).then_inc(S["ld_rt"], 16)
            sp.dma_start(iota, d["iota"]).then_inc(S["ld_rt"], 16)
            sp.wait_ge(S["ld_rt"], 48)

        @block.tensor
        def _(pe):
            for n in range(NG):
                t, b = divmod(n, 2)
                if n >= 8:
                    pe.wait_ge(S["rx_dve" if n % 2 else "rx_act"], (n - 8) // 2 + 1)
                for k in range(4):
                    kk = 4 * b + k
                    m = nc.tensor.transpose(ps[:, n % 8, k * P:(k + 1) * P], e.x[:, t, kk * P:(kk + 1) * P], e.ident[:, :])
                m.then_inc(S["rx_ps"], 1)
            pe.wait_ge(S["rx_act"], TILES)
            pe.wait_ge(S["rx_dve"], TILES)
            pe.wait_ge(S["ld_rt"], 48)
            for t in range(TILES):
                for k in range(KD):
                    m = nc.tensor.matmul(ps[:, 0, t * NE:(t + 1) * NE], hT[:, k, t * P:(t + 1) * P], rt[:, k, :],
                                         start=k == 0, stop=k == KD - 1)
            m.then_inc(S["lg_ps"], 1)
            pe.wait_ge(S["aff"], 1)
            for t in range(TILES):
                m = nc.tensor.transpose(ps[0:NE, 1 + t // 4, (t % 4) * P:(t % 4 + 1) * P], lg[:, t, :], e.ident[:, :])
            m.then_inc(S["af_ps"], 1)
            pe.wait_ge(S["top"], 1)
            nc.tensor.transpose(ps[0:CAP, 3, 0:NE], pf, e.ident[0:NE, 0:NE])
            nc.tensor.transpose(ps[0:CAP, 3, NE:2 * NE], val, e.ident[0:NE, 0:NE]).then_inc(S["ti_ps"], 1)

        @block.scalar
        def _(act):
            for n in range(0, NG, 2):
                t, b = divmod(n, 2)
                g = 1 if t else 0
                act.wait_ge(S["rx_ps"], n + 1)
                for k in range(4):
                    kk = 4 * b + k
                    m = nc.scalar.activation(hT[:, kk, t * P:(t + 1) * P], ps[:, n % 8, k * P:(k + 1) * P], ACT.Identity,
                                             bias=e.modc[:, g, 3, kk:kk + 1], scale=e.modc[:, g, 4, kk:kk + 1])
                m.then_inc(S["rx_act"], 1)
            act.wait_ge(S["lg_c"], 1)
            nc.scalar.activation(lg, lg, ACT.Exp).then_inc(S["lg_e"], 1)

        @block.vector
        def _(dve):
            v = e.chain("dve", dve)
            for n in range(1, NG, 2):
                t, b = divmod(n, 2)
                g = 1 if t else 0
                dve.wait_ge(S["rx_ps"], n + 1)
                for k in range(4):
                    kk = 4 * b + k
                    m = nc.vector.tensor_scalar(hT[:, kk, t * P:(t + 1) * P], ps[:, n % 8, k * P:(k + 1) * P],
                                                e.modc[:, g, 4, kk:kk + 1], e.modc[:, g, 3, kk:kk + 1], ALU.mult, ALU.add)
                m.then_inc(S["rx_dve"], 1)
            dve.wait_ge(S["lg_ps"], 1)
            v.link(nc.vector.tensor_copy(lg, ps[:, 0, 0:TILES * NE].rearrange("p (a b) -> p a b", a=TILES)))
            m3 = mx.rearrange("p (n o) -> p n o", o=1).to_broadcast([P, TILES, NE])
            v.link(nc.vector.reduce_max(mx, lg, AX))
            v.link(nc.vector.tensor_tensor(lg, lg, m3, ALU.subtract))
            dve.sem_inc(S["lg_c"], 1)
            dve.wait_ge(S["lg_e"], 1)
            v.link(nc.vector.reduce_sum(mx, lg, AX))
            v.link(nc.vector.reciprocal(mx, mx))
            v.link(nc.vector.tensor_tensor(lg, lg, m3, ALU.mult))
            dve.sem_inc(S["aff"], 1)
            dve.wait_ge(S["af_ps"], 1)
            v.link(nc.vector.tensor_copy(aT, ps[0:NE, 1:3, :].rearrange("p a b -> p (a b)")[:, 0:NTOK]))
            for c0, c1, k0, k1 in ((NPR, NTOK, 0, CAPS), (0, NPR, CAPS, CAP)):
                for k in range(k0, k1, 8):
                    v.link(nc.vector.max(val[:, k:k + 8], aT[:, c0:c1]))
                    v.link(nc.vector.max_index(pos[:, k:k + 8], val[:, k:k + 8], aT[:, c0:c1]))
                    v.link(nc.vector.match_replace(aT[:, c0:c1], val[:, k:k + 8], aT[:, c0:c1], -1.0))
            v.link(nc.vector.tensor_copy(pf, pos))
            dve.wait_ge(S["ld_rt"], 48)
            v.link(nc.vector.tensor_tensor(pf, pf, base, ALU.add))
            dve.sem_inc(S["top"], 1)
            dve.wait_ge(S["ti_ps"], 1)
            v.add(nc.vector.tensor_copy(iu, ps[0:CAP, 3, 0:NE]))
            v.add(nc.vector.memset(iC, -1.0))
            v.link(nc.vector.memset(gC, 0.0))
            for src, dP, dC in ((ps[:, 3, 0:NE], iP, iC), (ps[:, 3, NE:2 * NE], gP, gC)):
                two = src.rearrange("p (n b) -> p b n", b=2)
                for b in range(2):
                    v.add(nc.vector.tensor_copy(dP[b * CAPS:(b + 1) * CAPS, :], two[0:CAPS, b]))
                    v.add(nc.vector.tensor_copy(dC[b * 32:b * 32 + CAPP, :], two[CAPS:CAP, b]))
            v.join()
            e.done("dve", v)


EXPERTS_SEMS = (
    "turn", "yc_sb", "gc_sb",
    "ic", "xe_used", "xt_ps", "xt_sb", "xm", "xa", "g_sb", "ye_sb", "sc_ev", "sp_ps", "he", "hs", "h_ps", "w_used",
    "ld_e0", "ld_e1", "ld_e2", "ld_e3", "ld_f0", "ld_f1", "ld_f2", "ld_f3",
)


def phase_experts(e):
    nc, d, l, S, ps = e.nc, e.d, e.l, e.S, e.ps
    mem = expert_memory(e)
    w, yacc, xe, xT, hs, hA, hB, yP, yC, GP, GC, iP, gP, iC, gC, iu, ic, iota = (mem[k] for k in (
        "w", "yacc", "xe", "xT", "hs", "hA", "hB", "yP", "yC", "GP", "GC", "iP", "gP", "iC", "gC", "iu", "ic", "iota"))
    w13 = w[:, 0:8, :].rearrange("p s (k n) -> p s k n", k=KD)
    w2 = w[:, 8:12, :].rearrange("p s (k n) -> p s k n", k=2)
    NI = NE // 2
    hT = (hA, hB[:, :, P - WIDE:])
    rows = (hA[:, :, 0:CAP], hB)
    blocks = [(t, h) for t in range(1, TILES) for h in range(2)] + [(0, 0), (0, 1)]

    with nc.Block() as block:
        @block.sync
        def _(sp):
            e.clear_last(sp)

            def load(x, j, second):
                if not second:
                    for a, name in enumerate(("ex_w1", "ex_w3")):
                        sp.dma_start(w13[:, 4 * a + j], d[name][l, x].rearrange("(k p) n -> p k n", p=P)[:, :, j * 256:(j + 1) * 256]
                                     ).then_inc(S[f"ld_e{j}"], 16)
                else:
                    sp.dma_start(w2[:, j], d["ex_w2"][l, x, j * 256:(j + 1) * 256].rearrange("(k p) n -> p k n", p=P)
                                 ).then_inc(S[f"ld_f{j}"], 16)

            for second in range(2):
                for j in range(4):
                    load(0, j, second)
            with sp.Fori(1, NE) as x:
                for second in range(2):
                    for j in range(4):
                        if second:
                            sp.wait_ge(S["w_used"], x * 4 + (j + 1 - 4))
                        else:
                            sp.wait_ge(S["h_ps"], x * 8 + (2 * j + 2 - 8))
                        load(x, j, second)

        @block.gpsimd
        def _(pool):
            with pool.Fori(0, NI) as i:
                for b in range(2):
                    pool.wait_ge(S["xe_used"], i * 2 + (b + 1))
                    pool.sem_inc(S["turn"], 1)
                    nc.gpsimd.tensor_copy(ic[:, b:b + 1], iu[:, bass.ds(i * 2 + b, 1)]).then_inc(S["ic"], 1)
                    pool.wait_ge(S["ic"], i * 2 + (b + 1))
                    pool.sem_inc(S["turn"], 1)
                    nc.gpsimd.indirect_dma_start(xe[:, b, :], None, e.h2_d, bass.IndirectOffsetOnAxis(ap=ic[:, b:b + 1], axis=0)
                                                 ).then_inc(S[f"ld_x{b}"], 16)
            pool.wait_ge(S["xe_used"], NE + 1)
            nc.gpsimd.indirect_dma_start(xe[:, 0, :], None, e.h2_d, bass.IndirectOffsetOnAxis(ap=ic[:, 0:1], axis=0)
                                         ).then_inc(S["ld_x0"], 16)

        @block.tensor
        def _(pe):
            def turn_tokens(i, b, at):
                pe.wait_ge(S[f"ld_x{b}"], l * (16 * (NI + 1 - b)) + (i * 16 + 16))
                pe.wait_ge(S["xe_used"], at + 2)
                for k in range(KD):
                    m = nc.tensor.transpose(ps[:, k // 4, (k % 4) * CAP:(k % 4 + 1) * CAP], xe[:, b, k * P:(k + 1) * P],
                                            e.ident[0:CAP, 0:CAP])
                m.then_inc(S["xt_ps"], 1)

            def scatter(i):
                pe.wait_ge(S["ye_sb"], i * 2 + 2)
                pe.wait_ge(S["g_sb"], i + 1)
                for k, (t, h) in enumerate(blocks):
                    pe.wait_ge(S["sc_ev"], i * 10 + (k + 1))
                    if t:
                        m = nc.tensor.matmul(ps[:, 6 + h, :], GP[:, (t - 1) * P:t * P], yP[:, h * 512:(h + 1) * 512],
                                             start=True, stop=True)
                    else:
                        m = nc.tensor.matmul(ps[:, 6 + h, :], GC, yC[:, h * 512:(h + 1) * 512], start=True, stop=True)
                    m.then_inc(S["sp_ps"], 1)

            turn_tokens(0, 0, 0)
            with pe.Fori(0, NI) as i:
                for b in range(2):
                    x = i * 2 + b
                    for f in range(KD):
                        j = f // 2
                        if f % 2 == 0:
                            pe.wait_ge(S[f"ld_e{j}"], x * 32 + 32)
                        if f == 0:
                            pe.wait_ge(S["xt_sb"], x + 1)
                        pe.wait_ge(S["he"], x * 8 + (f + 1))
                        for a in range(2):
                            for k in range(KD):
                                m = nc.tensor.matmul(ps[:, 2 + f % 2, a * WIDE:(a + 1) * WIDE],
                                                     w13[:, 4 * a + j, k, (f % 2) * P:(f % 2 + 1) * P],
                                                     xT[:, b, k, :], start=k == 0, stop=k == KD - 1)
                        m.then_inc(S["h_ps"], 1)
                        if b == 0 and f == 3:
                            turn_tokens(i, 1, i * 2 + 1)
                    if b == 0:
                        scatter(i)
                    else:
                        turn_tokens(i + 1, 0, i * 2 + 2)
                    pe.wait_ge(S["he"], x * 8 + 10)
                    if b == 1:
                        pe.wait_ge(S["ye_sb"], i * 2 + 3)
                    for f in range(KD):
                        if f % 2 == 0:
                            pe.wait_ge(S[f"ld_f{f // 2}"], x * 16 + 16)
                        for h in range(2):
                            r = rows[b]
                            m = nc.tensor.matmul(ps[0:CAP if b == 0 else P, 4 + h, :], r[:, f, :],
                                                 w2[:, f // 2, f % 2, h * 512:(h + 1) * 512], start=f == 0, stop=f == KD - 1)
                        if f % 2:
                            m.then_inc(S["w_used"], 1)
            scatter(NI)

        @block.scalar
        def _(act):
            with act.Fori(0, NI) as i:
                for b in range(2):
                    x = i * 2 + b
                    for f in range(KD):
                        act.wait_ge(S["h_ps"], x * 8 + (f + 1))
                        act.wait_ge(S["he"], x * 8 + (f + 1))
                        nc.scalar.activation(hs[:, f % 2, :], ps[:, 2 + f % 2, 0:WIDE], ACT.Silu).then_inc(S["hs"], 1)
                    act.wait_ge(S["w_used"], x * 4 + 4)
                    if b == 0:
                        act.wait_ge(S["sp_ps"], i * 10 + 10)
                    yes = ps[:, 4:6, :].rearrange("p a b -> p (a b)")
                    c0, p0 = (CAPS, 0) if b == 0 else (32, CAPS)
                    nc.scalar.activation(yC[b * 32:b * 32 + CAPP, :], yes[c0:c0 + CAPP, :], ACT.Copy).then_inc(S["yc_sb"], 1)
                    nc.scalar.activation(yP[p0:p0 + CAPS, :], yes[p0:p0 + CAPS, :], ACT.Copy).then_inc(S["ye_sb"], 1)

        @block.vector
        def _(dve):
            v = e.chain("dve", dve)
            v.add(nc.vector.memset(yacc, 0.0))
            for a in (yP, yC, GP, GC, xT[:, :, :, :].rearrange("p a b c -> p (a b c)"), hB.rearrange("p a b -> p (a b)")):
                v.add(nc.vector.memset(a, 0.0))
            v.join()
            for name, n in (("ye_sb", 2), ("g_sb", 1), ("sc_ev", 2), ("he", 2), ("xe_used", 2)):
                dve.sem_inc(S[name], n)

            def tokens(b, at):
                dve.wait_ge(S["xt_ps"], at + 1)
                for c0, c1, to, g in ORDER[b]:
                    for q in range(2):
                        sc = e.modc[:, g, 4, 4 * q:4 * q + 4].rearrange("p (n o) -> p n o", o=1).to_broadcast([P, 4, c1 - c0])
                        nc.vector.tensor_tensor(xT[:, b, 4 * q:4 * q + 4, to:to + c1 - c0],
                                                ps[:, q, 0:4 * CAP].rearrange("p (a b) -> p a b", a=4)[:, :, c0:c1],
                                                sc, ALU.mult).then_inc(S["xm"], 1)
                dve.wait_ge(S["xm"], at * 4 + 4)
                dve.sem_inc(S["xe_used"], 1)
                for c0, c1, to, g in ORDER[b]:
                    sh = e.modc[:, g, 3, :].rearrange("p (n o) -> p n o", o=1).to_broadcast([P, KD, c1 - c0])
                    nc.vector.tensor_tensor(xT[:, b, :, to:to + c1 - c0], xT[:, b, :, to:to + c1 - c0], sh, ALU.add
                                            ).then_inc(S["xa"], 1)
                dve.wait_ge(S["xa"], at * 2 + 2)
                dve.sem_inc(S["xt_sb"], 1)

            def add(i):
                for k, (t, h) in enumerate(blocks):
                    dve.wait_ge(S["sp_ps"], i * 10 + (k + 1))
                    nc.vector.tensor_tensor(yacc[:, t, h * 512:(h + 1) * 512], yacc[:, t, h * 512:(h + 1) * 512], ps[:, 6 + h, :],
                                            ALU.add).then_inc(S["sc_ev"], 1)

            tokens(0, 0)
            with dve.Fori(0, NI) as i:
                for b in range(2):
                    x = i * 2 + b
                    for f in range(KD):
                        dve.wait_ge(S["hs"], x * 8 + (f + 1))
                        nc.vector.tensor_tensor(hT[b][:, f, :], hs[:, f % 2, :], ps[:, 2 + f % 2, WIDE:2 * WIDE], ALU.mult
                                                ).then_inc(S["he"], 1)
                        if b == 0 and f == 3:
                            tokens(1, i * 2 + 1)
                    if b == 0:
                        add(i)
                        nc.vector.tensor_scalar(GC, iota[:, 0:NPR], iC[:, bass.ds(i, 1)], gC[:, bass.ds(i, 1)],
                                                ALU.is_equal, ALU.mult).then_inc(S["gc_sb"], 1)
                        nc.vector.tensor_scalar(GP, iota[:, NPR:], iP[:, bass.ds(i, 1)], gP[:, bass.ds(i, 1)],
                                                ALU.is_equal, ALU.mult).then_inc(S["g_sb"], 1)
                    else:
                        tokens(0, i * 2 + 2)
            add(NI)
            e.done("dve", v)


NORM2_SEMS = (
    "n2ld", "n2ldg", "n2var", "n2sd", "n2nm", "n2xn", "n2x",
)


def phase_norm2(e):
    nc, S = e.nc, e.S
    yacc = expert_memory(e)["yacc"]
    brow, z = e.part(0, 2, DM)
    gb, z = e.part(z, 2, DM)
    y, z = e.part(z, 2, DM)
    st, z = e.part(z, TILES, 16)
    vector, scalar, pool, loads = norm_steps(
        e, "n2", lambda t, n: yacc[:, t, n * 512:(n + 1) * 512], brow, gb, y, st, lambda dve, t: None, None)
    with nc.Block() as block:
        @block.sync
        def _(sp):
            e.clear_last(sp)
            loads(sp, 1)

        @block.vector
        def _(dve):
            v = e.chain("dve", dve)
            vector(dve, v)
            e.done("dve", v)

        @block.scalar
        def _(act):
            scalar(act)

        @block.gpsimd
        def _(pl):
            c = e.chain("pool", pl)
            pool(pl, c)
            e.done("pool", c)


PHASES = [
    (phase_modulation, MODULATION_SEMS), (phase_project, PROJECT_SEMS), (phase_attention, ATTENTION_SEMS),
    (phase_hgrn, HGRN_SEMS), (phase_rwkv, RWKV_SEMS), (phase_output, OUTPUT_SEMS), (phase_route, ROUTE_SEMS),
    (phase_experts, EXPERTS_SEMS), (phase_norm2, NORM2_SEMS),
]


def kernel(**inputs):
    import numpy as _np
    import concourse.bacc as _bacc
    from concourse import mybir as _mybir
    from concourse.bass_utils import run_bass_kernel_spmd as _run

    nc = _bacc.Bacc("TRN2", target_bir_lowering=False, num_devices=1)
    arrays, d, o = {}, {}, {}
    for name, a in layout(inputs).items():
        arrays[f"in_{name}"] = a
        d[name] = nc.dram_tensor(f"in_{name}", a.shape, _mybir.dt.from_np(a.dtype), kind="ExternalInput").ap()
    for name, shape in OUTS:
        o[name] = nc.dram_tensor(f"out_{name}", shape, _mybir.dt.float32, kind="ExternalOutput").ap()
    program(nc, d, o)
    r = _run(nc, [arrays], core_ids=[0])
    return tuple(r.results[0][f"out_{name}"] for name, _ in OUTS)
```

```python
from contextlib import ExitStack

import numpy as np
import concourse.bass as bass
from concourse import mybir

F32 = mybir.dt.float32
U32 = mybir.dt.uint32
ALU = mybir.AluOpType
ACT = mybir.ActivationFunctionType
AX = mybir.AxisListType.X

P = 128
DEPTH, DM, NPR, NSM = 2, 1024, 128, 512
NTOK = NPR + NSM
TILES = NTOK // P
KD = DM // P
PAST = 256
GRID_W = 64
NH, NOPE, ROPE, DV = 8, 64, 32, 64
QK = NOPE + ROPE
QR, KVR = 384, 256
MLA_COLS = QR + KVR + ROPE
HH, HD = 4, 64
HG0 = MLA_COLS
RW0 = HG0 + 5 * HH * HD
NRW = 9
NE, FF = 16, 1024
CAPS, CAPP = 2 * NSM // NE, 2 * NPR // NE
CAP = CAPS + CAPP
WIDE = 96
ORDER = (((0, CAPS, 0, 1), (CAPS, CAP, CAPS, 0)), ((0, CAPS, WIDE - CAPS, 1), (CAPS, CAP, 0, 0)))
C = 64
NCH = NTOK // C
ARENA = 40600
LV = 7
ALPHA = float((2 * DEPTH) ** 0.25)
SCALE = float(QK) ** -0.5
PAD = NTOK + 3
TOKC = MLA_COLS + HH * HD
HGT = 6
WRING = 6


def pad_at(n):
    return n + 1 + (n >= NPR)


def constants():
    i = np.arange(P)
    s, t = i[:, None], i[None, :]
    m = np.zeros((2, LV + 1, P, P), np.float32)
    m[:, 0] = np.eye(P)
    for j in range(LV):
        h = 1 << j
        same = s // (2 * h) == t // (2 * h)
        m[0, j + 1] = same & (s % (2 * h) < h) & (t % (2 * h) >= h)
        m[1, j + 1] = m[0, j + 1].T
    hgm = m.transpose(2, 0, 1, 3).reshape(P, 2 * (LV + 1) * P)
    far = [[i[(i % (2 << j) >= 1 << j) != (d == 1)] for j in range(LV)] for d in range(2)]
    hgf = np.stack([np.concatenate([m[d, 0]] + [m[d, j + 1][:, far[d][j]] for j in range(LV)], 1) for d in range(2)], 1)
    rwm = np.zeros((P, 2, P), np.float32)
    a, b = np.arange(C)[:, None], np.arange(C)[None, :]
    for d in range(2):
        strict, incl = ((a < b), (a <= b)) if d == 0 else ((a > b), (a >= b))
        for r in range(2):
            rwm[r * C:(r + 1) * C, d, :C] = strict
            rwm[r * C:(r + 1) * C, d, C:] = incl
    bds = m[:, 1:7].sum(1).transpose(2, 0, 1)
    blk = (s // C == t // C).astype(np.float32)
    quarter = ROPE // 4
    pos = np.stack([np.arange(NSM) // GRID_W, np.arange(NSM) % GRID_W], -1).astype(np.float32)
    inv = (np.float32(10000.0) ** (-np.arange(quarter, dtype=np.float32) / np.float32(quarter))).astype(np.float32)
    ang = pos[:, :, None] * inv
    rope = np.zeros((QK, 2, NSM), np.float32)
    rope[:NOPE, 0] = 1.0
    rot = np.zeros((QK, ROPE), np.float32)
    for ax in range(2):
        for half in range(2):
            for q in range(quarter):
                c = ax * 2 * quarter + half * quarter + q
                rope[NOPE + c, 0] = np.cos(ang[:, ax, q])
                rope[NOPE + c, 1] = np.sin(ang[:, ax, q])
                o = ax * 2 * quarter + (1 - half) * quarter + q
                rot[NOPE + o, c] = 1.0 if half else -1.0
    reset = np.ones((P, 2, NTOK), np.float32)
    reset[:, 0, 0::C] = 0
    reset[:, 1, C - 1::C] = 0
    iota = np.broadcast_to(np.arange(NTOK, dtype=np.float32), (P, NTOK))
    base = np.broadcast_to(np.where(np.arange(CAP) < CAPS, NPR, 0).astype(np.float32), (NE, CAP))
    return {
        "ident": np.eye(P, dtype=np.float32), "hgm": hgm, "hgf": hgf, "rwm": rwm.reshape(P, -1), "bds": bds.reshape(P, -1),
        "blk": blk, "rope": rope.reshape(QK, -1), "rot": rot, "reset": reset.reshape(P, -1), "iota": iota,
        "base": base,
    }


PC = {}
_n = 0
for _name, _w in (("qn", 3), ("mu0", 9), ("mu1", 9), ("w0", 4), ("a0", 4), ("kk", 2), ("ka", 2), ("rk", 2),
                   ("hn", 2)):
    PC[_name] = _n
    _n += _w
NPC = _n


def layout(i):
    f = lambda n: np.asarray(i[n])
    cols = lambda a: a.reshape(DEPTH, -1, P).transpose(0, 2, 1)
    w = f("w_in").reshape(DEPTH, KD, P, -1)
    tch = [HG0 + P * n for n in (0, 1)] + [HG0 + 2 * HH * HD + P * n for n in range(4)] + [RW0 + P * n for n in range(NRW)]
    tch += [HG0 + 4 * HH * HD + P * n for n in (0, 1)]
    w_t = np.stack([w[:, :, :, c:c + P] for c in tch], 1).transpose(0, 1, 3, 2, 4)
    tok = np.concatenate([w[..., :MLA_COLS], w[..., HG0 + 256:HG0 + 512]], -1)
    ukv = f("mla_w_ukv").reshape(DEPTH, 2, P, NH, 2, NOPE)
    out = {
        "x": np.concatenate([f("x_prompt").reshape(NPR, DM), f("x_sample").reshape(NSM, DM)], 0),
        "cvec": np.stack([f("c_ctx").reshape(KD, P), f("c").reshape(KD, P)], -1).transpose(1, 0, 2),
        "ada_w": f("ada_w"), "ada_b": f("ada_b"),
        "w_t": w_t, "w_tok": tok.transpose(0, 2, 1, 3),
        "w_uq": f("mla_w_uq").reshape(DEPTH, 3, P, NH * QK).transpose(0, 2, 1, 3),
        "w_uk": ukv[..., 0, :].reshape(DEPTH, 2, P, NH * NOPE).transpose(0, 2, 1, 3),
        "w_uv": ukv[..., 1, :].reshape(DEPTH, 2, P, NH * DV).transpose(0, 2, 1, 3),
        "c_ckv": f("cache_ckv").reshape(DEPTH, PAST, KVR), "c_kr": f("cache_krope").reshape(DEPTH, PAST, ROPE),
        "lb": f("hg_lb_logits").reshape(DEPTH * 4, P).T,
        "pcol": np.concatenate([cols(f(n)) for n in
                                ("mla_q_norm",)] + [cols(f("rw_mu")[:, 0]), cols(f("rw_mu")[:, 1])] +
                               [cols(f(n)) for n in ("rw_w0", "rw_a0", "rw_k_k", "rw_k_a", "rw_r_k", "hg_norm")], -1),
        "prow": np.concatenate([f(n) for n in ("mla_kv_norm", "rw_gn_w", "rw_gn_b")], -1),
        "w_wa": np.stack([f("rw_w2"), f("rw_a2")], 1).reshape(DEPTH, 2, P, HH * HD).transpose(0, 2, 1, 3),
        "w_g2": f("rw_g2"),
        "s_hg": f("state_hgrn").reshape(DEPTH, 2, 2, P, HD),
        "s_rw": f("state_rwkv").reshape(DEPTH, 2, HH, HD, HD).transpose(0, 1, 2, 4, 3).reshape(DEPTH, 2, 2, P, HD),
        "w_out": f("w_out"), "ln_g": f("ln_g"), "ln_b": f("ln_b"),
        "router": f("router").reshape(DEPTH, KD, P, NE).transpose(0, 2, 1, 3),
        "ex_w1": f("ex_w1"), "ex_w3": f("ex_w3"), "ex_w2": f("ex_w2"),
    }
    out.update(constants())
    return {k: np.ascontiguousarray(v) for k, v in out.items()}


OUTS = [("y_p", (1, NPR, DM)), ("y_s", (1, NSM, DM)), ("n_ckv", (1, DEPTH, NPR, KVR)), ("n_kr", (1, DEPTH, NPR, ROPE)),
        ("n_hg", (1, DEPTH, 2, HH, HD, HD)), ("n_rw", (1, DEPTH, 2, HH, HD, HD))]


class Shared:
    pass


class Chain:

    def __init__(self, eng, sem, at=0):
        self.eng, self.sem, self.n = eng, sem, at

    def add(self, ins):
        self.n += 1
        ins.then_inc(self.sem, 1)
        return self.n

    def join(self):
        self.eng.wait_ge(self.sem, self.n)

    def link(self, ins):
        self.add(ins)
        self.join()


def program(nc, d, o, taps=(), depth=DEPTH, stop=99):
    ctx = ExitStack()
    used = []
    with ctx:
        def sb(name, shape, dt=F32):
            return ctx.enter_context(nc.sbuf_tensor(name, shape, dt))

        def sem(name):
            s = ctx.enter_context(nc.semaphore(name))
            used.append(s)
            return s

        x = sb("x_sb", [P, TILES, DM])
        ident = sb("ident_sb", [P, P])
        hgm = sb("hgm_sb", [P, 2, (LV + 1) * P])
        rwm = sb("rwm_sb", [P, 2, P])
        bds = sb("bds_sb", [P, 2, P])
        blk = sb("blk_sb", [P, P])
        rope = sb("rope_sb", [QK, 2, NSM])
        rot = sb("rot_sb", [QK, ROPE])
        reset = sb("reset_sb", [P, 2, NTOK])
        scT = sb("scT", [P, KD, 2])
        lball = sb("lball", [P, DEPTH, 4])
        lb = sb("lb_sb", [P, 4])
        oml = sb("oml", [P, 4])
        modc = sb("modc", [P, 2, 6, KD])
        pcol = sb("pcol_sb", [P, NPC])
        prow = sb("prow_sb", [P, 3, 256])
        eps = sb("eps_sb", [P, 3])
        arena = sb("arena", [P, ARENA])
        ps = ctx.enter_context(nc.psum_tensor("ps", [P, 8, 512], F32))
        mod_d = nc.dram_tensor("mod_d", (2, 6, KD, P), F32, kind="Internal").ap()
        h2_d = nc.dram_tensor("h2_d", (NTOK, DM), F32, kind="Internal").ap()

        def part(at, *shape, rows=P, dt=F32):
            n = int(np.prod(shape))
            v = arena[0:rows, at:at + n]
            if dt != F32:
                v = v.bitcast(dt)
            if len(shape) > 1:
                names = "abcdef"[:len(shape)]
                v = v.rearrange(f"p ({' '.join(names)}) -> p {' '.join(names)}", **dict(zip(names, shape)))
            return v, at + n

        hT, a0 = part(0, KD, NTOK)
        mixT = hT
        hgT, a1 = part(a0, HGT, NTOK)
        rwT, a2 = part(a1, NRW, PAD)
        tok, z = part(a2, TILES, TOKC)
        gT, FREE = part(z, 2, NTOK)

        chains = {k: sem(k + "_chain") for k in ("dve", "act", "pool", "pe")}
        count = dict.fromkeys(chains, 0)

        def chain(kind, eng):
            c = Chain(eng, chains[kind], count[kind])
            return c

        def done(kind, c):
            count[kind] = c.n

        S = {n: sem(n) for n in ("ld_const", "tap", "st_y")}
        S.update({n: ctx.enter_context(nc.semaphore(n)) for n in ("ld_x0", "ld_x1") + EXPERT_WEIGHT_SEMS})

        with nc.Block() as block:
            cv, z = part(0, KD, 2)
            lg, z = part(z, DEPTH, 4)
            tmp, z = part(z, 8, 4)

            @block.sync
            def _(sp):
                for dst, src in ((ident, "ident"), (blk, "blk"), (rot, "rot")):
                    sp.dma_start(dst[:, :], d[src]).then_inc(S["ld_const"], 16)
                sp.dma_start(hgm[:, :, :].rearrange("p a b -> p (a b)"), d["hgm"]).then_inc(S["ld_const"], 16)
                sp.dma_start(rwm[:, :, :].rearrange("p a b -> p (a b)"), d["rwm"]).then_inc(S["ld_const"], 16)
                sp.dma_start(bds[:, :, :].rearrange("p a b -> p (a b)"), d["bds"]).then_inc(S["ld_const"], 16)
                sp.dma_start(rope[:, :, :].rearrange("p a b -> p (a b)"), d["rope"]).then_inc(S["ld_const"], 16)
                sp.dma_start(reset[:, :, :].rearrange("p a b -> p (a b)"), d["reset"]).then_inc(S["ld_const"], 16)
                sp.dma_start(cv, d["cvec"]).then_inc(S["ld_const"], 16)
                sp.dma_start(lg.rearrange("p a b -> p (a b)"), d["lb"]).then_inc(S["ld_const"], 16)
                sp.dma_start(x[:, :, :], d["x"].rearrange("(t p) n -> p t n", p=P)).then_inc(S["ld_const"], 16)
                sp.wait_ge(S["ld_const"], 16 * 11)

            @block.scalar
            def _(act):
                a = chain("act", act)
                act.wait_ge(S["ld_const"], 176)
                a.add(nc.scalar.activation(scT[:, :, :], cv, ACT.Silu))
                act.wait_ge(chains["dve"], 2)
                a.link(nc.scalar.activation(tmp[:, 1:1 + DEPTH, :], tmp[:, 4:4 + DEPTH, :], ACT.Exp))
                done("act", a)

            @block.vector
            def _(dve):
                v = chain("dve", dve)
                dve.wait_ge(S["ld_const"], 176)
                v.link(nc.vector.tensor_tensor(tmp[:, 0, :], lg[:, 0, :], lg[:, 1, :], ALU.max))
                v.link(nc.vector.tensor_tensor(tmp[:, 4:4 + DEPTH, :], lg, tmp[:, 0:1, :].to_broadcast([P, DEPTH, 4]),
                                               ALU.subtract))
                dve.wait_ge(chains["act"], 2)
                v.link(nc.vector.tensor_tensor(tmp[:, 3, :], tmp[:, 1, :], tmp[:, 2, :], ALU.add))
                v.link(nc.vector.reciprocal(tmp[:, 3, :], tmp[:, 3, :]))
                v.link(nc.vector.tensor_tensor(tmp[:, 1:1 + DEPTH, :], tmp[:, 1:1 + DEPTH, :],
                                               tmp[:, 3:4, :].to_broadcast([P, DEPTH, 4]), ALU.mult))
                v.link(nc.vector.tensor_tensor(tmp[:, 6, :], tmp[:, 1, :], tmp[:, 1, :], ALU.subtract))
                v.link(nc.vector.tensor_scalar(lball[:, 0, :], tmp[:, 6, :], 0.0, None, ALU.max))
                v.link(nc.vector.tensor_tensor(tmp[:, 7, :], tmp[:, 1, :], tmp[:, 2, :], ALU.add))
                v.link(nc.vector.tensor_tensor(tmp[:, 7, :], tmp[:, 7, :], tmp[:, 1, :], ALU.subtract))
                v.link(nc.vector.tensor_scalar(lball[:, 1, :], tmp[:, 7, :], 0.0, None, ALU.max))
                v.add(nc.vector.memset(eps[:, 0:1], 1e-6))
                v.add(nc.vector.memset(eps[:, 1:2], 1e-5))
                v.link(nc.vector.memset(eps[:, 2:3], 64e-5))
                done("dve", v)

        def clear_all():
            nc.all_engine_barrier()
            with nc.Block() as block:
                @block.sync
                def _(sp):
                    for s in used:
                        sp.sem_clear(s)
            nc.all_engine_barrier()
            for k in count:
                count[k] = 0

        e = Shared()
        e.nc, e.d, e.o, e.x, e.ident, e.hgm = nc, d, o, x, ident, hgm
        e.rwm, e.bds, e.blk, e.rope, e.rot, e.reset = rwm, bds, blk, rope, rot, reset
        e.scT, e.lball, e.lb, e.oml, e.modc, e.pcol = scT, lball, lb, oml, modc, pcol
        e.prow, e.eps, e.ps, e.mod_d, e.h2_d, e.part = prow, eps, ps, mod_d, h2_d, part
        e.hT, e.mixT, e.hgT, e.rwT, e.tok, e.gT, e.a0 = hT, mixT, hgT, rwT, tok, gT, a0
        e.a1, e.a2, e.FREE, e.chains, e.count, e.chain = a1, a2, FREE, chains, count, chain
        e.done = done
        clear_all()
        with nc.Fori(0, depth) as l:
            e.l = l
            last = []

            def clear_last(sp):
                for s in last:
                    sp.sem_clear(s)

            e.clear_last = clear_last
            for n, (f, names) in enumerate(PHASES):
                if n >= stop:
                    break
                own = {name: nc.alloc_semaphore(name=f"{name}") for name in names}
                e.S = {**S, **own}
                f(e)
                for s in last:
                    nc.release_semaphore(s)
                last[:] = own.values()
            if taps:
                with nc.Block() as block:
                    @block.sync
                    def _(sp):
                        for k, (name, f) in enumerate(taps):
                            sp.dma_start(o[name][l], f(e)).then_inc(S["tap"], 16)
                        sp.wait_ge(S["tap"], 16 * len(taps))
            used.extend(last)
            clear_all()
        with nc.Block() as block:
            @block.sync
            def _(sp):
                sp.dma_start(o["y_p"][0], x[:, 0, :]).then_inc(S["st_y"], 16)
                sp.dma_start(o["y_s"][0].rearrange("(t p) n -> p t n", p=P), x[:, 1:TILES, :]).then_inc(S["st_y"], 16)
                sp.wait_ge(S["st_y"], 32)


MODULATION_SEMS = (
    "ld_adab",
    "mod_out", "mod_in", "ada_ps", "ada_row", "modt", "ld_par", "ld_ada0", "ld_ada1", "ld_ada2", "ld_ada3",
)


def phase_modulation(e):
    nc, d, l, S = e.nc, e.d, e.l, e.S
    NB = 6 * DM // 512
    RING = 4
    slot, z = e.part(0, RING, KD, 512)
    brow, z = e.part(z, 6 * DM, rows=2)
    mrow, z = e.part(z, 6 * DM, rows=2)
    mt, z = e.part(z, P, rows=96)
    ps = e.ps
    with nc.Block() as block:
        @block.sync
        def _(sp):
            e.clear_last(sp)
            sp.dma_start(brow, d["ada_b"][l].rearrange("(o n) -> o n", o=1).to_broadcast([2, 6 * DM])).then_inc(S["ld_adab"], 16)
            for n in range(NB):
                if n >= RING:
                    sp.wait_ge(S["ada_ps"], n - RING + 1)
                sp.dma_start(slot[:, n % RING], d["ada_w"][l].rearrange("(k p) n -> p k n", p=P)[:, :, n * 512:(n + 1) * 512]
                             ).then_inc(S[f"ld_ada{n % RING}"], 16)
            sp.dma_start(e.pcol[:, :], d["pcol"][l]).then_inc(S["ld_par"], 16)
            sp.dma_start(e.prow[:, :, :].rearrange("p a b -> p (a b)"),
                         d["prow"][l].rearrange("(o n) -> o n", o=1).to_broadcast([P, 3 * 256])).then_inc(S["ld_par"], 16)
            sp.wait_ge(S["ada_row"], NB)
            sp.dma_start(e.mod_d.rearrange("g s k p -> g (s k p)"), mrow).then_inc(S["mod_out"], 16)
            sp.wait_ge(S["mod_out"], 16)
            sp.dma_start(mt, e.mod_d.rearrange("g s k p -> (g s k) p")).then_inc(S["mod_in"], 16)
            sp.wait_ge(S["ld_par"], 32)

        @block.tensor
        def _(pe):
            for n in range(NB):
                pe.wait_ge(S[f"ld_ada{n % RING}"], 16 * (n // RING + 1))
                if n >= 8:
                    pe.wait_ge(S["ada_row"], n - 7)
                for k in range(KD):
                    i = nc.tensor.matmul(ps[0:2, n % 8, :], e.scT[:, k, :], slot[:, n % RING, k, :],
                                         start=k == 0, stop=k == KD - 1)
                i.then_inc(S["ada_ps"], 1)
            pe.wait_ge(S["mod_in"], 16)
            pe.wait_ge(S["ada_row"], NB)
            nc.tensor.transpose(ps[:, 0, 0:96], mt, e.ident[0:96, 0:96]).then_inc(S["modt"], 1)

        @block.vector
        def _(dve):
            v = e.chain("dve", dve)
            dve.wait_ge(S["ld_adab"], 16)
            for n in range(NB):
                dve.wait_ge(S["ada_ps"], n + 1)
                nc.vector.tensor_tensor(mrow[:, n * 512:(n + 1) * 512], ps[0:2, n % 8, :], brow[:, n * 512:(n + 1) * 512],
                                        ALU.add).then_inc(S["ada_row"], 1)
            dve.wait_ge(S["modt"], 1)
            v.link(nc.vector.tensor_copy(e.modc[:, :, :, :].rearrange("p g s k -> p (g s k)"), ps[:, 0, 0:96]))
            for s in (1, 4):
                v.add(nc.vector.tensor_scalar(e.modc[:, :, s, :], e.modc[:, :, s, :], 1.0, None, ALU.add))
            v.link(nc.vector.tensor_copy(e.lb[:, :], e.lball[:, bass.ds(l, 1), :].rearrange("p a b -> p (a b)")))
            v.link(nc.vector.tensor_scalar(e.oml[:, :], e.lb[:, :], -1.0, 1.0, ALU.mult, ALU.add))
            e.done("dve", v)


PROJECT_SEMS = (
    "ld_tokw", "pj_ps", "pj_act", "pj_dve", "ld_wt0", "ld_wt1", "ld_wt2", "ld_wt3", "ld_wt4", "ld_wt5",
)


def phase_project(e):
    nc, d, l, S, ps = e.nc, e.d, e.l, e.S, e.ps
    tokw, z = e.part(e.FREE, KD, TOKC)
    ring, z = e.part(z, WRING, KD, P)
    NT = HGT + NRW + 2
    spans = ((0, 512), (512, MLA_COLS), (MLA_COLS, TOKC))
    groups = [("x", t, h) for t in range(TILES) for h in range(2)]
    NX = len(groups)
    groups += [("T", c, g) for c in range(NT) for g in (1, 0)]
    groups += [("tok", t, s) for t in range(TILES) for s in range(3)]

    with nc.Block() as block:
        @block.sync
        def _(sp):
            e.clear_last(sp)
            for c in range(NT):
                if c >= WRING:
                    sp.wait_ge(S["pj_ps"], NX + 2 * (c - WRING + 1))
                sp.dma_start(ring[:, c % WRING], d["w_t"][l, c]).then_inc(S[f"ld_wt{c % WRING}"], 16)
                if c == WRING - 1:
                    sp.dma_start(tokw, d["w_tok"][l]).then_inc(S["ld_tokw"], 16)

        @block.tensor
        def _(pe):
            for n, (kind, a, b) in enumerate(groups):
                if n >= 8:
                    pe.wait_ge(S["pj_dve" if n % 2 else "pj_act"], (n - 8) // 2 + 1)
                if n == NX:
                    pe.wait_ge(S["pj_act"], NX // 2)
                    pe.wait_ge(S["pj_dve"], NX // 2)
                if kind == "x":
                    for k in range(4):
                        kk = 4 * b + k
                        i = nc.tensor.transpose(ps[:, n % 8, k * P:(k + 1) * P], e.x[:, a, kk * P:(kk + 1) * P], e.ident[:, :])
                elif kind == "T":
                    pe.wait_ge(S[f"ld_wt{a % WRING}"], 16 * (a // WRING + 1))
                    c0, c1 = (NPR, NTOK) if b else (0, NPR)
                    for k in range(KD):
                        i = nc.tensor.matmul(ps[:, n % 8, 0:c1 - c0], ring[:, a % WRING, k, :], e.hT[:, k, c0:c1],
                                             start=k == 0, stop=k == KD - 1)
                else:
                    pe.wait_ge(S["ld_tokw"], 16)
                    c0, c1 = spans[b]
                    for k in range(KD):
                        i = nc.tensor.matmul(ps[:, n % 8, 0:c1 - c0], e.hT[:, k, a * P:(a + 1) * P], tokw[:, k, c0:c1],
                                             start=k == 0, stop=k == KD - 1)
                i.then_inc(S["pj_ps"], 1)

        def place(n):
            kind, a, b = groups[n]
            if kind == "T":
                c0, c1 = (NPR, NTOK) if b else (0, NPR)
                if a < HGT:
                    dst = e.hgT[:, a, c0:c1]
                elif a < HGT + NRW:
                    dst = e.rwT[:, a - HGT, pad_at(c0):pad_at(c0) + c1 - c0]
                else:
                    dst = e.gT[:, a - HGT - NRW, c0:c1]
            else:
                c0, c1 = spans[b]
                dst = e.tok[:, a, c0:c1]
            return dst, ps[:, n % 8, 0:c1 - c0]

        @block.scalar
        def _(act):
            for n in range(0, len(groups), 2):
                act.wait_ge(S["pj_ps"], n + 1)
                kind, a, b = groups[n]
                if kind == "x":
                    g = 1 if a else 0
                    for k in range(4):
                        kk = 4 * b + k
                        i = nc.scalar.activation(e.hT[:, kk, a * P:(a + 1) * P], ps[:, n % 8, k * P:(k + 1) * P], ACT.Identity,
                                                 bias=e.modc[:, g, 0, kk:kk + 1], scale=e.modc[:, g, 1, kk:kk + 1])
                else:
                    dst, src = place(n)
                    i = nc.scalar.activation(dst, src, ACT.Copy)
                i.then_inc(S["pj_act"], 1)

        @block.vector
        def _(dve):
            v = e.chain("dve", dve)
            for col in (0, pad_at(NPR) - 1, PAD - 1):
                v.add(nc.vector.memset(e.rwT[:, :, col:col + 1], 0.0))
            for n in range(1, len(groups), 2):
                dve.wait_ge(S["pj_ps"], n + 1)
                kind, a, b = groups[n]
                if kind == "x":
                    g = 1 if a else 0
                    for k in range(4):
                        kk = 4 * b + k
                        i = nc.vector.tensor_scalar(e.hT[:, kk, a * P:(a + 1) * P], ps[:, n % 8, k * P:(k + 1) * P],
                                                    e.modc[:, g, 1, kk:kk + 1], e.modc[:, g, 0, kk:kk + 1], ALU.mult, ALU.add)
                else:
                    dst, src = place(n)
                    i = nc.vector.tensor_copy(dst, src)
                i.then_inc(S["pj_dve"], 1)
            e.done("dve", v)


ATTENTION_SEMS = (
    "st_cache", "ld_mla", "q_norm", "kv_norm", "rms", "tq_ps", "tq_ev", "tk_ps", "tk_ev", "v_ps", "v_ev", "krot_ps",
    "k_rope0", "k_rope", "qk_ps", "qk_free", "sc_ps", "sc_neg", "sc_exp", "pt_ps", "pt_sb", "pv_ps", "pv_o", "mo_ps",
    "mo_ev",
)


def phase_attention(e):
    nc, d, o, l, S, ps, tok = e.nc, e.d, e.o, e.l, e.S, e.ps, e.tok
    NKEY = NTOK + PAST
    KT = NKEY // P
    uq, z = e.part(e.FREE, 3, NH * QK)
    uk, z = e.part(z, 2, NH * NOPE)
    uv, z = e.part(z, 2, NH * DV)
    cqT, z = e.part(z, 3, NTOK)
    ckvT, z = e.part(z, 2, NKEY)
    V, z = e.part(z, KT, NH * DV)
    cache, z = e.part(z, 2, KVR + ROPE)
    QT, z = e.part(z, 2, NTOK, rows=QK)
    Kh, z = e.part(z, 2, NKEY, rows=QK)
    pr, z = e.part(z, 2, PAST + NSM)
    pT, z = e.part(z, 2, PAST + NSM)
    st, z = e.part(z, 2 * TILES)
    negm, z = e.part(z, NH * TILES)
    rsum, z = e.part(z, NH * TILES)
    rinv, z = e.part(z, NH * TILES)
    assert z <= ARENA
    rt = pT[NOPE:QK].rearrange("p a b -> p (a b)")
    units = [(h, t) for h in range(NH) for t in range(TILES)]
    U = len(units)
    om, z = e.part(z, NRW)
    r1, z = e.part(z, NSM)
    assert z <= ARENA, z
    r1 = r1[NOPE:QK]
    proj = ("q_grid", "rot", "q_ctx", "k_grid", "k_rest")

    with nc.Block() as block:
        @block.sync
        def _(sp):
            e.clear_last(sp)
            for dst, src in ((uq, d["w_uq"][l]), (uk, d["w_uk"][l]), (uv, d["w_uv"][l]),
                             (cache[:, :, 0:KVR], d["c_ckv"][l].rearrange("(t p) n -> p t n", p=P)),
                             (cache[:, :, KVR:], d["c_kr"][l].rearrange("(t p) n -> p t n", p=P))):
                sp.dma_start(dst, src).then_inc(S["ld_mla"], 16)
            sp.wait_ge(S["kv_norm"], 1)
            sp.dma_start(o["n_ckv"][0, l], tok[:, 0, QR:QR + KVR]).then_inc(S["st_cache"], 16)
            sp.dma_start(o["n_kr"][0, l], tok[:, 0, QR + KVR:MLA_COLS]).then_inc(S["st_cache"], 16)
            sp.wait_ge(S["st_cache"], 32)

        def head_product(pe, h, g):
            n = 5 * h + g
            if n:
                pe.wait_ge(S["qk_free"], n)
            if h >= 2 and g == 0:
                pe.wait_ge(S["sc_ps"], TILES * (h - 1))
            b = h % 2
            kind = proj[g]
            if kind in ("q_grid", "q_ctx"):
                c0, c1 = (NPR, NTOK) if kind == "q_grid" else (0, NPR)
                for k in range(3):
                    i = nc.tensor.matmul(ps[0:QK, 7, 0:c1 - c0], uq[:, k, h * QK:(h + 1) * QK], cqT[:, k, c0:c1],
                                         start=k == 0, stop=k == 2)
            elif kind == "rot":
                i = nc.tensor.matmul(ps[NOPE:QK, 7, :], e.rot[NOPE:QK, :], QT[NOPE:QK, b, NPR:NTOK], start=True, stop=True)
            else:
                c0, c1 = (NPR + PAST, NKEY) if kind == "k_grid" else (0, NPR + PAST)
                for k in range(2):
                    i = nc.tensor.matmul(ps[0:NOPE, 7, 0:c1 - c0], uk[:, k, h * NOPE:(h + 1) * NOPE], ckvT[:, k, c0:c1],
                                         start=k == 0, stop=k == 1)
            i.then_inc(S["qk_ps"], 1)

        def keys(t):
            return (0, NPR) if t == 0 else (NPR, NKEY)

        @block.tensor
        def _(pe):
            for t in range(TILES):
                pe.wait_ge(S["q_norm"], t + 1)
                if t >= 4:
                    pe.wait_ge(S["tq_ev"], t - 3)
                for k in range(3):
                    i = nc.tensor.transpose(ps[:, 2 * (t % 4), k * P:(k + 1) * P], tok[:, t, k * P:(k + 1) * P], e.ident[:, :])
                i.then_inc(S["tq_ps"], 1)
            pe.wait_ge(S["ld_mla"], 80)
            for t in range(KT):
                if t < TILES:
                    pe.wait_ge(S["kv_norm"], t + 1)
                    src = tok[:, t, QR:MLA_COLS]
                else:
                    src = cache[:, t - TILES, :]
                if t >= 4:
                    pe.wait_ge(S["tk_ev"], t - 3)
                for k in range(2):
                    nc.tensor.transpose(ps[:, 2 * (t % 4) + 1, k * P:(k + 1) * P], src[:, k * P:(k + 1) * P], e.ident[:, :])
                nc.tensor.transpose(ps[0:ROPE, 2 * (t % 4) + 1, 2 * P:3 * P], src[:, KVR:KVR + ROPE],
                                    e.ident[:, :]).then_inc(S["tk_ps"], 1)
            pe.wait_ge(S["tk_ev"], KT)
            pe.wait_ge(S["tq_ev"], TILES)
            for t in range(KT):
                if t >= 4:
                    pe.wait_ge(S["v_ev"], t - 3)
                for k in range(2):
                    i = nc.tensor.matmul(ps[:, t % 4, :], ckvT[:, k, t * P:(t + 1) * P], uv[:, k, :], start=k == 0, stop=k == 1)
                i.then_inc(S["v_ps"], 1)
            nc.tensor.matmul(ps[NOPE:QK, 6, :], e.rot[NOPE:QK, :], Kh[NOPE:QK, 0, NPR + PAST:], start=True, stop=True
                             ).then_inc(S["krot_ps"], 1)
            for g in range(5):
                if g == 1:
                    pe.wait_ge(S["qk_free"], 1)
                head_product(pe, 0, g)

            def scores(i):
                h, t = units[i]
                if t == 0:
                    pe.wait_ge(S["qk_free"], 5 * (h + 1))
                    pe.wait_ge(S["k_rope"], 1)
                if i >= 2:
                    pe.wait_ge(S["sc_exp"], i - 1)
                elif i == 0:
                    pe.wait_ge(S["v_ev"], KT)
                c0, c1 = keys(t)
                m = nc.tensor.matmul(ps[:, 2 * (i % 2), 0:min(512, c1 - c0)], QT[:, h % 2, t * P:(t + 1) * P],
                                     Kh[:, h % 2, c0:min(c0 + 512, c1)], start=True, stop=True)
                if c1 - c0 > 512:
                    m = nc.tensor.matmul(ps[:, 2 * (i % 2) + 1, 0:c1 - c0 - 512], QT[:, h % 2, t * P:(t + 1) * P],
                                         Kh[:, h % 2, c0 + 512:c1], start=True, stop=True)
                m.then_inc(S["sc_ps"], 1)

            def attend(i):
                h, t = units[i]
                c0, c1 = keys(t)
                pe.wait_ge(S["pt_sb"], i + 1)
                if i >= 2:
                    pe.wait_ge(S["pv_o"], i - 1)
                n = (c1 - c0) // P
                for k in range(n):
                    m = nc.tensor.matmul(ps[:, 6, (i % 2) * DV:(i % 2 + 1) * DV], pT[:, i % 2, k * P:(k + 1) * P],
                                         V[:, c0 // P + k, h * DV:(h + 1) * DV], start=k == 0, stop=k == n - 1)
                m.then_inc(S["pv_ps"], 1)

            scores(0)
            for i, (h, t) in enumerate(units):
                if h + 1 < NH:
                    head_product(pe, h + 1, t)
                if i + 1 < U:
                    scores(i + 1)
                if i == 1:
                    pe.wait_ge(S["k_rope"], 1)
                if i:
                    attend(i - 1)
                pe.wait_ge(S["sc_exp"], i + 1)
                if i:
                    pe.wait_ge(S["pt_sb"], i)
                c0, c1 = keys(t)
                for k in range((c1 - c0) // P):
                    m = nc.tensor.transpose(ps[:, 4 + k // 4, (k % 4) * P:(k % 4 + 1) * P], pr[:, i % 2, k * P:(k + 1) * P],
                                            e.ident[:, :])
                m.then_inc(S["pt_ps"], 1)
            attend(U - 1)
            for t in range(TILES):
                pe.wait_ge(S["pv_o"], U)
                pe.wait_ge(S["sc_exp"], U)
                if t >= 4:
                    pe.wait_ge(S["mo_ev"], t - 3)
                for k in range(4):
                    m = nc.tensor.transpose(ps[:, t % 4, k * P:(k + 1) * P], tok[:, t, k * P:(k + 1) * P], e.ident[:, :])
                m.then_inc(S["mo_ps"], 1)

        @block.scalar
        def _(act):
            a = e.chain("act", act)
            for t in range(TILES):
                a.add(nc.scalar.activation(pr[:, 0, 0:QR], tok[:, t, 0:QR], ACT.Square, accum_out=st[:, t:t + 1]))
                a.link(nc.scalar.activation(pr[:, 1, 0:KVR], tok[:, t, QR:QR + KVR], ACT.Square,
                                            accum_out=st[:, TILES + t:TILES + t + 1]))
            a.add(nc.scalar.activation(st[:, 0:TILES], st[:, 0:TILES], ACT.Sqrt, bias=e.eps[:, 0:1], scale=1.0 / QR))
            nc.scalar.activation(st[:, TILES:], st[:, TILES:], ACT.Sqrt, bias=e.eps[:, 0:1], scale=1.0 / KVR).then_inc(S["rms"], 1)
            for t in range(TILES):
                act.wait_ge(S["tq_ps"], t + 1)
                for k in range(3):
                    m = nc.scalar.activation(cqT[:, k, t * P:(t + 1) * P], ps[:, 2 * (t % 4), k * P:(k + 1) * P], ACT.Copy,
                                             scale=e.pcol[:, PC["qn"] + k:PC["qn"] + k + 1])
                m.then_inc(S["tq_ev"], 1)
            for t in range(KT):
                act.wait_ge(S["v_ps"], t + 1)
                nc.scalar.activation(V[:, t, :], ps[:, t % 4, :], ACT.Copy).then_inc(S["v_ev"], 1)

            def head_evacuate(h, g):
                kind, b = proj[g], h % 2
                if kind == "rot":
                    return
                act.wait_ge(S["qk_ps"], 5 * h + g + 1)
                if kind[0] == "q":
                    c0, c1 = (NPR, NTOK) if kind == "q_grid" else (0, NPR)
                    m = nc.scalar.activation(QT[:, b, c0:c1], ps[0:QK, 7, 0:c1 - c0], ACT.Copy)
                else:
                    c0, c1 = (NPR + PAST, NKEY) if kind == "k_grid" else (0, NPR + PAST)
                    m = nc.scalar.activation(Kh[0:NOPE, b, c0:c1], ps[0:NOPE, 7, 0:c1 - c0], ACT.Copy)
                m.then_inc(S["qk_free"], 1)

            def exponent(i):
                h, t = units[i]
                c0, c1 = keys(t)
                act.wait_ge(S["sc_neg"], i + 1)
                if i >= 2:
                    act.wait_ge(S["pt_ps"], i - 1)
                sc = ps[:, 2 * (i % 2):2 * (i % 2) + 2, :].rearrange("p a b -> p (a b)")
                nc.scalar.activation(pr[:, i % 2, 0:c1 - c0], sc[:, 0:c1 - c0], ACT.Exp, bias=negm[:, i:i + 1], scale=SCALE,
                                     accum_out=rsum[:, i:i + 1]).then_inc(S["sc_exp"], 1)

            for g in range(5):
                head_evacuate(0, g)
            exponent(0)
            for i, (h, t) in enumerate(units):
                if h + 1 < NH:
                    head_evacuate(h + 1, t)
                if i + 1 < U:
                    exponent(i + 1)
            for t in range(TILES):
                act.wait_ge(S["mo_ps"], t + 1)
                nc.scalar.activation(e.mixT[:, 0:4, t * P:(t + 1) * P], ps[:, t % 4, :].rearrange("p (k n) -> p k n", k=4),
                                     ACT.Copy).then_inc(S["mo_ev"], 1)
            e.done("act", a)

        @block.gpsimd
        def _(pool):
            pool.wait_ge(S["k_rope0"], 1)
            nc.gpsimd.tensor_copy(Kh[NOPE:QK, 1, :], Kh[NOPE:QK, 0, :]).then_inc(S["k_rope"], 1)
            pool.wait_ge(S["k_rope"], 1)
            c = e.chain("pool", pool)
            mu = [e.pcol[:, PC[n]:PC[n] + NRW] for n in ("mu0", "mu1")]
            c.link(nc.gpsimd.tensor_tensor(om, mu[0], mu[1], ALU.add))
            c.link(nc.gpsimd.tensor_scalar(om, om, -1.0, 1.0, ALU.mult, ALU.add))
            for n in range(NRW):
                for by, scale in ((0, om), (-1, mu[0]), (1, mu[1])):
                    for c0, c1 in ((0, NPR), (NPR, NTOK)):
                        q0 = pad_at(c0) + by
                        c.add(nc.gpsimd.tensor_scalar(e.mixT[:, 5 + by, c0:c1], e.rwT[:, n, q0:q0 + c1 - c0], scale[:, n:n + 1], None,
                                                      ALU.mult))
                c.join()
                c.link(nc.gpsimd.tensor_tensor(e.mixT[:, 5, :], e.mixT[:, 5, :], e.mixT[:, 4, :], ALU.add))
                c.link(nc.gpsimd.tensor_tensor(e.rwT[:, n, 0:NTOK], e.mixT[:, 5, :], e.mixT[:, 6, :], ALU.add))
            e.done("pool", c)

        @block.vector
        def _(dve):
            v = e.chain("dve", dve)
            dve.wait_ge(S["rms"], 1)
            v.link(nc.vector.reciprocal(st[:, :], st[:, :]))
            for t in range(TILES):
                nc.vector.tensor_scalar(tok[:, t, 0:QR], tok[:, t, 0:QR], st[:, t:t + 1], None, ALU.mult).then_inc(S["q_norm"], 1)
            for t in range(TILES):
                nc.vector.scalar_tensor_tensor(tok[:, t, QR:QR + KVR], tok[:, t, QR:QR + KVR], st[:, TILES + t:TILES + t + 1],
                                               e.prow[:, 0, :], ALU.mult, ALU.mult).then_inc(S["kv_norm"], 1)
            for t in range(KT):
                dve.wait_ge(S["tk_ps"], t + 1)
                at = 0 if t == 0 else (NPR + PAST + (t - 1) * P if t < TILES else NPR + (t - TILES) * P)
                v.add(nc.vector.tensor_copy(Kh[NOPE:QK, 0, at:at + P], ps[0:ROPE, 2 * (t % 4) + 1, 2 * P:3 * P]))
                nc.vector.tensor_copy(ckvT[:, :, at:at + P], ps[:, 2 * (t % 4) + 1, 0:2 * P].rearrange("p (k n) -> p k n", k=2)
                                      ).then_inc(S["tk_ev"], 1)
            g0 = NPR + PAST
            v.join()
            v.link(nc.vector.tensor_tensor(rt[:, 0:NSM], Kh[NOPE:QK, 0, g0:], e.rope[NOPE:QK, 0, :], ALU.mult))
            dve.wait_ge(S["krot_ps"], 1)
            v.link(nc.vector.tensor_tensor(r1, ps[NOPE:QK, 6, :], e.rope[NOPE:QK, 1, :], ALU.mult))
            nc.vector.tensor_tensor(Kh[NOPE:QK, 0, g0:], rt[:, 0:NSM], r1, ALU.add).then_inc(S["k_rope0"], 1)

            def rotate(h):
                b = h % 2
                dve.wait_ge(S["k_rope0"], 1)
                if h:
                    dve.wait_ge(S["qk_free"], 5 * h - 3)
                dve.wait_ge(S["qk_ps"], 5 * h + 2)
                v.link(nc.vector.tensor_tensor(r1, ps[NOPE:QK, 7, :], e.rope[NOPE:QK, 1, :], ALU.mult))
                v.link(nc.vector.tensor_tensor(QT[NOPE:QK, b, NPR:NTOK], QT[NOPE:QK, b, NPR:NTOK], e.rope[NOPE:QK, 0, :], ALU.mult))
                nc.vector.tensor_tensor(QT[NOPE:QK, b, NPR:NTOK], QT[NOPE:QK, b, NPR:NTOK], r1, ALU.add).then_inc(S["qk_free"], 1)

            def row_max(i):
                c0, c1 = keys(units[i][1])
                dve.wait_ge(S["sc_ps"], i + 1)
                sc = ps[:, 2 * (i % 2):2 * (i % 2) + 2, :].rearrange("p a b -> p (a b)")
                v.link(nc.vector.reduce_max(negm[:, i:i + 1], sc[:, 0:c1 - c0], AX))
                nc.vector.tensor_scalar(negm[:, i:i + 1], negm[:, i:i + 1], -SCALE, None, ALU.mult).then_inc(S["sc_neg"], 1)

            def output(i):
                h, t = units[i]
                dve.wait_ge(S["sc_exp"], i + 1)
                v.link(nc.vector.reciprocal(rinv[:, i:i + 1], rsum[:, i:i + 1]))
                dve.wait_ge(S["pv_ps"], i + 1)
                nc.vector.tensor_scalar(tok[:, t, h * DV:(h + 1) * DV], ps[:, 6, (i % 2) * DV:(i % 2 + 1) * DV],
                                        rinv[:, i:i + 1], None, ALU.mult).then_inc(S["pv_o"], 1)

            rotate(0)
            row_max(0)
            dve.wait_ge(S["st_cache"], 32)
            for i, (h, t) in enumerate(units):
                if t == 1 and h + 1 < NH:
                    rotate(h + 1)
                if i + 1 < U:
                    row_max(i + 1)
                if i:
                    output(i - 1)
                c0, c1 = keys(t)
                dve.wait_ge(S["pt_ps"], i + 1)
                if i >= 2:
                    dve.wait_ge(S["pv_ps"], i - 1)
                src = ps[:, 4:6, :].rearrange("p a b -> p (a b)")
                nc.vector.tensor_copy(pT[:, i % 2, 0:c1 - c0], src[:, 0:c1 - c0]).then_inc(S["pt_sb"], 1)
            output(U - 1)
            e.done("dve", v)


HGRN_SEMS = (
    "st_state", "ld_hg", "hg_mask", "hg_zero", "hg_s0", "hg_q", "hg_z", "hg_e", "hg_prep", "hg_kl0", "lv0", "lv1", "at_ps", "at_sb",
    "oh_ps", "ou_sb", "kr_ps", "kr_sb", "kv_ps", "st_new", "hg_state", "hg_g", "hg_o", "hg_sq", "hg_ss", "hg_rt", "hg_on",
)


def phase_hgrn(e):
    nc, d, o, l, S, ps, tok = e.nc, e.d, e.o, e.l, e.S, e.ps, e.tok
    HP = P // 2
    q = e.hgT[:, 0:2, :]
    f = e.hgT[:, 2:6, :]
    qz = e.mixT[:, 4:8, :].rearrange("p (a b) n -> p a b n", a=2)
    oT = tok[:, :, 0:2 * P].rearrange("p t (a n) -> p t a n", a=2)
    vcol = MLA_COLS
    kT, z = e.part(e.FREE, 4, NTOK)
    QL, QF, KL, KR, Pb, Rb, KRt, Sst = [], [], [], [], [], [], [], []
    for _ in range(2):
        v, z = e.part(z, LV, 2, P); QL.append(v)
        v, z = e.part(z, 2, 2, P); QF.append(v)
        v, z = e.part(z, LV - 1, 2, P); KL.append(v)
        v, z = e.part(z, 2, P); KR.append(v)
        v, z = e.part(z, 2, P); Pb.append(v)
        v, z = e.part(z, 2, P); Rb.append(v)
        v, z = e.part(z, 2, P); KRt.append(v)
        v, z = e.part(z, 2, 2, 2, HD); Sst.append(v)
    Sfin, z = e.part(z, 2, 2, HD)
    Ft, z = e.part(z, 2 * TILES, 2)
    am, z = e.part(z, 2, 4 * (LV + 2) * HP)
    hgf, z = e.part(z, 2, (LV + 2) * HP)
    Ed, z = e.part(z, 2, 2, P)
    assert z <= ARENA, z
    sq = kT[:, 0:2, :].rearrange("p a n -> p (a n)").rearrange("p (t a n) -> p t a n", t=TILES, a=2)
    rs = kT[:, 2:4, :]
    og = am[:, 0, 0:2 * NTOK].rearrange("p (a n) -> p a n", a=2)
    units = [(0, 0), (0, 1), (1, 0), (4, 1), (2, 0), (3, 1), (3, 0), (2, 1), (4, 0), (1, 1)]
    U = len(units)
    last = ((4, 0), (1, 1))
    NG = 5
    parts = ((0, P), (P, NTOK))

    def halves(a, h, s):
        return a.rearrange("p a (n s h) -> p a n s h", s=2, h=h)[:, :, :, s, :]

    def q_level(u, j, a):
        if u % 4 != 3:
            return QL[u % 2][:, j, a]
        if j < TILES:
            return tok[:, j, (2 + a) * P:(3 + a) * P]
        return tok[:, 2 * (j - TILES) + a, 4 * P:5 * P]

    def levels(eng, c, u):
        t, dr = units[u]
        cols = slice(t * P, (t + 1) * P)
        Pd, Rd, k = Pb[dr], Rb[dr], kT[:, 2 * dr:2 * dr + 2, cols]
        near, far = (0, 1) if dr == 0 else (1, 0)

        def edges(j):
            return Ed[:, dr, :, P - (P >> j):P - (P >> (j + 1))].rearrange("p a (n o) -> p a n o", o=1)

        if u >= 4:
            eng.wait_ge(S["at_ps"], NG * (u - 3))
        c.link(eng.tensor_copy(Pd, f[:, 2 * dr:2 * dr + 2, cols]))
        yield
        for j in range(LV):
            h = 1 << j
            n = P // (2 * h)
            for a in range(2):
                c.add(eng.tensor_tensor(
                    q_level(u, j, a).rearrange("p (b n h) -> p b n h", b=2, h=h),
                    qz[:, a, :, cols].rearrange("p b (n s h) -> p b n s h", s=2, h=h)[:, :, :, far, :],
                    halves(Pd, h, far)[:, a:a + 1].to_broadcast([P, 2, n, h]), ALU.mult))
                yield
            edge = h - 1 if dr == 0 else 0
            c.link(eng.tensor_copy(edges(j), halves(Pd, h, far)[:, :, :, edge:edge + 1]))
            yield
            c.link(eng.tensor_tensor(halves(Pd, h, far), halves(Pd, h, far),
                                     halves(Pd, h, near)[:, :, :, edge:edge + 1].to_broadcast([P, 2, n, h]), ALU.mult))
            yield
        end = P - 1 if dr == 0 else 0
        c.add(eng.tensor_copy(Ft[:, u, :], Pd[:, :, end:end + 1].rearrange("p a b -> p (a b)")))
        if u >= 4:
            eng.wait_ge(S["oh_ps"], u - 3)
        c.add(eng.tensor_tensor(QF[dr][:, u // 2 % 2], q[:, :, cols], Pd, ALU.mult))
        yield
        c.link(eng.memset(Rd, 1.0))
        if u >= 2:
            eng.wait_ge(S["at_ps"], NG * (u - 1))
        for j in range(LV):
            h = 1 << j
            if j:
                c.link(eng.tensor_tensor(halves(KL[dr][:, j - 1], h, near), halves(k, h, near), halves(Rd, h, near), ALU.mult))
                yield
            c.link(eng.tensor_tensor(halves(Rd, h, near), halves(Rd, h, near), edges(j).to_broadcast([P, 2, P // (2 * h), h]), ALU.mult))
            yield
        if u >= 2:
            eng.wait_ge(S["kr_ps"], u - 1)
        c.link(eng.tensor_tensor(KR[dr], k, Rd, ALU.mult))

    def bank(g):
        w = 512 if g < 4 else 256
        return ps[:, g, 0:w], slice(512 * g, 512 * g + w)

    with nc.Block() as block:
        @block.sync
        def _(sp):
            e.clear_last(sp)
            sp.dma_start(hgf, d["hgf"]).then_inc(S["hg_mask"], 16)
            sp.wait_ge(S["hg_s0"], 1)
            for dr in range(2):
                for b in range(2):
                    sp.dma_start(Sst[dr][b * HD:(b + 1) * HD, 1, :, b, :],
                                 d["s_hg"][l, dr, :, b * HD:(b + 1) * HD, :].rearrange("a p v -> p a v")).then_inc(S["ld_hg"], 16)
            sp.wait_ge(S["hg_state"], 2)
            for dr in range(2):
                sp.dma_start(o["n_hg"][0, l, dr].rearrange("(a b) k v -> a (b k) v", a=2).rearrange("a p v -> p a v"),
                             Sfin[:, dr]).then_inc(S["st_state"], 16)
            sp.wait_ge(S["st_state"], 32)

        @block.scalar
        def _(act):
            a = e.chain("act", act)
            for i, (c0, c1) in enumerate(parts):
                act.wait_ge(S["hg_z"], i + 1)
                a.add(nc.scalar.activation(kT[:, :, c0:c1], f[:, :, c0:c1], ACT.Sigmoid, scale=-1.0))
                a.join()
                nc.scalar.activation(f[:, :, c0:c1], f[:, :, c0:c1], ACT.Sigmoid).then_inc(S["hg_e"], 1)
                if i == 0:
                    act.wait_ge(S["hg_zero"], 1)
                for b in range(2):
                    r = slice(b * HD, (b + 1) * HD)
                    a.add(nc.scalar.activation(qz[r, :, b, c0:c1], q[r, :, c0:c1], ACT.Silu))
                a.join()
                nc.scalar.activation(q[:, :, c0:c1], q[:, :, c0:c1], ACT.Silu).then_inc(S["hg_q"], 1)
            for u, (t, dr) in enumerate(units):
                if (t, dr) in last:
                    continue
                act.wait_ge(S["kr_ps"], u + 1)
                if u >= 2:
                    act.wait_ge(S["kv_ps"], u - 1)
                nc.scalar.activation(KRt[dr], ps[:, 7, 0:2 * P].rearrange("p (a b) -> p a b", a=2), ACT.Copy
                                     ).then_inc(S["kr_sb"], 1)
            nc.scalar.activation(e.gT, e.gT, ACT.Silu).then_inc(S["hg_g"], 1)
            act.wait_ge(S["hg_o"], 1)
            nc.scalar.activation(sq, oT, ACT.Square).then_inc(S["hg_sq"], 1)
            for p in range(2):
                act.wait_ge(S["hg_ss"], p + 1)
                nc.scalar.activation(rs[:, p, :], ps[:, 2 * p:2 * p + 2, :].rearrange("p a b -> p (a b)")[:, 0:NTOK], ACT.Sqrt,
                                     bias=e.eps[:, 0:1], scale=1.0 / HD).then_inc(S["hg_rt"], 1)
            e.done("act", a)

        @block.gpsimd
        def _(pool):
            c = e.chain("pool", pool)
            nc.gpsimd.memset(qz, 0.0).then_inc(S["hg_zero"], 1)
            nc.gpsimd.memset(KL[0], 0.0).then_inc(S["hg_kl0"], 1)
            c.add(nc.gpsimd.memset(KL[1], 0.0))
            c.join()
            k = 0
            for u, (t, dr) in enumerate(units):
                if dr == 0:
                    continue
                if k < 2:
                    pool.wait_ge(S["hg_prep"], k + 1)
                    pool.wait_ge(S["hg_q"], k + 1)
                for _ in levels(nc.gpsimd, c, u):
                    pass
                k += 1
                pool.sem_inc(S["lv1"], 1)
            e.done("pool", c)

        @block.tensor
        def _(pe):
            def scores(u):
                t, dr = units[u]
                cols = slice(t * P, (t + 1) * P)

                def level(hp, j, dst):
                    keys = kT[:, 2 * dr + hp, cols] if j == 1 else KL[dr][:, j - 2, hp, :]
                    return nc.tensor.matmul(dst, keys, q_level(u, j - 1, hp), start=True, stop=True)

                pe.wait_ge(S[f"lv{dr}"], u // 2 + 1)
                for g in range(NG):
                    if u:
                        pe.wait_ge(S["at_sb"], NG * (u - 1) + g + 1)
                    if g < 4:
                        two = ps[:, g, :].rearrange("p (b n) -> p b n", b=2)
                        if g % 2 == 0:
                            nc.tensor.matmul(two[:, :, 0:P], kT[:, 2 * dr + g // 2, cols], qz[:, g // 2, :, cols], start=True, stop=True)
                            where = ((1, P), (2, P + HP))
                        else:
                            where = tuple((3 + n, n * HP) for n in range(4))
                        for j, at in where:
                            m = level(g // 2, j, two[:, :, at:at + HP])
                    else:
                        for hp in range(2):
                            m = level(hp, LV, ps[:, g, hp * P:(hp + 1) * P])
                    m.then_inc(S["at_ps"], 1)

            def out(u):
                t, dr = units[u]
                k = u // 2
                if u >= 2:
                    pe.wait_ge(S["ou_sb"], u - 1)
                if t:
                    if k == 1:
                        pe.wait_ge(S["ld_hg"], 64)
                    else:
                        pe.wait_ge(S["st_new"], u - 1)
                for hp in range(2):
                    whole = ps[:, 5 + u % 2, hp * P:(hp + 1) * P]
                    if t:
                        nc.tensor.matmul(whole, Sst[dr][:, k % 2, hp].rearrange("p b v -> p (b v)"), QF[dr][:, k % 2, hp, :],
                                         start=True, stop=False)
                    pe.wait_ge(S["at_sb"], NG * (u + 1))
                    for b in range(2):
                        r = slice(b * HD, (b + 1) * HD)
                        h = 2 * hp + b
                        vals = tok[:, t, vcol + h * HD:vcol + (h + 1) * HD]
                        at = 2 * hp * 512 + b * 256
                        nc.tensor.matmul(whole[r], vals, am[:, u % 2, at:at + P], start=t == 0, stop=False)
                        for j in range(1, LV + 1):
                            hf = 1 << (j - 1)
                            at = (2 * hp * 512 + b * 256 + P + (j - 1) * HP if j <= 2 else
                                  (2 * hp + 1) * 512 + b * 256 + (j - 3) * HP if j < LV else 4 * 512 + h * HP)
                            m = nc.tensor.matmul(whole[r].rearrange("p (n s h) -> p n s h", s=2, h=hf)[:, :, 1 - dr, :], vals,
                                                 am[:, u % 2, at:at + HP], start=False, stop=j == LV)
                m.then_inc(S["oh_ps"], 1)

            for u, (t, dr) in enumerate(units):
                scores(u)
                if (t, dr) not in last:
                    if u:
                        pe.wait_ge(S["st_new"], u)
                    for a in range(2):
                        m = nc.tensor.transpose(ps[:, 7, a * P:(a + 1) * P], KR[dr][:, a, :], e.ident[:, :])
                    m.then_inc(S["kr_ps"], 1)
                if u:
                    out(u - 1)
                if (t, dr) not in last:
                    pe.wait_ge(S["kr_sb"], u + 1)
                    for hh in range(HH):
                        m = nc.tensor.matmul(ps[HD * (hh % 2):HD * (hh % 2) + HD, 7, 2 * P + (hh // 2) * HD:2 * P + (hh // 2 + 1) * HD],
                                             KRt[dr][:, hh // 2, HD * (hh % 2):HD * (hh % 2) + HD],
                                             tok[:, t, vcol + hh * HD:vcol + (hh + 1) * HD], start=True, stop=True)
                    m.then_inc(S["kv_ps"], 1)
            out(U - 1)
            pe.wait_ge(S["hg_sq"], 1)
            for p in range(2):
                nc.tensor.matmul(ps[:, 2 * p, :], e.blk[:, :], sq[:, 0:4, p, :], start=True, stop=True)
                nc.tensor.matmul(ps[:, 2 * p + 1, 0:P], e.blk[:, :], sq[:, 4, p, :], start=True, stop=True
                                 ).then_inc(S["hg_ss"], 1)

        @block.vector
        def _(dve):
            v = e.chain("dve", dve)
            for c0, c1 in parts:
                nc.vector.tensor_scalar(f[:, :, c0:c1], f[:, :, c0:c1], 60.0, -60.0, ALU.min, ALU.max).then_inc(S["hg_z"], 1)
                if c0 == 0:
                    for dr in range(2):
                        v.add(nc.vector.memset(Sst[dr], 0.0))
                    v.join()
                    dve.sem_inc(S["hg_s0"], 1)

            def prepare(i):
                c0, c1 = parts[i]
                dve.wait_ge(S["hg_e"], i + 1)
                for c in range(4):
                    v.add(nc.vector.tensor_scalar(f[:, c, c0:c1], f[:, c, c0:c1], e.oml[:, c:c + 1], e.lb[:, c:c + 1], ALU.mult, ALU.add))
                    v.add(nc.vector.tensor_scalar(kT[:, c, c0:c1], kT[:, c, c0:c1], e.oml[:, c:c + 1], None, ALU.mult))
                v.join()
                dve.sem_inc(S["hg_prep"], 1)

            def run_levels(u):
                if u < 4:
                    dve.wait_ge(S["hg_q"], u // 2 + 1)
                if u == 0:
                    dve.wait_ge(S["hg_kl0"], 1)
                for _ in levels(nc.vector, v, u):
                    yield
                dve.sem_inc(S["lv0"], 1)

            def collect(u):
                t, dr = units[u]
                dve.wait_ge(S["oh_ps"], u + 1)
                src = ps[:, 5 + u % 2, 0:2 * P].rearrange("p (a n) -> p a n", a=2)
                if t in [x for x, _ in units[:u]]:
                    dve.wait_ge(S["ou_sb"], u)
                    nc.vector.tensor_tensor(oT[:, t], oT[:, t], src, ALU.add).then_inc(S["ou_sb"], 1)
                else:
                    nc.vector.tensor_copy(oT[:, t], src).then_inc(S["ou_sb"], 1)

            def state(u):
                t, dr = units[u]
                k = u // 2
                dve.wait_ge(S["kv_ps"], u + 1)
                dve.wait_ge(S[f"lv{dr}"], k + 1)
                src = ps[:, 7, 2 * P:2 * P + 2 * HD].rearrange("p (a b) -> p a b", a=2)
                if t == 0:
                    v.link(nc.vector.tensor_copy(Sfin[:, dr], src))
                    dve.sem_inc(S["hg_state"], 1)
                else:
                    dve.wait_ge(S["ld_hg"], 64)
                    for a in range(2):
                        for b in range(2):
                            r = slice(b * HD, (b + 1) * HD)
                            v.add(nc.vector.scalar_tensor_tensor(Sst[dr][r, (k + 1) % 2, a, b], Sst[dr][r, k % 2, a, b],
                                                                 Ft[r, u, a:a + 1], src[r, a], ALU.mult, ALU.add))
                    v.join()
                dve.sem_inc(S["st_new"], 1)

            prepare(0)
            for _ in run_levels(0):
                pass
            prepare(1)
            dve.wait_ge(S["hg_mask"], 16)
            nxt = None
            for u, (t, dr) in enumerate(units):
                for g in range(NG):
                    dve.wait_ge(S["at_ps"], NG * u + g + 1)
                    if g == 0 and u >= 2:
                        dve.wait_ge(S["oh_ps"], u - 1)
                    src, at = bank(g)
                    m0, m1, rep = ((0, 256, 2), (256, 512, 2))[g % 2] if g < 4 else (512, 576, 4)
                    nc.vector.tensor_tensor(am[:, u % 2, at].rearrange("p (b n) -> p b n", b=rep), src.rearrange("p (b n) -> p b n", b=rep),
                                            hgf[:, dr:dr + 1, m0:m1].to_broadcast([P, rep, m1 - m0]), ALU.mult
                                            ).then_inc(S["at_sb"], 1)
                if dr == 0 and u + 2 < U:
                    nxt = run_levels(u + 2)
                    for _ in range(22):
                        next(nxt)
                if dr == 1 and nxt:
                    for _ in nxt:
                        pass
                    nxt = None
                if u:
                    collect(u - 1)
                if (t, dr) not in last:
                    state(u)
            collect(U - 1)
            dve.wait_ge(S["ou_sb"], U)
            dve.sem_inc(S["hg_o"], 1)
            dve.wait_ge(S["hg_g"], 1)
            tiled = lambda a: a.rearrange("p (t n) -> p t n", t=TILES)
            for p in range(2):
                v.add(nc.vector.scalar_tensor_tensor(tiled(og[:, p, :]), tiled(e.gT[:, p, :]), e.pcol[:, PC["hn"] + p:PC["hn"] + p + 1],
                                                     oT[:, :, p, :], ALU.mult, ALU.mult))
            for p in range(2):
                dve.wait_ge(S["hg_rt"], p + 1)
                v.link(nc.vector.reciprocal(rs[:, p, :], rs[:, p, :]))
                nc.vector.tensor_tensor(e.mixT[:, 4 + p, :], og[:, p, :], rs[:, p, :], ALU.mult).then_inc(S["hg_on"], 1)
            e.done("dve", v)


RWKV_SEMS = (
    "ld_rw", "rw_wz", "rw_oka", "bo_ev", "bonus", "rw_th", "rw_k0", "rw_ksq", "lo_ps", "lo_ev", "vt_ps", "vt_ev", "kn_ps",
    "rw_kmax", "rw_krt", "rw_kn", "rw_kd", "rw_bon", "rw_E", "rw_ex", "rw_pre", "rw_G0", "rw_G", "m_ps", "l_ps",
    "kb_ps", "kb_sb", "mj", "t1_ps", "t1_sb", "sm", "vz", "rh_ps", "rh_sb", "u_ps", "u_sb", "rs_ps", "y_ps", "y_ev",
    "rw_sfin", "fin_ps", "rw_fin", "st_rw", "gn_c", "gn_sq", "gn_var", "gn_rt", "bo_ps", "ga_ps", "rw_out", "ro_ps",
    "ro_ev", "dxy_ps", "ls", "m_sb", "mt_ps", "mt_sb", "xy", "xy1",
)


def phase_rwkv(e):
    nc, d, o, l, S, ps = e.nc, e.d, e.o, e.l, e.S, e.ps
    R = slice(0, NTOK)
    HI, LO = slice(C, P), slice(0, C)
    kk, z = e.part(e.a0, 2, NTOK)
    T, z = e.part(z, 3, NTOK)
    assert z <= e.a1
    F = e.rwT[:, :, 0:NTOK]
    KB, z = e.part(e.a2, 4, NCH, 2, C)
    AR, z = e.part(z, 4, 2, NTOK)
    Vc, z = e.part(z, NCH, HH * HD, rows=C)
    VU, z = e.part(z, 2, 8, HD)
    KBt, z = e.part(z, 2, 4, P)
    RH, z = e.part(z, HH, HD)
    Sm, z = e.part(z, 4, 2, HD)
    Sn, z = e.part(z, 4, 2, HD)
    S0, z = e.part(z, 4, HD)
    S0b, z = e.part(z, 4, 2, HD)
    Sfin, z = e.part(z, 4, 2, HD)
    yst0 = z
    Yst, z = e.part(z, 2, TILES, HH, P)
    sq, _ = e.part(yst0, NCH * HH * HD, rows=C)
    msk, z1 = e.part(e.a0, 2, HH, P)
    Ms = (msk, VU.rearrange("p a b c -> p (a b c)").rearrange("p (l h n) -> p l h n", l=2, h=HH))
    Ls = KBt.rearrange("p a b c -> p (a b c)").rearrange("p (l h n) -> p l h n", l=2, h=HH)
    Mj, z1 = e.part(z1, 2, 2, HH, P)
    assert z1 <= e.a1
    M, z1 = e.part(e.a0, 2, 8, P)
    So, z1 = e.part(z1, 4, P)
    assert z1 <= e.a1
    x0, z1 = e.part(e.a1, 2, HH, P)
    T1, z1 = e.part(z1, 2, HH, P)
    ys, z1 = e.part(e.a1, NCH, HH * HD, rows=C)
    assert z1 <= e.a1 + 4 * PAD
    x1, z = e.part(z, 2, HH, P)
    X = (x0, x1)
    mid, z = e.part(z, 4, NCH)
    end, z = e.part(z, 4, NCH)
    G, z = e.part(z, 4, NCH)
    Gb, z = e.part(z, 4, NCH, 2)
    mu, z = e.part(z, NCH * HH, rows=C)
    rs, z = e.part(z, NCH * HH, rows=C)
    wwa, z = e.part(z, 2, 2, HH * HD)
    oka, z = e.part(z, 2)
    g2, z = e.part(z, HH * HD)
    assert z <= ARENA, z
    cut = ((NPR, NTOK), (0, NPR))
    DECAY = -float(np.exp(-0.5))
    steps = [(0, 1), (1, 0)] + [(2 + i, NCH - 1 - i) for i in range(NCH - 2)]
    NS = len(steps)
    LVC = 5

    def blockrow(c):
        return slice(C * (c % 2), C * (c % 2) + C)

    first = (True, False) + (True,) * 4 + (False,) * 4
    pc = e.pcol

    def col(name, i):
        return pc[:, PC[name] + i:PC[name] + i + 1]

    def ck(c):
        return slice(C * c, C * c + C)

    def by_chunk(a):
        return a.rearrange("p (c t) -> p c t", t=C)

    lora = [(w, dr, pair, i) for dr in range(2) for pair in range(2) for w in (1, 0) for i in range(2)]
    ksq = lambda p: AR[:, 2 + p, 1, R]

    with nc.Block() as block:
        @block.sync
        def _(sp):
            e.clear_last(sp)
            sp.wait_ge(S["rw_wz"], 1)
            for dr in range(2):
                r = slice(C * dr, C * dr + C)
                sp.dma_start(wwa[r, dr], d["w_wa"][l, r]).then_inc(S["ld_rw"], 16)
            sp.dma_start(g2, d["w_g2"][l]).then_inc(S["ld_rw"], 16)
            sp.dma_start(S0, d["s_rw"][l].rearrange("d a p v -> p (d a) v")).then_inc(S["ld_rw"], 16)
            sp.wait_ge(S["rw_fin"], 1)
            for dr in range(2):
                for par in range(2):
                    sp.dma_start(o["n_rw"][0, l, dr].rearrange("(a b) v k -> b v a k", a=2)[par],
                                 So[par * HD:(par + 1) * HD, 2 * dr:2 * dr + 2, par * HD:(par + 1) * HD]).then_inc(S["st_rw"], 16)
            sp.wait_ge(S["st_rw"], 64)

        @block.scalar
        def _(act):
            a = e.chain("act", act)
            nc.scalar.activation(F[:, 6, R], F[:, 6, R], ACT.Tanh).then_inc(S["rw_th"], 1)
            for p in range(2):
                act.wait_ge(S["rw_k0"], p + 1)
                nc.scalar.activation(ksq(p), kk[:, p, R], ACT.Square).then_inc(S["rw_ksq"], 1)
            for n, (w, dr, pair, i) in enumerate(lora):
                if n == 4:
                    for p in range(2):
                        act.wait_ge(S["rw_kmax"], p + 1)
                        nc.scalar.activation(ksq(p), ksq(p), ACT.Sqrt).then_inc(S["rw_krt"], 1)
                act.wait_ge(S["lo_ps"], n + 1)
                c0, c1 = cut[i]
                dst = by_chunk(AR[:, 2 * dr + pair, 0, c0:c1]) if w == 0 else KB[:, 2 * dr + pair, c0 // C:c1 // C, 1, :]
                nc.scalar.activation(dst, by_chunk(ps[:, n % 8, 0:c1 - c0]), ACT.Sigmoid, bias=col("a0" if w else "w0", 2 * dr + pair)
                                     ).then_inc(S["lo_ev"], 1)
            a.add(nc.scalar.activation(F[:, 8, R], F[:, 8, R], ACT.Sigmoid))
            for dp in range(4):
                act.wait_ge(S["rw_E"], dp + 1)
                nc.scalar.activation(T[:, 2, R], T[:, 0, R], ACT.Exp, scale=-1.0).then_inc(S["rw_ex"], 1)
                nc.scalar.activation(AR[:, dp, 1, R], T[:, 0, R], ACT.Exp).then_inc(S["rw_ex"], 1)
                nc.scalar.activation(AR[:, dp, 0, R], AR[:, dp, 0, R], ACT.Exp).then_inc(S["rw_ex"], 1)
            for n in range(NCH // 2):
                act.wait_ge(S["vt_ps"], n + 1)
                nc.scalar.activation(Vc[:, 2 * n:2 * n + 2, :], ps[LO, 2 * (n % 2), :].rearrange("p (a b) -> p a b", a=2), ACT.Copy
                                     ).then_inc(S["vt_ev"], 1)
            act.wait_ge(S["rw_G0"], 1)
            a.link(nc.scalar.activation(G, G, ACT.Exp))
            nc.scalar.activation(mid, mid, ACT.Exp).then_inc(S["rw_G"], 1)

            def transposed(t):
                for ln in range(2):
                    act.wait_ge(S["mt_ps"], 2 * t + ln + 1)
                    if t >= 2:
                        act.wait_ge(S["mj"], 2 * LVC * (t - 1))
                    nc.scalar.activation(Ms[t % 2][:, ln], ps[:, 6 + ln, :].rearrange("p (a b) -> p a b", a=HH), ACT.Copy
                                         ).then_inc(S["mt_sb"], 1)

            transposed(0)
            for t in range(TILES):
                for j in range(LVC):
                    for ln in range(2):
                        act.wait_ge(S["t1_ps"], (LVC * t + j) * 2 + ln + 1)
                        nc.scalar.activation(T1[:, ln], ps[:, 4 + ln, :].rearrange("p (a b) -> p a b", a=HH), ACT.Copy
                                             ).then_inc(S["t1_sb"], 1)
                    if j == 2 and t + 1 < TILES:
                        transposed(t + 1)
            for s in range(-1, NS):
                if s >= 0:
                    for dr in range(2):
                        act.wait_ge(S["u_ps"], 2 * s + dr + 1)
                        nc.scalar.activation(VU[HI, s % 2, 4 * dr:4 * dr + 4], ps[HI, 5 + dr, 0:4 * HD].rearrange("p (a b) -> p a b", a=4),
                                             ACT.Copy, scale=-1.0).then_inc(S["u_sb"], 1)
                if s + 1 < NS:
                    act.wait_ge(S["kb_ps"], s + 2)
                    nc.scalar.activation(KBt[:, (s + 1) % 2], ps[:, 4, :].rearrange("p (a b) -> p a b", a=4), ACT.Copy
                                         ).then_inc(S["kb_sb"], 1)
            act.wait_ge(S["fin_ps"], 1)
            nc.scalar.activation(So.rearrange("p a b -> p (a b)"), ps[:, 6, :], ACT.Copy).then_inc(S["rw_fin"], 1)
            act.wait_ge(S["gn_c"], 1)
            nc.scalar.activation(sq, ys.rearrange("p a b -> p (a b)"), ACT.Square).then_inc(S["gn_sq"], 1)
            act.wait_ge(S["gn_var"], 1)
            nc.scalar.activation(rs, rs, ACT.Sqrt, bias=e.eps[LO, 2:3], scale=1.0 / HD).then_inc(S["gn_rt"], 1)
            for k in range(2):
                act.wait_ge(S["ro_ps"], k + 1)
                nc.scalar.activation(e.mixT[:, 6 + k, :], ps[:, 2 * k:2 * k + 2, :].rearrange("p a b -> p (a b)")[:, 0:NTOK],
                                     ACT.Copy).then_inc(S["ro_ev"], 1)
            e.done("act", a)

        @block.gpsimd
        def _(pool):
            c = e.chain("pool", pool)
            for dp in range(4):
                dr, p = divmod(dp, 2)
                if dp == 0:
                    pool.wait_ge(S["rw_oka"], 1)
                pool.wait_ge(S["lo_ev"], 4 * dp + 2)
                c.link(nc.gpsimd.tensor_scalar(by_chunk(T[:, 1, R]), KB[:, dp, :, 1, :], col("ka", p), oka[:, p:p + 1], ALU.mult, ALU.add))
                c.link(nc.gpsimd.tensor_tensor(KB[:, dp, :, 0, :], by_chunk(T[:, 1, R]), by_chunk(F[:, 2 + p, R]), ALU.mult))
                if dp == 0:
                    pool.wait_ge(S["lo_ev"], len(lora))
                if dr == 0:
                    m = nc.gpsimd.tensor_copy(by_chunk(F[:, 6 + p, R]), KB[:, dp, :, 0, :])
                else:
                    m = nc.gpsimd.tensor_tensor(by_chunk(F[:, 6 + p, R]), by_chunk(F[:, 6 + p, R]), KB[:, dp, :, 0, :], ALU.add)
                m.then_inc(S["rw_kd"], 1)
                pool.wait_ge(S["rw_kd"], dp + 1)
            for p in range(2):
                c.link(nc.gpsimd.tensor_tensor(F[:, 6 + p, R], F[:, 6 + p, R], F[:, p, R], ALU.mult))
                nc.gpsimd.tensor_scalar(F[:, 6 + p, R], F[:, 6 + p, R], col("rk", p), None, ALU.mult).then_inc(S["rw_bon"], 1)
            pool.wait_ge(S["rw_pre"], 4)
            pool.wait_ge(S["rw_bon"], 2)

            def masked(dst, src, dr, j):
                return nc.gpsimd.tensor_tensor(dst, src, e.hgm[:, dr, (j + 1) * P:(j + 2) * P].rearrange("p (o n) -> p o n", o=1)
                                               .to_broadcast([P, HH, P]), ALU.mult)

            def next_mask(t, j, ln):
                k = LVC * t + j
                if k >= 2:
                    pool.wait_ge(S["t1_ps"], 2 * (k - 2) + ln + 1)
                masked(Mj[:, ln, k % 2], Ms[t % 2][:, ln], ln, j + 1).then_inc(S["mj"], 1)

            idn = e.ident[:, :].rearrange("p (o n) -> p o n", o=1).to_broadcast([P, HH, P])
            for t in range(TILES):
                for ln in range(2):
                    pool.wait_ge(S["mt_sb"], 2 * t + ln + 1)
                    c.add(masked(X[t % 2][:, ln], Ls[:, ln], 1 - ln, 0))
                    c.link(masked(Yst[:, ln, t], Ms[t % 2][:, ln], ln, 0))
                    c.add(nc.gpsimd.tensor_tensor(X[t % 2][:, ln], idn, X[t % 2][:, ln], ALU.subtract))
                    c.link(nc.gpsimd.tensor_tensor(Yst[:, ln, t], idn, Yst[:, ln, t], ALU.subtract))
                    pool.sem_inc(S["xy1"], 1)
                    next_mask(t, 0, ln)
                for j in range(1, LVC):
                    for ln in range(2):
                        next_mask(t, j, ln)
            pool.wait_ge(S["vt_ev"], NCH // 2)
            pool.wait_ge(S["mj"], 2 * LVC * TILES)
            for s, chunks in enumerate(steps):
                if s >= 2:
                    pool.wait_ge(S["y_ps"], s - 1)
                for dr in range(2):
                    c.add(nc.gpsimd.tensor_copy(VU[LO, s % 2, 4 * dr:4 * dr + 4, :],
                                                Vc[:, chunks[dr], :].rearrange("p (a v) -> p a v", a=4)))
                c.join()
                nc.gpsimd.memset(VU[HI, s % 2], 0.0).then_inc(S["vz"], 1)
            Vv = Vc.rearrange("p c (h v) -> p (c h) v", v=HD)
            pool.wait_ge(S["bo_ev"], 1)
            pool.wait_ge(S["vz"], NS)
            c.link(nc.gpsimd.tensor_tensor(Vv, Vv, mu.rearrange("p (n o) -> p n o", o=1).to_broadcast([C, NCH * HH, HD]), ALU.mult))
            nc.gpsimd.tensor_tensor(Vc, Vc, e.prow[LO, 2:3, :].to_broadcast([C, NCH, HH * HD]), ALU.add).then_inc(S["bonus"], 1)
            e.done("pool", c)

        @block.tensor
        def _(pe):
            pe.wait_ge(S["rw_th"], 1)
            for p in range(2):
                pe.wait_ge(S["rw_ksq"], p + 1)
                for i, (c0, c1) in enumerate(cut):
                    nc.tensor.matmul(ps[:, 4 + 2 * p + i, 0:c1 - c0], e.blk[:, :], ksq(p)[:, c0:c1], start=True, stop=True
                                     ).then_inc(S["kn_ps"], 1)
            pe.wait_ge(S["ld_rw"], 64)
            for n, (w, dr, pair, i) in enumerate(lora):
                if n == 4:
                    pe.wait_ge(S["rw_kmax"], 2)
                if n >= 8:
                    pe.wait_ge(S["lo_ev"], n - 7)
                c0, c1 = cut[i]
                nc.tensor.matmul(ps[:, n % 8, 0:c1 - c0], wwa[:, dr, w, pair * P:(pair + 1) * P], F[:, 6 + w, c0:c1],
                                 start=True, stop=True).then_inc(S["lo_ps"], 1)
            pe.wait_ge(S["lo_ev"], len(lora))
            for n in range(NCH // 2):
                if n >= 2:
                    pe.wait_ge(S["vt_ev"], n - 1)
                for i in range(2):
                    for p in range(2):
                        m = nc.tensor.transpose(ps[LO, 2 * (n % 2), i * 256 + p * P:i * 256 + (p + 1) * P], F[:, 4 + p, ck(2 * n + i)],
                                                e.ident[:, :])
                m.then_inc(S["vt_ps"], 1)
            pe.wait_ge(S["rw_pre"], 4)
            pe.wait_ge(S["vt_ev"], NCH // 2)

            def products(t):
                if t:
                    pe.wait_ge(S["mt_sb"], 2 * t)
                for par in range(2):
                    for ln in range(2):
                        for pair in range(2):
                            r, dp = slice(HD * par, HD * par + HD), 2 * ln + pair
                            m = nc.tensor.matmul(ps[:, 6 + par, (2 * ln + pair) * P:(2 * ln + pair + 1) * P],
                                                 AR[r, dp, 0, t * P:(t + 1) * P], KB[r, dp, 2 * t:2 * t + 2, 1, :], start=True, stop=True)
                m.then_inc(S["l_ps"], 1)

            def turn(t):
                pe.wait_ge(S["ls"], t + 1)
                for ln in range(2):
                    for h in range(HH):
                        m = nc.tensor.transpose(ps[:, 6 + ln, h * P:(h + 1) * P], Ls[:, ln, h, :], e.ident[:, :])
                    m.then_inc(S["mt_ps"], 1)

            products(0)
            turn(0)
            for t in range(TILES):
                for j in range(LVC):
                    for ln in range(2):
                        n = (LVC * t + j) * 2 + ln
                        if j == 0:
                            pe.wait_ge(S["xy1"], 2 * t + ln + 1)
                        if n >= 2:
                            pe.wait_ge(S["xy"], n - 1)
                        pe.wait_ge(S["mj"], n + 1)
                        for h in range(HH):
                            m = nc.tensor.matmul(ps[:, 4 + ln, h * P:(h + 1) * P], Mj[:, ln, (LVC * t + j) % 2, h, :], X[t % 2][:, ln, h, :],
                                                 start=True, stop=True)
                        m.then_inc(S["t1_ps"], 1)
                    for ln in range(2):
                        pe.wait_ge(S["t1_sb"], (LVC * t + j) * 2 + ln + 1)
                        if j < LVC - 1:
                            for h in range(HH):
                                nc.tensor.matmul(ps[:, 2 * ln, h * P:(h + 1) * P], Yst[:, ln, t, h, :], T1[:, ln, h, :],
                                                 start=True, stop=True)
                        for h in range(HH):
                            m = nc.tensor.matmul(ps[:, 2 * ln + 1, h * P:(h + 1) * P], T1[:, ln, h, :], Yst[:, ln, t, h, :],
                                                 start=True, stop=True)
                        m.then_inc(S["dxy_ps"], 1)
                    if j < 2 and t + 1 < TILES:
                        (products, turn)[j](t + 1)
            pe.wait_ge(S["rw_G"], 1)
            pe.wait_ge(S["xy"], 2 * LVC * TILES)

            def matrices(s):
                chunks = steps[s]
                if s:
                    pe.wait_ge(S["m_sb"], 4 * s)
                    pe.wait_ge(S["kb_sb"], s)
                for par in range(2):
                    for dp in range(4):
                        r, c = slice(HD * par, HD * par + HD), chunks[dp // 2]
                        m = nc.tensor.matmul(ps[:, par, dp * P:(dp + 1) * P], KB[r, dp, c].rearrange("p a b -> p (a b)"),
                                             AR[r, dp, :, ck(c)], start=True, stop=True)
                    m.then_inc(S["m_ps"], 1)
                for dp in range(4):
                    m = nc.tensor.transpose(ps[:, 4, dp * P:(dp + 1) * P], KB[:, dp, chunks[dp // 2]].rearrange("p a b -> p (a b)"),
                                            e.ident[:, :])
                m.then_inc(S["kb_ps"], 1)

            def with_state(dst, dp, c, w, s):
                nc.tensor.matmul(dst, AR[:, dp, w, ck(c)], Sm[:, dp].rearrange("p a b -> p (a b)"), start=True, stop=False,
                                 skip_group_check=True)
                for par in range(2):
                    u = 2 * dp + par
                    m = nc.tensor.matmul(dst[:, par * HD:(par + 1) * HD], M[:, s % 2, u, w * C:(w + 1) * C], VU[:, s % 2, u, :],
                                         start=False, stop=True, skip_group_check=True)
                return m

            matrices(0)
            for s, chunks in enumerate(steps):
                pe.wait_ge(S["sm"], s + 1)
                pe.wait_ge(S["vz"], s + 1)
                pe.wait_ge(S["m_sb"], 4 * s + 4)
                for dp in range(4):
                    c = chunks[dp // 2]
                    m = with_state(ps[blockrow(c), 2, (dp % 2) * P:(dp % 2 + 1) * P], dp, c, 0, s)
                m.then_inc(S["rh_ps"], 1)
                pe.wait_ge(S["rh_sb"], s + 1)
                if s:
                    pe.wait_ge(S["y_ev"], s)
                for dr in range(2):
                    c = chunks[dr]
                    for h in range(HH):
                        m = nc.tensor.matmul(ps[HI, 5 + dr, h * HD:(h + 1) * HD], Yst[blockrow(c), dr, c // 2, h, blockrow(c)],
                                             RH[blockrow(c), h, :], start=True, stop=True)
                    m.then_inc(S["u_ps"], 1)
                if s + 1 < NS:
                    matrices(s + 1)
                pe.wait_ge(S["u_sb"], 2 * s + 2)
                pe.wait_ge(S["kb_sb"], s + 1)
                for dp in range(4):
                    m = nc.tensor.matmul(ps[:, 7, dp * P:(dp + 1) * P], KBt[:, s % 2, dp, :],
                                         VU[:, s % 2, 2 * dp:2 * dp + 2, :].rearrange("p a b -> p (a b)"), start=True, stop=True)
                m.then_inc(S["rs_ps"], 1)
                for dp in range(4):
                    m = with_state(ps[LO, 5, dp * P:(dp + 1) * P], dp, chunks[dp // 2], 1, s)
                m.then_inc(S["y_ps"], 1)
            pe.wait_ge(S["rw_sfin"], 1)
            for dp in range(4):
                m = nc.tensor.transpose(ps[:, 6, dp * P:(dp + 1) * P], Sfin[:, dp].rearrange("p a b -> p (a b)"), e.ident[:, :])
            m.then_inc(S["fin_ps"], 1)
            pe.wait_ge(S["rw_bon"], 2)
            pe.wait_ge(S["y_ev"], NS)
            for c in range(NCH):
                for p in range(2):
                    m = nc.tensor.matmul(ps[LO, 7, c * HH + 2 * p:c * HH + 2 * p + 2], F[:, 6 + p, ck(c)], e.blk[:, 0:P:C],
                                         start=True, stop=True)
            m.then_inc(S["bo_ps"], 1)
            for c in range(NCH):
                m = nc.tensor.matmul(ps[LO, c // 2, (c % 2) * 256:(c % 2 + 1) * 256], F[:, 8, ck(c)], g2, start=True, stop=True)
            m.then_inc(S["ga_ps"], 1)
            pe.wait_ge(S["rw_out"], 1)
            for k in range(2):
                for c in range(NCH):
                    m = nc.tensor.transpose(ps[:, 2 * k + c // 8, (c % 8) * C:(c % 8 + 1) * C], ys[:, c, k * P:(k + 1) * P],
                                            e.ident[LO, LO])
                m.then_inc(S["ro_ps"], 1)

        @block.vector
        def _(dve):
            v = e.chain("dve", dve)
            for p in range(2):
                nc.vector.tensor_scalar(kk[:, p, R], F[:, 2 + p, R], col("kk", p), None, ALU.mult).then_inc(S["rw_k0"], 1)
            nc.vector.memset(wwa, 0.0).then_inc(S["rw_wz"], 1)
            nc.vector.tensor_scalar(oka, pc[:, PC["ka"]:PC["ka"] + 2], -1.0, 1.0, ALU.mult, ALU.add).then_inc(S["rw_oka"], 1)
            for p in range(2):
                dve.wait_ge(S["kn_ps"], 2 * p + 2)
                for i, (c0, c1) in enumerate(cut):
                    m = nc.vector.tensor_scalar(ksq(p)[:, c0:c1], ps[:, 4 + 2 * p + i, 0:c1 - c0], 1e-12, None, ALU.max)
                    if i == 0:
                        v.link(m)
                m.then_inc(S["rw_kmax"], 1)
            for p in range(2):
                dve.wait_ge(S["rw_krt"], p + 1)
                v.link(nc.vector.reciprocal(ksq(p), ksq(p)))
                dve.wait_ge(S["rw_k0"], p + 1)
                nc.vector.tensor_tensor(kk[:, p, R], kk[:, p, R], ksq(p), ALU.mult).then_inc(S["rw_kn"], 1)
            dve.wait_ge(S["rw_kn"], 2)
            for dp in range(4):
                dr, p = divmod(dp, 2)
                lw = AR[:, dp, 0, R]
                dve.wait_ge(S["lo_ev"], 4 * dp + 4)
                v.link(nc.vector.tensor_scalar(lw, lw, DECAY, None, ALU.mult))
                if dp:
                    dve.wait_ge(S["rw_ex"], 3 * dp)
                a, b, c = e.reset[:, dr, R], lw, T[:, 0, R]
                if dr:
                    a, b, c = a[:, ::-1], b[:, ::-1], c[:, ::-1]
                v.link(nc.vector.tensor_tensor_scan(c, a, b, 0.0, ALU.mult, ALU.add))
                m0, e0 = (C // 2 - 1, C - 1) if dr == 0 else (C // 2, 0)
                g = by_chunk(T[:, 0, R])
                per = lambda a: a[:, dp, :].rearrange("p (c o) -> p c o", o=1)
                v.add(nc.vector.tensor_copy(per(mid), g[:, :, m0:m0 + 1]))
                v.link(nc.vector.tensor_copy(per(end), g[:, :, e0:e0 + 1]))
                v.link(nc.vector.tensor_tensor(g, g, per(mid).to_broadcast([P, NCH, C]), ALU.subtract))
                nc.vector.tensor_tensor(lw, T[:, 0, R], lw, ALU.subtract).then_inc(S["rw_E"], 1)
                dve.wait_ge(S["rw_E"], dp + 1)
                dve.wait_ge(S["rw_kd"], dp + 1)
                v.link(nc.vector.tensor_tensor(KB[:, dp, :, 1, :], KB[:, dp, :, 1, :], by_chunk(kk[:, p, R]), ALU.mult))
                dve.wait_ge(S["rw_ex"], 3 * dp + 1)
                for w in range(2):
                    v.add(nc.vector.tensor_tensor(KB[:, dp, :, w, :], KB[:, dp, :, w, :], by_chunk(T[:, 2, R]), ALU.mult))
                dve.wait_ge(S["rw_ex"], 3 * dp + 2)
                v.add(nc.vector.tensor_tensor(AR[:, dp, 1, R], AR[:, dp, 1, R], F[:, p, R], ALU.mult))
                dve.wait_ge(S["rw_ex"], 3 * dp + 3)
                m = nc.vector.tensor_tensor(lw, lw, kk[:, p, R], ALU.mult)
                v.link(m)
                dve.sem_inc(S["rw_pre"], 1)
            v.link(nc.vector.tensor_tensor(G, end, mid, ALU.subtract))
            for dst, src, rows in ((slice(0, 1), slice(1, 2), (0, 2)), (slice(2, NCH - 1), slice(3, NCH), (0, 2)),
                                   (slice(1, 2), slice(0, 1), (2, 4)), (slice(3, NCH), slice(2, NCH - 1), (2, 4))):
                q = slice(*rows)
                v.link(nc.vector.tensor_tensor(G[:, q, dst], G[:, q, dst], mid[:, q, src], ALU.add))
            dve.sem_inc(S["rw_G0"], 1)
            v.add(nc.vector.memset(Sm, 0.0))
            v.add(nc.vector.memset(S0b, 0.0))
            v.link(nc.vector.memset(Gb, 0.0))
            dve.wait_ge(S["rw_G"], 1)
            dve.wait_ge(S["ld_rw"], 64)
            for par, r in enumerate((LO, HI)):
                v.add(nc.vector.tensor_copy(Gb[r, :, :, par:par + 1], G[r].rearrange("p a (c o) -> p a c o", o=1)))
                for dr, c in ((0, 2), (1, NCH - 1)):
                    v.add(nc.vector.tensor_tensor(S0b[r, 2 * dr:2 * dr + 2, par, :], S0[r, 2 * dr:2 * dr + 2, :],
                                                  mid[r, 2 * dr:2 * dr + 2, c:c + 1].to_broadcast([C, 2, HD]), ALU.mult))
            v.join()
            dve.sem_inc(S["sm"], 1)

            def strictly(t):
                dve.wait_ge(S["l_ps"], t + 1)
                if t:
                    dve.wait_ge(S["xy1"], 2 * t)
                    dve.wait_ge(S["mt_ps"], 2 * t)
                for ln in range(2):
                    strict = e.bds[:, ln:ln + 1, :].to_broadcast([P, 2, P])
                    for par in range(2):
                        v.add(nc.vector.tensor_tensor(Ls[:, ln].rearrange("p (a b) c -> p a b c", a=2)[:, :, par, :],
                                                      ps[:, 6 + par, 2 * ln * P:2 * (ln + 1) * P].rearrange("p (a b) -> p a b", a=2),
                                                      strict, ALU.mult))
                v.join()
                dve.sem_inc(S["ls"], 1)

            strictly(0)
            for t in range(TILES):
                for j in range(LVC):
                    for ln in range(2):
                        dve.wait_ge(S["dxy_ps"], (LVC * t + j) * 2 + ln + 1)
                        if j < LVC - 1:
                            Xt = X[t % 2][:, ln]
                            v.add(nc.vector.tensor_tensor(Xt, Xt, ps[:, 2 * ln, :].rearrange("p (a b) -> p a b", a=HH), ALU.subtract))
                        v.link(nc.vector.tensor_tensor(Yst[:, ln, t], Yst[:, ln, t],
                                                       ps[:, 2 * ln + 1, :].rearrange("p (a b) -> p a b", a=HH), ALU.subtract))
                        dve.sem_inc(S["xy"], 1)
                    if j == 0 and t + 1 < TILES:
                        strictly(t + 1)

            def mask(s):
                for par in range(2):
                    dve.wait_ge(S["m_ps"], 2 * s + par + 1)
                    Mv = M[:, s % 2].rearrange("p (d a b) c -> p d a b c", d=2, a=2)
                    for dr in range(2):
                        nc.vector.tensor_tensor(Mv[:, dr, :, par, :], ps[:, par, dr * 2 * P:(dr + 1) * 2 * P].rearrange("p (a c) -> p a c", a=2),
                                                e.rwm[:, dr:dr + 1, :].to_broadcast([P, 2, P]), ALU.mult).then_inc(S["m_sb"], 1)

            mask(0)
            for s, chunks in enumerate(steps):
                dve.wait_ge(S["rh_ps"], s + 1)
                nc.vector.tensor_copy(RH, ps[:, 2, 0:4 * HD].rearrange("p (a b) -> p a b", a=4)).then_inc(S["rh_sb"], 1)
                if s + 1 < NS:
                    mask(s + 1)
                dve.wait_ge(S["rs_ps"], s + 1)
                v.link(nc.vector.tensor_tensor(Sn, Sm, ps[:, 7, :].rearrange("p (a b c) -> p a b c", a=4, b=2), ALU.add))
                dve.wait_ge(S["y_ps"], s + 1)
                to = Sfin if s == 1 else Sm
                for dr in range(2):
                    q = slice(2 * dr, 2 * dr + 2)
                    v.add(nc.vector.tensor_tensor(to[:, q], Sn[:, q], Gb[:, q, chunks[dr], :].rearrange("p a (b o) -> p a b o", o=1)
                                                  .to_broadcast([P, 2, 2, HD]), ALU.mult))
                v.join()
                if s == 1:
                    v.link(nc.vector.tensor_copy(Sm, S0b))
                    dve.sem_inc(S["rw_sfin"], 1)
                dve.sem_inc(S["sm"], 1)
                for dr in range(2):
                    dst = ys[:, chunks[dr], :]
                    src = ps[LO, 5, dr * 4 * HD:(dr + 1) * 4 * HD]
                    if first[s]:
                        v.add(nc.vector.tensor_copy(dst, src))
                    else:
                        v.add(nc.vector.tensor_tensor(dst, dst, src, ALU.add))
                v.join()
                dve.sem_inc(S["y_ev"], 1)
            yv = ys.rearrange("p c (h v) -> p (c h) v", v=HD)
            col3 = lambda a: a.rearrange("p (n o) -> p n o", o=1).to_broadcast([C, NCH * HH, HD])
            row3 = lambda i: e.prow[LO, i:i + 1, :].to_broadcast([C, NCH, HH * HD])
            v.link(nc.vector.reduce_sum(mu, yv, AX))
            v.link(nc.vector.tensor_scalar(mu, mu, 1.0 / HD, None, ALU.mult))
            v.link(nc.vector.tensor_tensor(yv, yv, col3(mu), ALU.subtract))
            dve.sem_inc(S["gn_c"], 1)
            dve.wait_ge(S["bo_ps"], 1)
            nc.vector.tensor_copy(mu, ps[LO, 7, 0:NCH * HH]).then_inc(S["bo_ev"], 1)
            dve.wait_ge(S["gn_sq"], 1)
            v.link(nc.vector.reduce_sum(rs, sq.rearrange("p (n v) -> p n v", v=HD), AX))
            dve.sem_inc(S["gn_var"], 1)
            dve.wait_ge(S["gn_rt"], 1)
            v.link(nc.vector.reciprocal(rs, rs))
            v.link(nc.vector.tensor_tensor(yv, yv, col3(rs), ALU.mult))
            v.link(nc.vector.tensor_tensor(ys, ys, row3(1), ALU.mult))
            dve.wait_ge(S["bonus"], 1)
            v.link(nc.vector.tensor_tensor(ys, ys, Vc, ALU.add))
            dve.wait_ge(S["ga_ps"], 1)
            v.link(nc.vector.tensor_tensor(ys.rearrange("p c v -> p (c v)"), ys.rearrange("p c v -> p (c v)"),
                                           ps[LO, 0:5, :].rearrange("p a b -> p (a b)"), ALU.mult))
            dve.sem_inc(S["rw_out"], 1)
            e.done("dve", v)


def load_norm_rows(e, sp, which, brow, gb, sem):
    d, l = e.d, e.l
    for g in range(2):
        sp.dma_start(brow[:, g, :], e.mod_d[g, 2 + 3 * which].rearrange("k p -> (k p)").rearrange("(o n) -> o n", o=1)
                     .to_broadcast([P, DM])).then_inc(sem, 16)
    for i, name in enumerate(("ln_g", "ln_b")):
        sp.dma_start(gb[:, i, :], d[name][l, which].rearrange("(o n) -> o n", o=1).to_broadcast([P, DM])).then_inc(sem, 16)


def norm_steps(e, pre, src, brow, gb, y, st, src_ready, src_sem, behind):
    nc, S, x = e.nc, e.S, e.x

    def vector(dve, v):
        def scales(t):
            dve.wait_ge(S[pre + "sd"], t + 1)
            v.link(nc.vector.reciprocal(st[:, t, 14:15], st[:, t, 14:15]))
            v.link(nc.vector.tensor_scalar(st[:, t, 15:16], st[:, t, 12:13], st[:, t, 14:15], -1.0, ALU.mult, ALU.mult))
            dve.sem_inc(S[pre + "nm"], 1)

        dve.wait_ge(S[pre + "ld"], 64)
        for t in range(TILES):
            g = 1 if t else 0
            b = t % 2
            src_ready(dve, t)
            if t >= 2:
                dve.wait_ge(S[pre + "xn"], t - 1)
            for n in range(2):
                m = nc.vector.tensor_tensor(y[:, b, n * 512:(n + 1) * 512], src(t, n), brow[:, g, n * 512:(n + 1) * 512], ALU.mult)
                v.add(m)
            v.join()
            if src_sem:
                dve.sem_inc(S[src_sem], 1)
            v.link(nc.vector.scalar_tensor_tensor(y[:, b, :], x[:, t, :], ALPHA, y[:, b, :], ALU.mult, ALU.add))
            for n in range(2):
                v.add(nc.vector.bn_stats(st[:, t, 6 * n:6 * n + 6], y[:, b, n * 512:(n + 1) * 512]))
            v.join()
            v.link(nc.vector.bn_aggr(st[:, t, 12:14], st[:, t, 0:12]))
            dve.sem_inc(S[pre + "var"], 1)
            if behind and t:
                scales(t - 1)
            if not behind or t == TILES - 1:
                scales(t)
        if behind:
            last = x[:, TILES - 1, :]
            dve.wait_ge(S[pre + "xn"], TILES)
            v.link(nc.vector.tensor_tensor(last, last, gb[:, 0, :], ALU.mult))
            v.link(nc.vector.tensor_tensor(last, last, gb[:, 1, :], ALU.add))

    def scalar(act):
        for t in range(TILES):
            act.wait_ge(S[pre + "var"], t + 1)
            nc.scalar.activation(st[:, t, 14:15], st[:, t, 13:14], ACT.Sqrt, bias=e.eps[:, 1:2]).then_inc(S[pre + "sd"], 1)
            act.wait_ge(S[pre + "nm"], t + 1)
            nc.scalar.activation(x[:, t, :], y[:, t % 2, :], ACT.Identity, bias=st[:, t, 15:16], scale=st[:, t, 14:15]
                                 ).then_inc(S[pre + "xn"], 1)

    def pool(pl, c):
        pl.wait_ge(S[pre + "ld"], 64)
        for t in range(TILES - 1 if behind else TILES):
            pl.wait_ge(S[pre + "xn"], t + 1)
            c.link(nc.gpsimd.tensor_tensor(x[:, t, :], x[:, t, :], gb[:, 0, :], ALU.mult))
            nc.gpsimd.tensor_tensor(x[:, t, :], x[:, t, :], gb[:, 1, :], ALU.add).then_inc(S[pre + "x"], 1)

    return vector, scalar, pool


OUTPUT_SEMS = (
    "n1x", "op_ps", "op_ev", "st_x", "n1ld", "n1var", "n1sd", "n1nm", "n1xn", "ld_wo0", "ld_wo1",
)


def phase_output(e):
    nc, d, l, S, ps = e.nc, e.d, e.l, e.S, e.ps
    z = e.a0
    wo, z = e.part(z, 2, KD, 512)
    brow, z = e.part(z, 2, DM)
    gb, z = e.part(z, 2, DM)
    y, z = e.part(z, 2, DM)
    st, z = e.part(z, TILES, 16)
    mem = expert_memory(e)
    assert z <= mem["early"]

    def ready(dve, t):
        dve.wait_ge(S["op_ps"], 2 * t + 2)

    vector, scalar, pool = norm_steps(
        e, "n1", lambda t, n: ps[:, 2 * (t % 4) + n, :], brow, gb, y, st, ready, "op_ev", False)
    with nc.Block() as block:
        @block.sync
        def _(sp):
            e.clear_last(sp)
            for n in range(2):
                sp.dma_start(wo[:, n], d["w_out"][l].rearrange("(k p) n -> p k n", p=P)[:, :, n * 512:(n + 1) * 512]
                             ).then_inc(S[f"ld_wo{n}"], 16)
            load_norm_rows(e, sp, 0, brow, gb, S["n1ld"])
            for j in range(4):
                load_w13(e, sp, 0, j, mem)
            for j in (0, 1):
                load_w2(e, sp, 0, j, mem)
            for t in range(TILES):
                sp.wait_ge(S["n1x"], t + 1)
                sp.dma_start(e.h2_d[t * P:(t + 1) * P, :], e.x[:, t, :]).then_inc(S["st_x"], 16)
            sp.wait_ge(S["st_x"], 16 * TILES)

        @block.tensor
        def _(pe):
            for t in range(TILES):
                if t >= 4:
                    pe.wait_ge(S["op_ev"], t - 3)
                for n in range(2):
                    if t == 0:
                        pe.wait_ge(S[f"ld_wo{n}"], 16)
                    for k in range(KD):
                        m = nc.tensor.matmul(ps[:, 2 * (t % 4) + n, :], e.mixT[:, k, t * P:(t + 1) * P], wo[:, n, k, :],
                                             start=k == 0, stop=k == KD - 1)
                    m.then_inc(S["op_ps"], 1)

        @block.vector
        def _(dve):
            v = e.chain("dve", dve)
            vector(dve, v)
            e.done("dve", v)

        @block.scalar
        def _(act):
            scalar(act)

        @block.gpsimd
        def _(pl):
            c = e.chain("pool", pl)
            pool(pl, c)
            e.done("pool", c)


def expert_memory(e):
    z = 0
    r = {}
    r["yacc"], z = e.part(z, TILES, DM)
    r["xe"], z = e.part(z, 2, DM, rows=CAP)
    r["xT"], z = e.part(z, 2, KD, WIDE)
    r["hs"], z = e.part(z, 2, WIDE)
    r["hA"], z = e.part(z, KD, WIDE)
    r["hB"], z = e.part(z, KD, P)
    r["yP"], z = e.part(z, DM)
    r["yC"], z = e.part(z, DM)
    r["GP"], z = e.part(z, NSM)
    r["GC"], z = e.part(z, NPR)
    r["kept"] = z
    for n in ("iP", "gP", "iC", "gC"):
        r[n], z = e.part(z, NE // 2)
    r["iu"], z = e.part(z, NE, rows=CAP, dt=U32)
    r["ic"], z = e.part(z, 2, rows=CAP, dt=U32)
    r["iota"], z = e.part(z, NTOK)
    first = ARENA - 12 * 2048
    assert z <= first
    r["early"] = first + 2 * 2048
    w, z = e.part(first, 12, 2048)
    r["w2"] = w[:, 0:4].rearrange("p s (k n) -> p s k n", k=2)
    r["w13"] = w[:, 4:12].rearrange("p s (k n) -> p s k n", k=KD)
    return r


def norm2_rows(e):
    brow, z = e.part(ARENA - 8 * 2048, 2, DM)
    gb, z = e.part(z, 2, DM)
    return brow, gb


def load_w13(e, sp, x, j, mem):
    for a, name in enumerate(("ex_w1", "ex_w3")):
        sp.dma_start(mem["w13"][:, 4 * a + j], e.d[name][e.l, x].rearrange("(k p) n -> p k n", p=P)[:, :, j * 256:(j + 1) * 256]
                     ).then_inc(e.S[f"ld_e{j}"], 16)


def load_w2(e, sp, x, j, mem):
    sp.dma_start(mem["w2"][:, (j + 2) % 4], e.d["ex_w2"][e.l, x, j * 256:(j + 1) * 256].rearrange("(k p) n -> p k n", p=P)
                 ).then_inc(e.S[f"ld_f{j}"], 16)


ROUTE_SEMS = (
    "ld_rt", "rx_ps", "rx_act", "rx_dve", "lg_ps", "lg_c", "lg_e", "aff", "af_ps", "top", "ti_ps",
)


def phase_route(e):
    nc, d, l, S, ps = e.nc, e.d, e.l, e.S, e.ps
    mem = expert_memory(e)
    iu, iota, iP, gP, iC, gC = (mem[k] for k in ("iu", "iota", "iP", "gP", "iC", "gC"))
    hT, z = e.part(0, KD, NTOK)
    rt, z = e.part(z, KD, NE)
    lg, z = e.part(z, TILES, NE)
    mx, z = e.part(z, TILES)
    aT, z = e.part(z, NTOK, rows=NE)
    val, z = e.part(z, CAP, rows=NE)
    pos, z = e.part(z, CAP, rows=NE, dt=U32)
    pf, z = e.part(z, CAP, rows=NE)
    base, z = e.part(z, CAP, rows=NE)
    assert z <= mem["kept"]
    NG = 2 * TILES
    with nc.Block() as block:
        @block.sync
        def _(sp):
            e.clear_last(sp)
            sp.dma_start(rt, d["router"][l]).then_inc(S["ld_rt"], 16)
            sp.dma_start(base, d["base"]).then_inc(S["ld_rt"], 16)
            sp.dma_start(iota, d["iota"]).then_inc(S["ld_rt"], 16)
            sp.wait_ge(S["ld_rt"], 48)

        @block.tensor
        def _(pe):
            for n in range(NG):
                t, b = divmod(n, 2)
                if n >= 8:
                    pe.wait_ge(S["rx_dve" if n % 2 else "rx_act"], (n - 8) // 2 + 1)
                for k in range(4):
                    kk = 4 * b + k
                    m = nc.tensor.transpose(ps[:, n % 8, k * P:(k + 1) * P], e.x[:, t, kk * P:(kk + 1) * P], e.ident[:, :])
                m.then_inc(S["rx_ps"], 1)
            pe.wait_ge(S["rx_act"], TILES)
            pe.wait_ge(S["rx_dve"], TILES)
            pe.wait_ge(S["ld_rt"], 48)
            for t in range(TILES):
                for k in range(KD):
                    m = nc.tensor.matmul(ps[:, 0, t * NE:(t + 1) * NE], hT[:, k, t * P:(t + 1) * P], rt[:, k, :],
                                         start=k == 0, stop=k == KD - 1)
            m.then_inc(S["lg_ps"], 1)
            pe.wait_ge(S["aff"], 1)
            for t in range(TILES):
                m = nc.tensor.transpose(ps[0:NE, 1 + t // 4, (t % 4) * P:(t % 4 + 1) * P], lg[:, t, :], e.ident[:, :])
            m.then_inc(S["af_ps"], 1)
            pe.wait_ge(S["top"], 1)
            nc.tensor.transpose(ps[0:CAP, 3, 0:NE], pf, e.ident[0:NE, 0:NE])
            nc.tensor.transpose(ps[0:CAP, 3, NE:2 * NE], val, e.ident[0:NE, 0:NE]).then_inc(S["ti_ps"], 1)

        @block.scalar
        def _(act):
            for n in range(0, NG, 2):
                t, b = divmod(n, 2)
                g = 1 if t else 0
                act.wait_ge(S["rx_ps"], n + 1)
                for k in range(4):
                    kk = 4 * b + k
                    m = nc.scalar.activation(hT[:, kk, t * P:(t + 1) * P], ps[:, n % 8, k * P:(k + 1) * P], ACT.Identity,
                                             bias=e.modc[:, g, 3, kk:kk + 1], scale=e.modc[:, g, 4, kk:kk + 1])
                m.then_inc(S["rx_act"], 1)
            act.wait_ge(S["lg_c"], 1)
            nc.scalar.activation(lg, lg, ACT.Exp).then_inc(S["lg_e"], 1)

        @block.vector
        def _(dve):
            v = e.chain("dve", dve)
            for n in range(1, NG, 2):
                t, b = divmod(n, 2)
                g = 1 if t else 0
                dve.wait_ge(S["rx_ps"], n + 1)
                for k in range(4):
                    kk = 4 * b + k
                    m = nc.vector.tensor_scalar(hT[:, kk, t * P:(t + 1) * P], ps[:, n % 8, k * P:(k + 1) * P],
                                                e.modc[:, g, 4, kk:kk + 1], e.modc[:, g, 3, kk:kk + 1], ALU.mult, ALU.add)
                m.then_inc(S["rx_dve"], 1)
            dve.wait_ge(S["lg_ps"], 1)
            v.link(nc.vector.tensor_copy(lg, ps[:, 0, 0:TILES * NE].rearrange("p (a b) -> p a b", a=TILES)))
            m3 = mx.rearrange("p (n o) -> p n o", o=1).to_broadcast([P, TILES, NE])
            v.link(nc.vector.reduce_max(mx, lg, AX))
            v.link(nc.vector.tensor_tensor(lg, lg, m3, ALU.subtract))
            dve.sem_inc(S["lg_c"], 1)
            dve.wait_ge(S["lg_e"], 1)
            v.link(nc.vector.reduce_sum(mx, lg, AX))
            v.link(nc.vector.reciprocal(mx, mx))
            v.link(nc.vector.tensor_tensor(lg, lg, m3, ALU.mult))
            dve.sem_inc(S["aff"], 1)
            dve.wait_ge(S["af_ps"], 1)
            v.link(nc.vector.tensor_copy(aT, ps[0:NE, 1:3, :].rearrange("p a b -> p (a b)")[:, 0:NTOK]))
            for c0, c1, k0, k1 in ((NPR, NTOK, 0, CAPS), (0, NPR, CAPS, CAP)):
                for k in range(k0, k1, 8):
                    v.link(nc.vector.max(val[:, k:k + 8], aT[:, c0:c1]))
                    v.link(nc.vector.max_index(pos[:, k:k + 8], val[:, k:k + 8], aT[:, c0:c1]))
                    if k + 8 < k1:
                        v.link(nc.vector.match_replace(aT[:, c0:c1], val[:, k:k + 8], aT[:, c0:c1], -1.0))
            v.link(nc.vector.tensor_copy(pf, pos))
            dve.wait_ge(S["ld_rt"], 48)
            v.link(nc.vector.tensor_tensor(pf, pf, base, ALU.add))
            dve.sem_inc(S["top"], 1)
            dve.wait_ge(S["ti_ps"], 1)
            v.add(nc.vector.tensor_copy(iu, ps[0:CAP, 3, 0:NE]))
            v.add(nc.vector.memset(iC, -1.0))
            v.link(nc.vector.memset(gC, 0.0))
            for src, dP, dC in ((ps[:, 3, 0:NE], iP, iC), (ps[:, 3, NE:2 * NE], gP, gC)):
                two = src.rearrange("p (n b) -> p b n", b=2)
                for b in range(2):
                    v.add(nc.vector.tensor_copy(dP[b * CAPS:(b + 1) * CAPS, :], two[0:CAPS, b]))
                    v.add(nc.vector.tensor_copy(dC[b * 32:b * 32 + CAPP, :], two[CAPS:CAP, b]))
            v.join()
            e.done("dve", v)


EXPERTS_SEMS = (
    "turn", "yc_sb", "gc_sb", "ld_n2",
    "ic", "xe_used", "xt_ps", "xt_sb", "xm", "xa", "g_sb", "ye_sb", "sc_ev", "sp_ps", "he", "hs", "h_ps", "w_used",
)
EXPERT_WEIGHT_SEMS = ("ld_e0", "ld_e1", "ld_e2", "ld_e3", "ld_f0", "ld_f1", "ld_f2", "ld_f3")


def phase_experts(e):
    nc, d, l, S, ps = e.nc, e.d, e.l, e.S, e.ps
    mem = expert_memory(e)
    w13, w2, yacc, xe, xT, hs, hA, hB, yP, yC, GP, GC, iP, gP, iC, gC, iu, ic, iota = (mem[k] for k in (
        "w13", "w2", "yacc", "xe", "xT", "hs", "hA", "hB", "yP", "yC", "GP", "GC", "iP", "gP", "iC", "gC", "iu", "ic", "iota"))
    NI = NE // 2
    hT = (hA, hB[:, :, P - WIDE:])
    rows = (hA[:, :, 0:CAP], hB)
    blocks = [(t, h) for t in range(1, TILES) for h in range(2)] + [(0, 0), (0, 1)]

    with nc.Block() as block:
        @block.sync
        def _(sp):
            e.clear_last(sp)

            for j in (2, 3):
                load_w2(e, sp, 0, j, mem)
            with sp.Fori(1, NE) as x:
                for second in range(2):
                    for j in range(4):
                        if second:
                            sp.wait_ge(S["w_used"], x * 4 + (j + 1 - 4))
                            load_w2(e, sp, x, j, mem)
                        else:
                            sp.wait_ge(S["h_ps"], x * 8 + (2 * j + 2 - 8))
                            load_w13(e, sp, x, j, mem)
            sp.wait_ge(S["h_ps"], 8 * NE)
            load_norm_rows(e, sp, 1, *norm2_rows(e), S["ld_n2"])
            sp.wait_ge(S["ld_n2"], 64)

        @block.gpsimd
        def _(pool):
            with pool.Fori(0, NI) as i:
                for b in range(2):
                    pool.wait_ge(S["xe_used"], i * 2 + (b + 1))
                    pool.sem_inc(S["turn"], 1)
                    nc.gpsimd.tensor_copy(ic[:, b:b + 1], iu[:, bass.ds(i * 2 + b, 1)]).then_inc(S["ic"], 1)
                    pool.wait_ge(S["ic"], i * 2 + (b + 1))
                    pool.sem_inc(S["turn"], 1)
                    nc.gpsimd.indirect_dma_start(xe[:, b, :], None, e.h2_d, bass.IndirectOffsetOnAxis(ap=ic[:, b:b + 1], axis=0)
                                                 ).then_inc(S[f"ld_x{b}"], 16)
            pool.wait_ge(S["xe_used"], NE + 1)
            nc.gpsimd.indirect_dma_start(xe[:, 0, :], None, e.h2_d, bass.IndirectOffsetOnAxis(ap=ic[:, 0:1], axis=0)
                                         ).then_inc(S["ld_x0"], 16)

        @block.tensor
        def _(pe):
            def turn_tokens(i, b, at):
                pe.wait_ge(S[f"ld_x{b}"], l * (16 * (NI + 1 - b)) + (i * 16 + 16))
                pe.wait_ge(S["xe_used"], at + 2)
                for k in range(KD):
                    m = nc.tensor.transpose(ps[:, k // 4, (k % 4) * CAP:(k % 4 + 1) * CAP], xe[:, b, k * P:(k + 1) * P],
                                            e.ident[0:CAP, 0:CAP])
                m.then_inc(S["xt_ps"], 1)

            def scatter(i):
                pe.wait_ge(S["ye_sb"], i * 2 + 2)
                pe.wait_ge(S["g_sb"], i + 1)
                for k, (t, h) in enumerate(blocks):
                    pe.wait_ge(S["sc_ev"], i * 10 + (k + 1))
                    if t:
                        m = nc.tensor.matmul(ps[:, 6 + h, :], GP[:, (t - 1) * P:t * P], yP[:, h * 512:(h + 1) * 512],
                                             start=True, stop=True)
                    else:
                        m = nc.tensor.matmul(ps[:, 6 + h, :], GC, yC[:, h * 512:(h + 1) * 512], start=True, stop=True)
                    m.then_inc(S["sp_ps"], 1)

            turn_tokens(0, 0, 0)
            with pe.Fori(0, NI) as i:
                for b in range(2):
                    x = i * 2 + b
                    for f in range(KD):
                        j = f // 2
                        if f % 2 == 0:
                            pe.wait_ge(S[f"ld_e{j}"], l * (32 * NE) + (x * 32 + 32))
                        if f == 0:
                            pe.wait_ge(S["xt_sb"], x + 1)
                        pe.wait_ge(S["he"], x * 8 + (f + 1))
                        for a in range(2):
                            for k in range(KD):
                                m = nc.tensor.matmul(ps[:, 2 + f % 2, a * WIDE:(a + 1) * WIDE],
                                                     w13[:, 4 * a + j, k, (f % 2) * P:(f % 2 + 1) * P],
                                                     xT[:, b, k, :], start=k == 0, stop=k == KD - 1)
                        m.then_inc(S["h_ps"], 1)
                        if b == 0 and f == 3:
                            turn_tokens(i, 1, i * 2 + 1)
                    if b == 0:
                        scatter(i)
                    else:
                        turn_tokens(i + 1, 0, i * 2 + 2)
                    pe.wait_ge(S["he"], x * 8 + 10)
                    if b == 1:
                        pe.wait_ge(S["ye_sb"], i * 2 + 3)
                    for f in range(KD):
                        if f % 2 == 0:
                            pe.wait_ge(S[f"ld_f{f // 2}"], l * (16 * NE) + (x * 16 + 16))
                        for h in range(2):
                            r = rows[b]
                            m = nc.tensor.matmul(ps[0:CAP if b == 0 else P, 4 + h, :], r[:, f, :],
                                                 w2[:, (f // 2 + 2) % 4, f % 2, h * 512:(h + 1) * 512], start=f == 0, stop=f == KD - 1)
                        if f % 2:
                            m.then_inc(S["w_used"], 1)
            scatter(NI)

        @block.scalar
        def _(act):
            with act.Fori(0, NI) as i:
                for b in range(2):
                    x = i * 2 + b
                    for f in range(KD):
                        act.wait_ge(S["h_ps"], x * 8 + (f + 1))
                        act.wait_ge(S["he"], x * 8 + (f + 1))
                        nc.scalar.activation(hs[:, f % 2, :], ps[:, 2 + f % 2, 0:WIDE], ACT.Silu).then_inc(S["hs"], 1)
                    act.wait_ge(S["w_used"], x * 4 + 4)
                    if b == 0:
                        act.wait_ge(S["sp_ps"], i * 10 + 10)
                    yes = ps[:, 4:6, :].rearrange("p a b -> p (a b)")
                    c0, p0 = (CAPS, 0) if b == 0 else (32, CAPS)
                    nc.scalar.activation(yC[b * 32:b * 32 + CAPP, :], yes[c0:c0 + CAPP, :], ACT.Copy).then_inc(S["yc_sb"], 1)
                    nc.scalar.activation(yP[p0:p0 + CAPS, :], yes[p0:p0 + CAPS, :], ACT.Copy).then_inc(S["ye_sb"], 1)

        @block.vector
        def _(dve):
            v = e.chain("dve", dve)
            v.add(nc.vector.memset(yacc, 0.0))
            for a in (yP, yC, GP, GC, xT[:, :, :, :].rearrange("p a b c -> p (a b c)"), hB.rearrange("p a b -> p (a b)")):
                v.add(nc.vector.memset(a, 0.0))
            v.join()
            for name, n in (("ye_sb", 2), ("g_sb", 1), ("sc_ev", 2), ("he", 2), ("xe_used", 2)):
                dve.sem_inc(S[name], n)

            def tokens(b, at):
                dve.wait_ge(S["xt_ps"], at + 1)
                for c0, c1, to, g in ORDER[b]:
                    for q in range(2):
                        sc = e.modc[:, g, 4, 4 * q:4 * q + 4].rearrange("p (n o) -> p n o", o=1).to_broadcast([P, 4, c1 - c0])
                        nc.vector.tensor_tensor(xT[:, b, 4 * q:4 * q + 4, to:to + c1 - c0],
                                                ps[:, q, 0:4 * CAP].rearrange("p (a b) -> p a b", a=4)[:, :, c0:c1],
                                                sc, ALU.mult).then_inc(S["xm"], 1)
                dve.wait_ge(S["xm"], at * 4 + 4)
                dve.sem_inc(S["xe_used"], 1)
                for c0, c1, to, g in ORDER[b]:
                    sh = e.modc[:, g, 3, :].rearrange("p (n o) -> p n o", o=1).to_broadcast([P, KD, c1 - c0])
                    nc.vector.tensor_tensor(xT[:, b, :, to:to + c1 - c0], xT[:, b, :, to:to + c1 - c0], sh, ALU.add
                                            ).then_inc(S["xa"], 1)
                dve.wait_ge(S["xa"], at * 2 + 2)
                dve.sem_inc(S["xt_sb"], 1)

            def add(i):
                for k, (t, h) in enumerate(blocks):
                    dve.wait_ge(S["sp_ps"], i * 10 + (k + 1))
                    nc.vector.tensor_tensor(yacc[:, t, h * 512:(h + 1) * 512], yacc[:, t, h * 512:(h + 1) * 512], ps[:, 6 + h, :],
                                            ALU.add).then_inc(S["sc_ev"], 1)

            tokens(0, 0)
            with dve.Fori(0, NI) as i:
                for b in range(2):
                    x = i * 2 + b
                    for f in range(KD):
                        dve.wait_ge(S["hs"], x * 8 + (f + 1))
                        nc.vector.tensor_tensor(hT[b][:, f, :], hs[:, f % 2, :], ps[:, 2 + f % 2, WIDE:2 * WIDE], ALU.mult
                                                ).then_inc(S["he"], 1)
                        if b == 0 and f == 3:
                            tokens(1, i * 2 + 1)
                    if b == 0:
                        add(i)
                        nc.vector.tensor_scalar(GC, iota[:, 0:NPR], iC[:, bass.ds(i, 1)], gC[:, bass.ds(i, 1)],
                                                ALU.is_equal, ALU.mult).then_inc(S["gc_sb"], 1)
                        nc.vector.tensor_scalar(GP, iota[:, NPR:], iP[:, bass.ds(i, 1)], gP[:, bass.ds(i, 1)],
                                                ALU.is_equal, ALU.mult).then_inc(S["g_sb"], 1)
                    else:
                        tokens(0, i * 2 + 2)
            add(NI)
            e.done("dve", v)


NORM2_SEMS = (
    "n2ld", "n2var", "n2sd", "n2nm", "n2xn", "n2x",
)


def phase_norm2(e):
    nc, S = e.nc, e.S
    yacc = expert_memory(e)["yacc"]
    brow, gb = norm2_rows(e)
    y, z = e.part(TILES * DM, 2, DM)
    st, z = e.part(z, TILES, 16)
    vector, scalar, pool = norm_steps(
        e, "n2", lambda t, n: yacc[:, t, n * 512:(n + 1) * 512], brow, gb, y, st, lambda dve, t: None, None, True)
    with nc.Block() as block:
        @block.sync
        def _(sp):
            e.clear_last(sp)
            sp.sem_inc(S["n2ld"], 64)

        @block.vector
        def _(dve):
            v = e.chain("dve", dve)
            vector(dve, v)
            e.done("dve", v)

        @block.scalar
        def _(act):
            scalar(act)

        @block.gpsimd
        def _(pl):
            c = e.chain("pool", pl)
            pool(pl, c)
            e.done("pool", c)


PHASES = [
    (phase_modulation, MODULATION_SEMS), (phase_project, PROJECT_SEMS), (phase_attention, ATTENTION_SEMS),
    (phase_hgrn, HGRN_SEMS), (phase_rwkv, RWKV_SEMS), (phase_output, OUTPUT_SEMS), (phase_route, ROUTE_SEMS),
    (phase_experts, EXPERTS_SEMS), (phase_norm2, NORM2_SEMS),
]


def kernel(**inputs):
    import numpy as _np
    import concourse.bacc as _bacc
    from concourse import mybir as _mybir
    from concourse.bass_utils import run_bass_kernel_spmd as _run

    nc = _bacc.Bacc("TRN2", target_bir_lowering=False, num_devices=1)
    arrays, d, o = {}, {}, {}
    for name, a in layout(inputs).items():
        arrays[f"in_{name}"] = a
        d[name] = nc.dram_tensor(f"in_{name}", a.shape, _mybir.dt.from_np(a.dtype), kind="ExternalInput").ap()
    for name, shape in OUTS:
        o[name] = nc.dram_tensor(f"out_{name}", shape, _mybir.dt.float32, kind="ExternalOutput").ap()
    program(nc, d, o)
    r = _run(nc, [arrays], core_ids=[0])
    return tuple(r.results[0][f"out_{name}"] for name, _ in OUTS)
```
